# Optimizing a Trainium2 kernel written in Bass

```python
import math
import jax, jax.numpy as jnp
from jax import lax
import numpy as np

D_MODEL = 1024
BATCH = 1
SEQ = 256
DEPTH = 2

N_MIXERS = 2
N_ATTN_LAYERS = (DEPTH + 1) // 2
N_MLSTM_LAYERS = DEPTH // 2

DA_HEADS = 8
DA_HEAD_DIM = 64
DA_V_DIM = 2 * DA_HEAD_DIM
DA_PROJ = 3 * DA_HEADS * 2 * DA_HEAD_DIM
Q_BLOCK = 128

REL_BUCKETS = 32
REL_MAX_DIST = 128

ML_HEADS = 4
ML_V_DIM = D_MODEL // ML_HEADS
ML_QK_DIM = ML_V_DIM // 2
ML_CHUNK = 64
CONV_WIDTH = 4
ML_QK_WIDTH = 2 * ML_HEADS * ML_QK_DIM
ML_V_WIDTH = ML_HEADS * ML_V_DIM
ML_PROJ = ML_QK_WIDTH + 2 * ML_V_WIDTH + 2 * ML_HEADS

D_FF = 4 * D_MODEL

EPS = 1e-6


def rmsnorm(x, g):
    xf = x.astype(jnp.float32)
    y = xf * lax.rsqrt(jnp.mean(xf * xf, axis=-1, keepdims=True) + EPS)
    return (y * g.astype(jnp.float32)).astype(x.dtype)

def t5_causal_bucket(dist):
    max_exact = REL_BUCKETS // 2
    d = jnp.maximum(dist, 1).astype(jnp.float32)
    large = max_exact + (jnp.log(d / max_exact) / math.log(REL_MAX_DIST / max_exact)
                         * (REL_BUCKETS - max_exact)).astype(jnp.int32)
    large = jnp.minimum(large, REL_BUCKETS - 1)
    return jnp.where(dist < max_exact, dist, large)

def diff_attention(h, w_in, lq1, lk1, lq2, lk2, subln_w, w_out, rel_table, lambda_init):
    B, S, _ = h.shape
    qkv = h @ w_in
    q, k, v = jnp.split(qkv, 3, axis=-1)
    q = q.reshape(B, S, DA_HEADS, 2, DA_HEAD_DIM)
    k = k.reshape(B, S, DA_HEADS, 2, DA_HEAD_DIM)
    v = v.reshape(B, S, DA_HEADS, DA_V_DIM)
    lam = (jnp.exp(jnp.sum(lq1.astype(jnp.float32) * lk1.astype(jnp.float32)))
           - jnp.exp(jnp.sum(lq2.astype(jnp.float32) * lk2.astype(jnp.float32)))
           + lambda_init)
    scale = DA_HEAD_DIM ** -0.5
    outs = []
    for blk in range(S // Q_BLOCK):
        q0 = blk * Q_BLOCK
        kend = q0 + Q_BLOCK
        qb = q[:, q0:kend]
        kb = k[:, :kend]
        vb = v[:, :kend]
        dist = (q0 + jnp.arange(Q_BLOCK))[:, None] - jnp.arange(kend)[None, :]
        bias = rel_table[t5_causal_bucket(jnp.maximum(dist, 0))]
        bias = jnp.transpose(bias, (2, 0, 1)).astype(jnp.float32)
        logits = jnp.einsum('bqhmd,bkhmd->bmhqk', qb, kb).astype(jnp.float32) * scale + bias
        logits = jnp.where(dist >= 0, logits, -jnp.inf)
        p = jax.nn.softmax(logits, axis=-1)
        attn = p[:, 0] - lam * p[:, 1]
        outs.append(jnp.einsum('bhqk,bkhd->bqhd', attn.astype(vb.dtype), vb))
    o = jnp.concatenate(outs, axis=1)
    o = rmsnorm(o, subln_w) * (1.0 - lambda_init)
    return o.reshape(B, S, DA_HEADS * DA_V_DIM) @ w_out

def causal_depthwise_conv(x, w, b):
    C = x.shape[-1]
    y = lax.conv_general_dilated(x, w[:, None, :].astype(x.dtype), window_strides=(1,),
                                 padding=[(CONV_WIDTH - 1, 0)],
                                 dimension_numbers=('NWC', 'WIO', 'NWC'),
                                 feature_group_count=C)
    return y + b.astype(x.dtype)

def mlstm_chunkwise(q, k, v, i_pre, log_f):
    B, S, H, dk = q.shape
    dv = v.shape[-1]
    L = ML_CHUNK
    NC = S // L
    f32 = jnp.float32
    q = (q.astype(f32) * dk ** -0.5).reshape(B, NC, L, H, dk).transpose(0, 3, 1, 2, 4)
    k = k.astype(f32).reshape(B, NC, L, H, dk).transpose(0, 3, 1, 2, 4)
    v = v.astype(f32).reshape(B, NC, L, H, dv).transpose(0, 3, 1, 2, 4)
    ig = i_pre.astype(f32).reshape(B, NC, L, H).transpose(0, 3, 1, 2)
    lf = log_f.astype(f32).reshape(B, NC, L, H).transpose(0, 3, 1, 2)
    b = jnp.cumsum(lf, axis=-1)
    b_last = b[..., -1]

    a = b_last[..., None] - b + ig
    m_loc = jnp.max(a, axis=-1)
    wgt = jnp.exp(a - m_loc[..., None])
    C_loc = jnp.einsum('bhcsv,bhcsk->bhcvk', wgt[..., None] * v, k)
    n_loc = jnp.einsum('bhcs,bhcsk->bhck', wgt, k)

    def step(carry, inp):
        C, n, m = carry
        bl, Cl, nl, ml = inp
        m_new = jnp.maximum(bl + m, ml)
        decay = jnp.exp(bl + m - m_new)
        gain = jnp.exp(ml - m_new)
        C_new = decay[..., None, None] * C + gain[..., None, None] * Cl
        n_new = decay[..., None] * n + gain[..., None] * nl
        return (C_new, n_new, m_new), (C, n, m)

    init = (jnp.zeros((B, H, dv, dk), f32), jnp.zeros((B, H, dk), f32), jnp.zeros((B, H), f32))
    xs = (jnp.moveaxis(b_last, 2, 0), jnp.moveaxis(C_loc, 2, 0),
          jnp.moveaxis(n_loc, 2, 0), jnp.moveaxis(m_loc, 2, 0))
    _, (C_prev, n_prev, m_prev) = lax.scan(step, init, xs)
    C_prev = jnp.moveaxis(C_prev, 0, 2)
    n_prev = jnp.moveaxis(n_prev, 0, 2)
    m_prev = jnp.moveaxis(m_prev, 0, 2)

    causal = jnp.tril(jnp.ones((L, L), dtype=bool))
    D = b[..., :, None] - b[..., None, :] + ig[..., None, :]
    D = jnp.where(causal, D, -jnp.inf)
    m_inter = b + m_prev[..., None]
    m_j = jnp.maximum(m_inter, jnp.max(D, axis=-1))
    Sc = jnp.einsum('bhcjk,bhcsk->bhcjs', q, k) * jnp.exp(D - m_j[..., None])
    inter = jnp.exp(m_inter - m_j)
    num = (jnp.einsum('bhcjs,bhcsv->bhcjv', Sc, v)
           + inter[..., None] * jnp.einsum('bhcjk,bhcvk->bhcjv', q, C_prev))
    den = jnp.sum(Sc, axis=-1) + inter * jnp.einsum('bhcjk,bhck->bhcj', q, n_prev)
    h = num / jnp.maximum(jnp.abs(den), jnp.exp(-m_j))[..., None]
    return h.transpose(0, 2, 3, 1, 4).reshape(B, S, H, dv)

def mlstm_mixer(h, w_in, b_i, b_f, conv_w, conv_b, head_norm_w, w_out):
    B, S, _ = h.shape
    proj = h @ w_in
    qk = proj[..., :ML_QK_WIDTH]
    v = proj[..., ML_QK_WIDTH:ML_QK_WIDTH + ML_V_WIDTH]
    o_pre = proj[..., ML_QK_WIDTH + ML_V_WIDTH:ML_QK_WIDTH + 2 * ML_V_WIDTH]
    gates = proj[..., ML_QK_WIDTH + 2 * ML_V_WIDTH:].astype(jnp.float32)
    qk = jax.nn.silu(causal_depthwise_conv(qk, conv_w, conv_b))
    q = qk[..., :ML_QK_WIDTH // 2].reshape(B, S, ML_HEADS, ML_QK_DIM)
    k = qk[..., ML_QK_WIDTH // 2:].reshape(B, S, ML_HEADS, ML_QK_DIM)
    v = v.reshape(B, S, ML_HEADS, ML_V_DIM)
    i_pre = gates[..., :ML_HEADS] + b_i.astype(jnp.float32)
    log_f = jax.nn.log_sigmoid(gates[..., ML_HEADS:] + b_f.astype(jnp.float32))
    ht = mlstm_chunkwise(q, k, v, i_pre, log_f)
    ht = rmsnorm(ht, head_norm_w.reshape(ML_HEADS, ML_V_DIM))
    out = jax.nn.sigmoid(o_pre.astype(jnp.float32)) * ht.reshape(B, S, ML_V_WIDTH)
    return out.astype(h.dtype) @ w_out

def sqrelu_mlp(h, w1, w2):
    return jnp.square(jax.nn.relu(h @ w1)) @ w2

def first_inputs(seed: int = 0) -> dict:
    key = jax.random.key(seed)
    ks = jax.random.split(key, 24)
    f32 = jnp.float32
    nA, nM = N_ATTN_LAYERS, N_MLSTM_LAYERS

    def nrm(k, shape, scale):
        return jax.random.normal(k, shape, f32) * scale

    def gain(k, shape):
        return 1.0 + 0.05 * jax.random.normal(k, shape, f32)

    return {
        "x": jax.random.normal(ks[0], (BATCH, SEQ, D_MODEL), f32),
        "rel_bias": nrm(ks[1], (REL_BUCKETS, DA_HEADS), 0.5),
        "attn_norm": gain(ks[2], (nA, D_MODEL)),
        "attn_w_in": nrm(ks[3], (nA, D_MODEL, DA_PROJ), D_MODEL ** -0.5),
        "attn_lambda_q1": nrm(ks[4], (nA, DA_HEAD_DIM), 0.1),
        "attn_lambda_k1": nrm(ks[5], (nA, DA_HEAD_DIM), 0.1),
        "attn_lambda_q2": nrm(ks[6], (nA, DA_HEAD_DIM), 0.1),
        "attn_lambda_k2": nrm(ks[7], (nA, DA_HEAD_DIM), 0.1),
        "attn_subln": gain(ks[8], (nA, DA_V_DIM)),
        "attn_w_out": nrm(ks[9], (nA, DA_HEADS * DA_V_DIM, D_MODEL), (DA_HEADS * DA_V_DIM) ** -0.5),
        "mlstm_norm": gain(ks[10], (nM, D_MODEL)),
        "mlstm_w_in": nrm(ks[11], (nM, D_MODEL, ML_PROJ), D_MODEL ** -0.5),
        "mlstm_b_i": nrm(ks[12], (nM, ML_HEADS), 0.1),
        "mlstm_b_f": jnp.broadcast_to(jnp.linspace(3.0, 6.0, ML_HEADS, dtype=f32), (nM, ML_HEADS))
                     + nrm(ks[13], (nM, ML_HEADS), 0.01),
        "mlstm_conv_w": nrm(ks[14], (nM, CONV_WIDTH, ML_QK_WIDTH), CONV_WIDTH ** -0.5),
        "mlstm_conv_b": nrm(ks[15], (nM, ML_QK_WIDTH), 0.02),
        "mlstm_head_norm": gain(ks[16], (nM, ML_V_WIDTH)),
        "mlstm_w_out": nrm(ks[17], (nM, ML_V_WIDTH, D_MODEL), ML_V_WIDTH ** -0.5),
        "mlp_norm": gain(ks[18], (DEPTH, D_MODEL)),
        "mlp_w1": nrm(ks[19], (DEPTH, D_MODEL, D_FF), D_MODEL ** -0.5),
        "mlp_w2": nrm(ks[20], (DEPTH, D_FF, D_MODEL), D_FF ** -0.5),
        "final_norm": gain(ks[21], (D_MODEL,)),
    }

def first_block(x, rel_bias, attn_norm, attn_w_in, attn_lambda_q1, attn_lambda_k1,
              attn_lambda_q2, attn_lambda_k2, attn_subln, attn_w_out,
              mlstm_norm, mlstm_w_in, mlstm_b_i, mlstm_b_f, mlstm_conv_w, mlstm_conv_b,
              mlstm_head_norm, mlstm_w_out, mlp_norm, mlp_w1, mlp_w2, final_norm):
    h = x
    for layer in range(DEPTH):
        j = layer // N_MIXERS
        if layer % N_MIXERS == 0:
            lambda_init = 0.8 - 0.6 * math.exp(-0.3 * layer)
            mix = diff_attention(rmsnorm(h, attn_norm[j]), attn_w_in[j],
                                 attn_lambda_q1[j], attn_lambda_k1[j],
                                 attn_lambda_q2[j], attn_lambda_k2[j],
                                 attn_subln[j], attn_w_out[j], rel_bias, lambda_init)
        else:
            mix = mlstm_mixer(rmsnorm(h, mlstm_norm[j]), mlstm_w_in[j], mlstm_b_i[j],
                              mlstm_b_f[j], mlstm_conv_w[j], mlstm_conv_b[j],
                              mlstm_head_norm[j], mlstm_w_out[j])
        h = h + mix.astype(h.dtype)
        h = h + sqrelu_mlp(rmsnorm(h, mlp_norm[layer]), mlp_w1[layer], mlp_w2[layer]).astype(h.dtype)
    return rmsnorm(h, final_norm)


DEPTH_2 = 1

PLE_DIM = 256
RET_HEADS = 4
RET_QK_DIM = 256
RET_V_DIM = 512
RET_CHUNK = 128
MLA_HEADS = 8
MLA_NOPE_DIM = 128
MLA_ROPE_DIM = 64
MLA_QK_DIM = MLA_NOPE_DIM + MLA_ROPE_DIM
MLA_V_DIM = 128
MLA_Q_LORA = 384
MLA_KV_LORA = 256
ATTN_BLOCK = 128
D_FF_2 = 4 * D_MODEL
ROPE_BASE = 10000.0
RMS_EPS = 1e-6

RET_QK_W = RET_HEADS * RET_QK_DIM
RET_V_W = RET_HEADS * RET_V_DIM
MLA_V_W = MLA_HEADS * MLA_V_DIM
IN_SIZES = (RET_QK_W, RET_QK_W, RET_V_W, RET_V_W, MLA_Q_LORA, MLA_KV_LORA, MLA_ROPE_DIM, D_MODEL, D_MODEL)
IN_WIDTH = sum(IN_SIZES)


def rms_norm(x, gain):
    xf = x.astype(jnp.float32)
    y = xf * lax.rsqrt(jnp.mean(xf * xf, axis=-1, keepdims=True) + RMS_EPS)
    return (y * gain.astype(jnp.float32)).astype(x.dtype)

def rope(x, pos):
    half = x.shape[-1] // 2
    inv = ROPE_BASE ** (-jnp.arange(half, dtype=jnp.float32) / half)
    ang = pos.astype(jnp.float32)[:, :, None] * inv
    cos = jnp.cos(ang)[:, :, None, :]
    sin = jnp.sin(ang)[:, :, None, :]
    xf = x.astype(jnp.float32)
    x1, x2 = xf[..., :half], xf[..., half:]
    return jnp.concatenate([x1 * cos - x2 * sin, x2 * cos + x1 * sin], axis=-1).astype(x.dtype)

def retention(q, k, v):
    B, S, H, dk = q.shape
    dv = v.shape[-1]
    C = RET_CHUNK
    N = S // C
    log_g = jnp.log1p(-jnp.exp2(-5.0 - jnp.arange(H, dtype=jnp.float32)))
    idx = jnp.arange(C, dtype=jnp.float32)
    diff = idx[:, None] - idx[None, :]
    decay_in = jnp.where(diff >= 0, jnp.exp(jnp.maximum(diff, 0.0)[None] * log_g[:, None, None]), 0.0)
    q_dec = jnp.exp((idx + 1.0)[None, :] * log_g[:, None])
    k_dec = jnp.exp((C - 1.0 - idx)[None, :] * log_g[:, None])
    chunk_dec = jnp.exp(C * log_g)

    def to_chunks(t):
        return t.astype(jnp.float32).reshape(B, N, C, H, t.shape[-1]).transpose(1, 0, 3, 2, 4)

    def step(state, inp):
        qc, kc, vc = inp
        scores = jnp.einsum('bhnd,bhmd->bhnm', qc, kc) * decay_in
        o = (jnp.einsum('bhnm,bhmv->bhnv', scores, vc)
             + jnp.einsum('bhnd,bhdv->bhnv', qc, state) * q_dec[None, :, :, None])
        state = (state * chunk_dec[None, :, None, None]
                 + jnp.einsum('bhmd,bhmv->bhdv', kc * k_dec[None, :, :, None], vc))
        return state, o

    state0 = jnp.zeros((B, H, dk, dv), jnp.float32)
    _, o = lax.scan(step, state0, (to_chunks(q), to_chunks(k), to_chunks(v)))
    return o.transpose(1, 0, 3, 2, 4).reshape(B, S, H, dv).astype(v.dtype)

def causal_block_attention(q, k, v):
    B, S, H, D = q.shape
    nb = S // ATTN_BLOCK
    scale = D ** -0.5
    qb = q.reshape(B, nb, ATTN_BLOCK, H, D).transpose(1, 0, 2, 3, 4)
    key_pos = jnp.arange(S)

    def one(args):
        qi, bi = args
        s = jnp.einsum('bqhd,bkhd->bhqk', qi, k).astype(jnp.float32) * scale
        q_pos = bi * ATTN_BLOCK + jnp.arange(ATTN_BLOCK)
        s = jnp.where(key_pos[None, :] <= q_pos[:, None], s, -1e30)
        pr = jax.nn.softmax(s, axis=-1).astype(v.dtype)
        return jnp.einsum('bhqk,bkhv->bqhv', pr, v)

    o = lax.map(one, (qb, jnp.arange(nb)))
    return o.transpose(1, 0, 2, 3, 4).reshape(B, S, H, v.shape[-1])

def hybrid_layer(x, p_l, pos, norm_mix, w_in, ret_norm, q_lat_norm, kv_lat_norm, w_uq, w_ukv,
                 q_norm, k_norm, w_br, w_bm, w_o, norm_mlp, w_up, w_down, norm_ple, w_ple_gate, w_ple):
    B, S, _ = x.shape
    h = rms_norm(x, norm_mix)
    proj = h @ w_in
    offsets = np.cumsum(IN_SIZES)[:-1].tolist()
    rq, rk, rv, rg, cq, ckv, krope, gr, gm = jnp.split(proj, offsets, axis=-1)

    rq = rope(rq.reshape(B, S, RET_HEADS, RET_QK_DIM), pos)
    rk = rope(rk.reshape(B, S, RET_HEADS, RET_QK_DIM), pos) * (RET_QK_DIM ** -0.5)
    rv = rv.reshape(B, S, RET_HEADS, RET_V_DIM)
    ro = retention(rq, rk, rv)
    ro = rms_norm(ro, ret_norm.reshape(RET_HEADS, RET_V_DIM)).reshape(B, S, RET_V_W)
    a_ret = (ro * jax.nn.silu(rg)) @ w_br

    cq = rms_norm(cq, q_lat_norm)
    q = (cq @ w_uq).reshape(B, S, MLA_HEADS, MLA_QK_DIM)
    ckv = rms_norm(ckv, kv_lat_norm)
    kv = (ckv @ w_ukv).reshape(B, S, MLA_HEADS, MLA_NOPE_DIM + MLA_V_DIM)
    k_nope, v = kv[..., :MLA_NOPE_DIM], kv[..., MLA_NOPE_DIM:]
    k_rope = jnp.broadcast_to(krope[:, :, None, :], (B, S, MLA_HEADS, MLA_ROPE_DIM))
    k = jnp.concatenate([k_nope, k_rope], axis=-1)
    q = rms_norm(q, q_norm)
    k = rms_norm(k, k_norm)
    q = jnp.concatenate([q[..., :MLA_NOPE_DIM], rope(q[..., MLA_NOPE_DIM:], pos)], axis=-1)
    k = jnp.concatenate([k[..., :MLA_NOPE_DIM], rope(k[..., MLA_NOPE_DIM:], pos)], axis=-1)
    mo = causal_block_attention(q, k, v).reshape(B, S, MLA_V_W)
    a_mla = mo @ w_bm

    mixed = jax.nn.sigmoid(gr) * a_ret + jax.nn.sigmoid(gm) * a_mla
    x = x + mixed @ w_o

    h2 = rms_norm(x, norm_mlp)
    x = x + jnp.square(jax.nn.relu(h2 @ w_up)) @ w_down

    gate = jax.nn.sigmoid(rms_norm(x, norm_ple) @ w_ple_gate)
    x = x + gate * (p_l @ w_ple)
    return x

def second_inputs(seed: int = 0) -> dict:
    key = jax.random.key(seed)
    ks = jax.random.split(key, 24)

    def dense(k, shape, fan_in):
        return jax.random.normal(k, shape, jnp.float32) * (fan_in ** -0.5)

    def gain(k, n):
        return 1.0 + 0.05 * jax.random.normal(k, (DEPTH_2, n), jnp.float32)

    x = jax.random.normal(ks[0], (BATCH, SEQ, D_MODEL), jnp.float32)
    p = jax.random.normal(ks[1], (DEPTH_2, BATCH, SEQ, PLE_DIM), jnp.float32)
    offset = jax.random.randint(ks[2], (BATCH, 1), 0, 1024, dtype=jnp.int32)
    positions = offset + jnp.arange(SEQ, dtype=jnp.int32)[None, :]
    return {
        "x": x,
        "p": p,
        "positions": positions,
        "norm_mix": gain(ks[3], D_MODEL),
        "w_in": dense(ks[4], (DEPTH_2, D_MODEL, IN_WIDTH), D_MODEL),
        "ret_norm": gain(ks[5], RET_V_W),
        "q_lat_norm": gain(ks[6], MLA_Q_LORA),
        "kv_lat_norm": gain(ks[7], MLA_KV_LORA),
        "w_uq": dense(ks[8], (DEPTH_2, MLA_Q_LORA, MLA_HEADS * MLA_QK_DIM), MLA_Q_LORA),
        "w_ukv": dense(ks[9], (DEPTH_2, MLA_KV_LORA, MLA_HEADS * (MLA_NOPE_DIM + MLA_V_DIM)), MLA_KV_LORA),
        "q_norm": gain(ks[10], MLA_QK_DIM),
        "k_norm": gain(ks[11], MLA_QK_DIM),
        "w_br": dense(ks[12], (DEPTH_2, RET_V_W, D_MODEL), RET_V_W),
        "w_bm": dense(ks[13], (DEPTH_2, MLA_V_W, D_MODEL), MLA_V_W),
        "w_o": dense(ks[14], (DEPTH_2, D_MODEL, D_MODEL), D_MODEL),
        "norm_mlp": gain(ks[15], D_MODEL),
        "w_up": dense(ks[16], (DEPTH_2, D_MODEL, D_FF_2), D_MODEL),
        "w_down": dense(ks[17], (DEPTH_2, D_FF_2, D_MODEL), D_FF_2),
        "norm_ple": gain(ks[18], D_MODEL),
        "w_ple_gate": dense(ks[19], (DEPTH_2, D_MODEL, D_MODEL), D_MODEL),
        "w_ple": dense(ks[20], (DEPTH_2, PLE_DIM, D_MODEL), PLE_DIM),
    }

def second_block(x, p, positions, norm_mix, w_in, ret_norm, q_lat_norm, kv_lat_norm, w_uq, w_ukv,
              q_norm, k_norm, w_br, w_bm, w_o, norm_mlp, w_up, w_down, norm_ple, w_ple_gate, w_ple):
    for i in range(DEPTH_2):
        x = hybrid_layer(x, p[i], positions, norm_mix[i], w_in[i], ret_norm[i], q_lat_norm[i],
                         kv_lat_norm[i], w_uq[i], w_ukv[i], q_norm[i], k_norm[i], w_br[i], w_bm[i],
                         w_o[i], norm_mlp[i], w_up[i], w_down[i], norm_ple[i], w_ple_gate[i], w_ple[i])
    return x


def setup_inputs(seed=0):
    out = dict(first_inputs(seed))
    for name, value in second_inputs(seed + 1).items():
        if name != "x":
            out[name + "_2"] = value
    return out


def reference(
    x, rel_bias, attn_norm, attn_w_in, attn_lambda_q1, attn_lambda_k1, attn_lambda_q2,
    attn_lambda_k2, attn_subln, attn_w_out, mlstm_norm, mlstm_w_in, mlstm_b_i, mlstm_b_f,
    mlstm_conv_w, mlstm_conv_b, mlstm_head_norm, mlstm_w_out, mlp_norm, mlp_w1, mlp_w2,
    final_norm, p_2, positions_2, norm_mix_2, w_in_2, ret_norm_2, q_lat_norm_2, kv_lat_norm_2,
    w_uq_2, w_ukv_2, q_norm_2, k_norm_2, w_br_2, w_bm_2, w_o_2, norm_mlp_2, w_up_2, w_down_2,
    norm_ple_2, w_ple_gate_2, w_ple_2,
):
    x = first_block(
        x, rel_bias, attn_norm, attn_w_in, attn_lambda_q1, attn_lambda_k1, attn_lambda_q2,
        attn_lambda_k2, attn_subln, attn_w_out, mlstm_norm, mlstm_w_in, mlstm_b_i, mlstm_b_f,
        mlstm_conv_w, mlstm_conv_b, mlstm_head_norm, mlstm_w_out, mlp_norm, mlp_w1, mlp_w2,
        final_norm,
    )
    return second_block(
        x, p_2, positions_2, norm_mix_2, w_in_2, ret_norm_2, q_lat_norm_2, kv_lat_norm_2,
        w_uq_2, w_ukv_2, q_norm_2, k_norm_2, w_br_2, w_bm_2, w_o_2, norm_mlp_2, w_up_2,
        w_down_2, norm_ple_2, w_ple_gate_2, w_ple_2,
    )


_drawn_inputs = setup_inputs


def setup_inputs(seed=0):
    import zlib

    import numpy as np

    out = dict(_drawn_inputs(seed))
    spreads = {}
    factors = {'mlstm_b_i': 64.0,
     'mlstm_conv_b': 8.0,
     'mlstm_head_norm': 2.814,
     'ret_norm_2': 10.796,
     'q_lat_norm_2': 8.0,
     'kv_lat_norm_2': 4.75,
     'q_norm_2': 8.0,
     'k_norm_2': 8.0,
     'norm_ple_2': 146.935,
     'norm_mlp_2': 3.539}
    for name, (base, spread) in spreads.items():
        noise = np.random.default_rng([zlib.crc32(name.encode()), seed]).standard_normal(out[name].shape)
        drawn = base * np.exp(spread * noise) if base else spread * noise
        out[name] = __import__('jax').numpy.asarray(drawn.astype(out[name].dtype))
    for name, factor in factors.items():
        out[name] = (out[name] * factor).astype(out[name].dtype)
    return out
```

```python
import math
from contextlib import ExitStack

import numpy as np

import concourse.bass as bass
from concourse import mybir

F32 = mybir.dt.float32
F32R = mybir.dt.float32r
BF16 = mybir.dt.bfloat16
I32 = mybir.dt.int32
ALU = mybir.AluOpType
ACT = mybir.ActivationFunctionType
AXIS = mybir.AxisListType.X

P = 128
S = 256
TT = S // P
D = 1024
DC = D // P
FF = 4 * D
HALF = 512
EPS = 1e-6
NEG = -1e30

UNIT = 1024
RAW = 4
RING = 8
AHEAD = 5

DA_H, DA_D = 8, 64
ML_H, ML_QK, ML_V = 4, 128, 256
CONV = 4
RET_H, RET_QK, RET_V = 4, 256, 512
MLA_H, NOPE, ROPE = 8, 128, 64
MLA_QK = NOPE + ROPE
Q_LORA, KV_LORA = 384, 256
LAT = Q_LORA + KV_LORA
BUCKETS = 32
LAMBDA_INIT = 0.8 - 0.6 * math.exp(-0.3 * 0)

WIDE, TALL = slice(0, 2 * P), slice(2 * P, 3 * P)
SCORE = 3 * P

GAIN_ROWS = [("attn_norm", 8), ("mlp_norm", 16), ("mlstm_norm", 8), ("mlstm_head_norm", 8), ("norm_mix_2", 8),
             ("ret_norm_2", 16), ("q_lat_norm_2", 3), ("kv_lat_norm_2", 2), ("norm_mlp_2", 8), ("norm_ple_2", 8),
             ("attn_subln", 1), ("mlstm_conv_w", 32), ("mlstm_conv_b", 8), ("q_norm_2", 1), ("k_norm_2", 1)]
GAIN = {}
for _name, _rows in GAIN_ROWS:
    GAIN[_name] = sum(r for n, r in GAIN_ROWS[:len(GAIN)])
assert sum(r for _, r in GAIN_ROWS) == P

TWO_PI = 2 * math.pi
PI_A = 6.28125
PI_B = float(np.float32(math.floor((TWO_PI - PI_A) * 2**20) / 2**20))
PI_C = TWO_PI - PI_A - PI_B
ROUND = 1.5 * 2**23
PI_SAFE = 3.1415925


def constants():
    i = np.arange(P)
    causal = np.where(i[:, None] >= i[None, :], 0.0, NEG)
    dist = S - 1 - np.arange(3 * P - 1)
    d = np.maximum(dist, 1).astype(np.float32)
    exact = BUCKETS // 2
    large = exact + (np.log(d / exact) / math.log(128 / exact) * (BUCKETS - exact)).astype(np.int32)
    bucket = np.where(dist < exact, dist, np.minimum(large, BUCKETS - 1))
    bucket = np.where(dist < 0, BUCKETS, bucket)
    onehot = bucket[None, :] == np.arange(BUCKETS + 1)[:, None]
    log_g = np.log1p(-np.exp2(-5.0 - np.arange(RET_H)))
    diff = np.arange(S)[None, :] - i[:, None]
    wide = np.where(diff[:, None, :] >= 0, np.exp(np.maximum(diff, 0)[:, None, :] * log_g[None, :, None]), 0.0)
    decay = np.concatenate([wide, wide[:, :, 0:P]], axis=2)
    inv = [10000.0 ** (-np.arange(n, dtype=np.float32) / np.float32(n)) for n in (RET_QK // 2, ROPE // 2)]
    square = np.stack([np.eye(P), np.ones((P, P)), i[:, None] <= i[None, :], causal, causal.T], axis=1)
    mask = np.concatenate([np.zeros((P, P)), causal, causal], axis=1)
    out = {"c_square": square, "c_onehot": onehot, "c_decay": decay, "c_inv": np.concatenate(inv)[None, :],
           "c_mask": mask}
    return {k: np.ascontiguousarray(v, dtype=np.float32) for k, v in out.items()}


NINV = RET_QK // 2 + ROPE // 2


def schedule(w):
    groups, stream = {}, []
    count = [0]

    def group(name, weight, col, ncols, source, nchunks, act, dve, rows=0, per=2):
        units, c = [], 0
        while weight is not None and c < nchunks:
            n = min(per, nchunks - c)
            src = weight[rows + c * P:rows + (c + n) * P, col:col + ncols].rearrange("(c p) n -> p c n", p=P)
            units.append((count[0], c, n))
            stream.append(("unit", count[0], src, n, ncols))
            count[0] += 1
            c += n
        groups[name] = dict(index=len(groups), units=units, ncols=ncols, source=source, act=act, dve=dve)

    def mlp(which, w1, w2):
        stream.append(("mlp", count[0], w1, w2, which))
        mlps.append(count[0])
        count[0] += 2 * 4 * (FF // HALF)

    mlps = []
    qkv = w["attn_w_in"]
    for name, col in (("q0", 0), ("k0", D), ("q1", HALF), ("k1", D + HALF), ("v0", 2 * D), ("v1", 2 * D + HALF)):
        group(name, qkv, col, HALF, "x0", DC, 2, 0)
    for n in range(2):
        group(f"ao{n}", w["attn_w_out"], n * HALF, HALF, "oT", DC, 0, 0)
    mlp(0, w["mlp_w1"][0], w["mlp_w2"][0])
    ml = w["mlstm_w_in"]
    group("gate", ml, 3 * D, 2 * ML_H, "x2", DC, 2, 0, per=8)
    for name, col in (("mq", 0), ("mk", HALF), ("mv0", D), ("mv1", D + HALF), ("mo0", 2 * D), ("mo1", 2 * D + HALF)):
        group(name, ml, col, HALF, "x2", DC, 2, 0)
    for n in range(2):
        group(f"mw{n}", w["mlstm_w_out"], n * HALF, HALF, "yT", DC, 0, 0)
    mlp(1, w["mlp_w1"][1], w["mlp_w2"][1])
    win = w["w_in_2"]
    at = np.cumsum([0, D, D, 2 * D, 2 * D, Q_LORA, KV_LORA + ROPE, D, D]).tolist()
    group("cq", win, at[4], Q_LORA, "x5", DC, 2, 0)
    group("ckv", win, at[5], KV_LORA + ROPE, "x5", DC, 2, 0)
    for name, col in (("rq0", at[0]), ("rq1", at[0] + HALF), ("rk0", at[1]), ("rk1", at[1] + HALF)):
        group(name, win, col, HALF, "x5", DC, 2, 0)
    for n in range(3):
        group(f"uq{n}", w["w_uq_2"], n * HALF, HALF, "latq", Q_LORA // P, 2, 0)
    for n in range(4):
        group(f"ukv{n}", w["w_ukv_2"], n * HALF, HALF, "latkv", KV_LORA // P, 2, 0)
    for n in range(4):
        group(f"rv{n}", win, at[2] + n * HALF, HALF, "x5", DC, 2, 0)
        if n:
            group(f"ret{n - 1}", None, 0, HALF, None, 0, 2, 2)
    group("rg0", win, at[3], HALF, "x5", DC, 2, 2)
    group("ret3", None, 0, HALF, None, 0, 2, 2)
    for n in range(1, 4):
        group(f"rg{n}", win, at[3] + n * HALF, HALF, "x5", DC, 2, 2)
    for name, col in (("gm0", at[7]), ("gm1", at[7] + HALF), ("gr0", at[6]), ("gr1", at[6] + HALF)):
        group(name, win, col, HALF, "x5", DC, 2, 0)
    for n in range(2):
        group(f"br{n}", w["w_br_2"], n * HALF, HALF, "roT", 2 * DC, 0, 2)
    for n in range(2):
        group(f"bm{n}", w["w_bm_2"], n * HALF, HALF, "moT", DC, 0, 2)
    for n in range(2):
        group(f"wo{n}", w["w_o_2"], n * HALF, HALF, "mixT", DC, 0, 0)
    mlp(2, w["w_up_2"], w["w_down_2"])
    for n in range(2):
        group(f"pl{n}", w["w_ple_2"], n * HALF, HALF, "pT", 2, 2, 0)
    for n in range(2):
        group(f"pg{n}", w["w_ple_gate_2"], n * HALF, HALF, "x7", DC, 2, 0)

    act = dve = 0
    by_index = []
    for g in groups.values():
        act, dve = act + g["act"], dve + g["dve"]
        g["act_end"], g["dve_end"] = act, dve
        by_index.append(g)
    return groups, by_index, stream, mlps


def turns():
    order = [("gains", 1, 0)]

    def split(name, chunks):
        c = 0
        for n in chunks:
            order.append((f"{name}.{c}", n, n))
            c += n

    pairs = [2] * (DC // 2)
    split("x0", pairs)
    for name in ("q0", "k0", "q1", "k1"):
        order.extend([(f"{name}a", 0, 1), (f"{name}b", 0, 1)])
    for h in range(DA_H + 1):
        if h:
            order.append((f"av{h - 1}", 2, 1))
        if h in (6, 8):
            split(f"oT{h // 8}", [2, 2])
        if h < DA_H:
            order.append((f"ap{h}", 1, 0))
    split("x1", pairs)
    split("x2", pairs)
    for b in range(4):
        order.append((f"conv{b}", 0, 1))
    for h in range(ML_H):
        order.extend([(f"mv{h}.0", 1, 1), (f"mv{h}.1", 1, 1)])
    split("yT", pairs)
    split("x3", pairs)
    split("x5", pairs)
    split("lat", [2, 2, 1])
    for name in ("rq0", "rq1", "rk0", "rk1"):
        order.extend([(f"{name}a", 0, 1), (f"{name}b", 0, 1)])
    for name in ("mq", "mk"):
        order.extend([(f"{name}n{b}", 1, 0) for b in range(4)])
        order.extend([(f"{name}r{b}", 0, 1) for b in range(2)])
    for h in range(MLA_H + 1):
        if h:
            order.append((f"lv{h - 1}", 2, 0))
        if h < MLA_H:
            order.append((f"lp{h}", 1, 0))
    split("roT", pairs + pairs)
    split("moT", pairs)
    split("mixT", pairs)
    split("x6", pairs)
    split("pT", [2])
    split("x7", pairs)
    table, act, dve = {}, 0, 0
    for i, (name, a, d) in enumerate(order):
        table[name] = dict(index=i, act=act, dve=dve, act_end=act + a, dve_end=dve + d)
        act, dve = act + a, dve + d
    by_index = [table[name] for name, _, _ in order]
    return table, by_index


def turn_of(source, c):
    if source == "oT":
        name, c = f"oT{c // 4}", c % 4
    elif source == "latq":
        name = "lat"
    elif source == "latkv":
        name, c = "lat", c + Q_LORA // P
    else:
        name = source
    return f"{name}.{c // 2 * 2}", c % 2


def build(nc, w, out):
    groups, group_list, stream, mlps = schedule(w)
    turn, turn_list = turns()
    total_units = stream[-1][1] + 1
    NX = 8

    with ExitStack() as ctx:
        def sb(name, shape, dt=F32, scope=ctx):
            return scope.enter_context(nc.sbuf_tensor(name, [P, *shape], dt))

        def sem(name):
            return ctx.enter_context(nc.semaphore(name))

        x = sb("x", [TT, D])
        raw = sb("raw", [RAW, UNIT])
        w_hi = sb("w_hi", [RING, UNIT], F32R)
        w_lo = sb("w_lo", [RING, UNIT], F32R)
        a_hi = sb("a_hi", [DC, S], F32R)
        a_lo = sb("a_lo", [DC, S], F32R)
        junk = sb("junk", [D], BF16)
        square = sb("square", [5, P])
        ident, ones, triu, causal, causal_t = (square[:, i, :] for i in range(5))
        gains = sb("gains", [P])
        trig = sb("trig", [2, TT, NINV])
        zeros = sb("zeros", [HALF], BF16)
        mhalf = sb("mhalf", [2 * DA_H])
        ssx = sb("ssx", [NX, TT])
        msx = sb("msx", [NX, TT])
        rstd = sb("rstd", [NX, TT])
        inv_ms = sb("inv_ms", [NX, TT])
        lam_s = sb("lam_s", [2])
        lam_e = sb("lam_e", [2])
        neg_lam = sb("neg_lam", [1])

        with ExitStack() as ph:
            qk_sb = sb("qk_sb", [2, TT, HALF], scope=ph)
            da_q = sb("da_q", [DA_H, S], scope=ph)
            da_k = sb("da_k", [DA_H, S], scope=ph)
            da_v = sb("da_v", [TT, D], scope=ph)
            bias = sb("bias", [DA_H, SCORE], scope=ph)
            da_e = sb("da_e", [2, 2, SCORE], scope=ph)
            da_p = sb("da_p", [DA_H, SCORE], scope=ph)
            da_pt = sb("da_pt", [2, SCORE], scope=ph)
            da_o = sb("da_o", [TT, D], scope=ph)
            o_hi = sb("o_hi", [DC, S], F32R, scope=ph)
            o_lo = sb("o_lo", [DC, S], F32R, scope=ph)
            da_nm = sb("da_nm", [2, 4], scope=ph)
            da_sum = sb("da_sum", [2, 4], scope=ph)
            da_rec = sb("da_rec", [2, 4], scope=ph)
            da_nl = sb("da_nl", [2, 2], scope=ph)
            da_ss = sb("da_ss", [2, TT, DA_H // 2], scope=ph)
            da_ms = sb("da_ms", [2, TT, DA_H // 2], scope=ph)
            da_r = sb("da_r", [2, TT, DA_H // 2], scope=ph)
        with ExitStack() as ph:
            sb("below_setup", [2 * TT * HALF + 2 * DA_H * S], scope=ph)
            gain_rows = sb("gain_rows", [P], scope=ph)
            onehot = sb("onehot", [3 * P - 1], scope=ph)
            table = sb("table", [DA_H], scope=ph)
            bias_rows = sb("bias_rows", [3 * P - 1], scope=ph)
            lam_in = sb("lam_in", [4, DA_D], scope=ph)
            lam_prod = sb("lam_prod", [2, DA_D], scope=ph)
            pos_i = sb("pos_i", [TT], I32, scope=ph)
            pos_f = sb("pos_f", [TT], scope=ph)
            inv = sb("inv", [NINV], scope=ph)
        with ExitStack() as ph:
            sb("below_angles", [2 * TT * HALF + 2 * DA_H * S + TT * D + DA_H * SCORE + 4 * SCORE + DA_H * SCORE
                                + 2 * SCORE], scope=ph)
            ang = sb("ang", [2, TT, NINV], scope=ph)
            turns_k = sb("turns_k", [2, TT, NINV], scope=ph)

        with ExitStack() as ph:
            relu = sb("relu", [TT, HALF], scope=ph)
            hid = sb("hid", [TT, HALF], scope=ph)
            h_hi = sb("h_hi", [HALF // P, S], F32R, scope=ph)
            h_lo = sb("h_lo", [HALF // P, S], F32R, scope=ph)
            final_gain = sb("final_gain", [D], scope=ph)
            p_sb = sb("p_sb", [TT, 2 * P], scope=ph)
            p_hi = sb("p_hi", [2, S], F32R, scope=ph)
            p_lo = sb("p_lo", [2, S], F32R, scope=ph)
            ple = sb("ple", [TT, D], scope=ph)
            gate = sb("gate", [TT, D], scope=ph)

        with ExitStack() as ph:
            ml_qk = sb("ml_qk", [2, TT, HALF], scope=ph)
            ml_t = sb("ml_t", [2 * ML_H, S], scope=ph)
            ml_sig = sb("ml_sig", [2, 2, S], scope=ph)
            ml_v = sb("ml_v", [TT, ML_H, ML_V + 1], scope=ph)
            ml_o = sb("ml_o", [TT, D], scope=ph)
            ml_n = sb("ml_n", [TT, ML_H, ML_V + 1], scope=ph)
            ml_w = sb("ml_w", [ML_H, SCORE], scope=ph)
            ml_s = sb("ml_s", [ML_H, SCORE], scope=ph)
            diag = sb("diag", [ML_H, S], scope=ph)
            maxed = sb("maxed", [ML_H, P], scope=ph)
            y_hi = sb("y_hi", [DC, S], F32R, scope=ph)
            y_lo = sb("y_lo", [DC, S], F32R, scope=ph)
            gate_b = sb("gate_b", [2 * ML_H], scope=ph)
            ml_g = sb("ml_g", [14, TT, ML_H], scope=ph)
            (g_fz, g_nfz, g_abs, g_exp, g_ln, g_lf, g_i, g_F, g_g, g_max, g_max2, g_nm, g_em, g_den) = (
                ml_g[:, i, :, :] for i in range(14))
            ml_r = sb("ml_r", [8, TT, ML_H], scope=ph)
            (r_abs, r_dmax, r_dinv, r_ss, r_t, r_ms, r_r, r_sc) = (ml_r[:, i, :, :] for i in range(8))
            gate_in = sb("gate_in", [TT, 2 * ML_H], scope=ph)

        ph = ctx
        lq_sb = sb("lq_sb", [TT, MLA_H, MLA_QK], scope=ph)
        ret = sb("ret", [TT, RET_H * RET_V], scope=ph)
        ret_s = sb("ret_s", [RET_H, SCORE], scope=ph)
        work = sb("work", [2, TT, HALF], scope=ph)
        mask = sb("mask", [SCORE], scope=ph)
        rope_gain = sb("rope_gain", [2, ROPE], scope=ph)
        lat_ss = sb("lat_ss", [2, TT], scope=ph)
        lat_ms = sb("lat_ms", [2, TT], scope=ph)
        lat_r = sb("lat_r", [2, TT], scope=ph)
        lq_ss = sb("lq_ss", [TT, MLA_H], scope=ph)
        lq_ms = sb("lq_ms", [TT, MLA_H], scope=ph)
        lq_r = sb("lq_r", [TT, MLA_H], scope=ph)
        lk_ss = sb("lk_ss", [TT, MLA_H], scope=ph)
        lk_ms = sb("lk_ms", [TT, MLA_H], scope=ph)
        lk_r = sb("lk_r", [TT, MLA_H], scope=ph)
        kr_ss = sb("kr_ss", [TT], scope=ph)
        l_nm = sb("l_nm", [2, TT], scope=ph)
        l_sum = sb("l_sum", [2, TT], scope=ph)
        l_rec = sb("l_rec", [2, TT], scope=ph)
        ret_ss = sb("ret_ss", [TT, RET_H], scope=ph)
        ret_ms = sb("ret_ms", [TT, RET_H], scope=ph)
        ret_r = sb("ret_r", [TT, RET_H], scope=ph)
        kr_sb = sb("kr_sb", [4, TT, ROPE], scope=ph)
        ret_t = ret[:, :, :].rearrange("p t n -> p (t n)").rearrange("p (c s) -> p c s", s=S)
        rq_t, rk_t = ret_t[:, 0:DC, :], ret_t[:, DC:2 * DC, :]
        flat_q = lq_sb[:, :, :, :].rearrange("p t h d -> p (t h d)")
        lo_sb = flat_q[:, 0:TT * D].rearrange("p (t n) -> p t n", t=TT)
        mix = lo_sb
        KV = TT * MLA_H * (NOPE + P)
        with ExitStack() as ph:
            lat_sb = sb("lat_sb", [TT, LAT + ROPE], scope=ph)
            sb("below_lat", [KV - TT * (LAT + ROPE)], scope=ph)
            lat_hi = sb("lat_hi", [LAT // P, S], F32R, scope=ph)
            lat_lo = sb("lat_lo", [LAT // P, S], F32R, scope=ph)
        with ExitStack() as ph:
            kv = sb("kv", [TT, MLA_H, NOPE + P], scope=ph)
            lq_n = sb("lq_n", [MLA_H, S], scope=ph)
            lq_t = sb("lq_t", [MLA_H // 2, S], scope=ph)
            lk_n = sb("lk_n", [MLA_H, S], scope=ph)
            lk_t = sb("lk_t", [MLA_H // 2, S], scope=ph)
            l_work = sb("l_work", [2048], scope=ph)
        lk_flat = lk_n[:, :, :].rearrange("p h s -> p (h s)")
        rot = l_work[:, 0:TT * MLA_H * ROPE].rearrange("p (t h d) -> p t h d", t=TT, h=MLA_H)
        prod = l_work[:, 1024:2048].rearrange("p (t h d) -> p t h d", t=TT, h=MLA_H)
        l_e = l_work[:, 0:2 * SCORE].rearrange("p (b n) -> p b n", b=2)
        l_pt = l_work[:, 2 * SCORE:4 * SCORE].rearrange("p (b n) -> p b n", b=2)
        with ExitStack() as ph:
            gm = sb("gm", [TT, D], scope=ph)
            gr = sb("gr", [TT, D], scope=ph)
            b_hi = sb("b_hi", [2 * DC, S], F32R, scope=ph)
            b_lo = sb("b_lo", [2 * DC, S], F32R, scope=ph)

        pair = [ctx.enter_context(nc.psum_tensor(f"pair{i}", [P, TT, HALF], F32)) for i in range(2)]
        turn_ps = ctx.enter_context(nc.psum_tensor("turn_ps", [P, 2, HALF], F32))
        score = ctx.enter_context(nc.psum_tensor("score", [P, 2, HALF], F32))
        down = [pair[1], score]

        landed = [sem(f"landed{i}") for i in range(RAW)]
        hi_ready = sem("hi_ready")
        lo_ready = sem("lo_ready")
        unit_used = sem("unit_used")
        group_act = sem("group_act")
        group_dve = sem("group_dve")
        turn_filled = sem("turn_filled")
        turn_act = sem("turn_act")
        turn_dve = sem("turn_dve")
        x_loaded = sem("x_loaded")
        x_ready = sem("x_ready")
        x_squared = sem("x_squared")
        rstd_ready = sem("rstd_ready")
        inv_ready = sem("inv_ready")
        act_step = sem("act_step")
        dve_step = sem("dve_step")
        pool_step = sem("pool_step")
        const_loaded = sem("const_loaded")
        gains_loaded = sem("gains_loaded")
        small_loaded = sem("small_loaded")
        pos_loaded = sem("pos_loaded")
        set_ready = sem("set_ready")
        table_ready = sem("table_ready")
        bias_psum = sem("bias_psum")
        bias_rows_ready = sem("bias_rows_ready")
        bias_stored = sem("bias_stored")
        bias_loaded = sem("bias_loaded")
        lam_loaded = sem("lam_loaded")
        lam_sum = sem("lam_sum")
        lam_exp = sem("lam_exp")
        angles_ready = sem("angles_ready")
        trig_ready = sem("trig_ready")
        da_scored = sem("da_scored")
        da_biased = sem("da_biased")
        da_maxed = sem("da_maxed")
        da_exped = sem("da_exped")
        da_mixed = sem("da_mixed")
        da_norm = sem("da_norm")
        da_scaled = sem("da_scaled")
        up_relu = sem("up_relu")
        hid_ready = sem("hid_ready")
        hid_turned = sem("hid_turned")
        hid_hi = sem("hid_hi")
        hid_lo = sem("hid_lo")
        fgain_loaded = sem("fgain_loaded")
        ml_loaded = sem("ml_loaded")
        ml_abs = sem("ml_abs")
        ml_ln = sem("ml_ln")
        ml_lf = sem("ml_lf")
        ml_cum = sem("ml_cum")
        ml_diag = sem("ml_diag")
        ml_spread = sem("ml_spread")
        ml_args = sem("ml_args")
        ml_wexp = sem("ml_wexp")
        ml_em = sem("ml_em")
        ml_ones = sem("ml_ones")
        ml_sigm = sem("ml_sigm")
        ml_silu = sem("ml_silu")
        ml_scored = sem("ml_scored")
        ml_weighted = sem("ml_weighted")
        ml_ms = sem("ml_ms")
        ml_norm = sem("ml_norm")
        ml_y = sem("ml_y")
        b2_loaded = sem("b2_loaded")
        ret_roped = sem("ret_roped")
        lat_sq = sem("lat_sq")
        lat_norm = sem("lat_norm")
        ret_scored = sem("ret_scored")
        ret_decayed = sem("ret_decayed")
        ret_out = sem("ret_out")
        ret_norm = sem("ret_norm")
        l_squares = sem("l_squares")
        l_sq = sem("l_sq")
        l_norm = sem("l_norm")
        lq_ready = sem("lq_ready")
        lk_ready = sem("lk_ready")
        l_scored = sem("l_scored")
        l_masked = sem("l_masked")
        l_maxed = sem("l_maxed")
        l_exped = sem("l_exped")
        l_reced = sem("l_reced")
        gated = sem("gated")
        mixed = sem("mixed")
        p_loaded = sem("p_loaded")
        out_ready = sem("out_ready")
        out_stored = sem("out_stored")

        bias_dram = nc.dram_tensor("bias_scratch", (DA_H, SCORE), F32, kind="Internal").ap()
        bias_rep = nc.dram_tensor("bias_replicas", (P, DA_H, SCORE), F32, kind="Internal").ap()

        def own_order(eng, step):
            count = [0]

            def mark(ins):
                ins.then_inc(step, 1)
                count[0] += 1
                return count[0]

            def wait(n=None):
                eng.wait_ge(step, count[0] if n is None else n)
            return mark, wait

        def gain(name, c):
            i = GAIN[name] + c
            return gains[:, i:i + 1]

        def wait_group(eng, name):
            eng.wait_ge(unit_used, groups[name]["units"][-1][0] + 1)

        def group_ps(name):
            return pair[groups[name]["index"] % 2]

        def turn_bank(name):
            return turn_ps[:, turn[name]["index"] % 2, :]

        def wait_turn(eng, name):
            eng.wait_ge(turn_filled, turn[name]["index"] + 1)

        OPERAND = {"x0": (a_hi, a_lo, 0), "x2": (a_hi, a_lo, 0), "x5": (a_hi, a_lo, 0), "x7": (a_hi, a_lo, 0),
                   "oT": (o_hi, o_lo, 0), "yT": (y_hi, y_lo, 0), "latq": (lat_hi, lat_lo, 0),
                   "latkv": (lat_hi, lat_lo, Q_LORA // P), "roT": (b_hi, b_lo, 0), "moT": (a_hi, a_lo, 0),
                   "mixT": (b_hi, b_lo, 0), "pT": (p_hi, p_lo, 0)}
        SPLIT = {"x0": (a_hi, a_lo, "attn_norm", 0), "x1": (a_hi, a_lo, "mlp_norm", 0),
                 "x2": (a_hi, a_lo, "mlstm_norm", 0), "x3": (a_hi, a_lo, "mlp_norm", DC),
                 "x5": (a_hi, a_lo, "norm_mix_2", 0), "x6": (a_hi, a_lo, "norm_mlp_2", 0),
                 "x7": (a_hi, a_lo, "norm_ple_2", 0), "oT0": (o_hi, o_lo, "attn_subln", None),
                 "oT1": (o_hi, o_lo, "attn_subln", None), "yT": (y_hi, y_lo, "mlstm_head_norm", 0),
                 "lat": (lat_hi, lat_lo, "q_lat_norm_2", 0), "roT": (b_hi, b_lo, "ret_norm_2", 0),
                 "moT": (a_hi, a_lo, None, 0), "mixT": (b_hi, b_lo, None, 0), "pT": (p_hi, p_lo, None, 0)}

        def split_parts(name):
            base, c0 = name.split(".")
            hi, lo, g, at = SPLIT[base]
            c0 = int(c0)
            n = turn[name]["act_end"] - turn[name]["act"]
            for j in range(n):
                c = c0 + j + (4 if base == "oT1" else 0)
                scale = None if g is None else gain(g, 0 if at is None else at + c)
                yield turn_bank(name)[:, j * S:(j + 1) * S], hi[:, c, :], lo[:, c, :], scale

        def run_group(name, each, slots=None):
            for n, unit in enumerate(groups[name]["units"]):
                each(unit)
                if slots and n in slots:
                    slots[n]()

        def x_version(v, nblocks=4):
            return 4 * (v - 1) + nblocks

        block = ctx.enter_context(nc.Block())

        @block.sync
        def _(sp):
            for tt in range(TT):
                sp.dma_start(x[:, tt, :], w["x"][0, tt * P:(tt + 1) * P, :]).then_inc(x_loaded, 16)

            def load(k, src, chunks, ncols, it=None):
                if it is not None or k >= RAW:
                    used = k - RAW + 1
                    sp.wait_ge(lo_ready, used if it is None else it * RING + used)
                dst = raw[:, k % RAW, 0:chunks * ncols].rearrange("p (c n) -> p c n", n=ncols)
                sp.dma_start(dst, src).then_inc(landed[k % RAW], 16)

            def load_up(w1, k, i, it=None):
                cols = slice(i * HALF, (i + 1) * HALF) if it is None else bass.ds(it * HALF, HALF)
                rows = w1.rearrange("(c p) n -> p c n", p=P)
                for u in range(4):
                    load(k + u, rows[:, 2 * u:2 * u + 2, cols], 2, HALF, it)

            def load_down(w2, k, i, it=None):
                for u in range(4):
                    at = i * HALF + u * P if it is None else it * HALF + (u * P - HALF)
                    src = w2[at:at + P, :] if it is None else w2[bass.ds(at, P), :]
                    load(k + u, src.rearrange("p (c n) -> p c n", c=1), 1, D, it)

            for item in stream:
                if item[0] == "unit":
                    _, k, src, chunks, ncols = item
                    load(k, src, chunks, ncols)
                else:
                    _, k, w1, w2, _ = item
                    load_up(w1, k, 0)
                    with sp.Fori(1, FF // HALF) as i:
                        load_up(w1, k - 4, None, i)
                        load_down(w2, k, None, i)
                    load_down(w2, k + 60, FF // HALF - 1)
            for n in range(2):
                for tt in range(TT):
                    sp.wait_ge(out_ready, 2 * n + tt + 1)
                    sp.dma_start(out[0, tt * P:(tt + 1) * P, n * HALF:(n + 1) * HALF],
                                 gate[:, tt, n * HALF:(n + 1) * HALF]).then_inc(out_stored, 16)
            sp.wait_ge(out_stored, 64)

        @block.tensor
        def _(pe):
            seen = {"source": 0}
            next_turn = [0]

            def product(o, hi, lo, whi, wlo, start, stop):
                pe.matmul(o, hi, whi, start=start, stop=False)
                pe.matmul(o, hi, wlo, start=False, stop=False)
                return pe.matmul(o, lo, whi, start=False, stop=stop)

            def wait_source(source, c):
                name, j = turn_of(source, c)
                value = turn[name]["dve"] + j + 1
                if value > seen["source"]:
                    pe.wait_ge(turn_dve, value)
                    seen["source"] = value

            def open_turn(name):
                assert turn[name]["index"] == next_turn[0], name
                next_turn[0] += 1
                if turn[name]["index"] >= 2:
                    before = turn_list[turn[name]["index"] - 2]
                    if before["act_end"] > before["act"]:
                        pe.wait_ge(turn_act, before["act_end"])
                    if before["dve_end"] > before["dve"]:
                        pe.wait_ge(turn_dve, before["dve_end"])
                return turn_bank(name)

            def transposed(name, sources):
                bank = open_turn(name)
                for j, src in enumerate(sources):
                    last = pe.transpose(bank[:, j * P:(j + 1) * P], src, ident)
                last.then_inc(turn_filled, 1)

            def chunks_of(tile, c0, n):
                return [tile[:, tt, c * P:(c + 1) * P] for c in range(c0, c0 + n) for tt in range(TT)]

            def x_turn(v, c):
                if v == 0:
                    pe.wait_ge(x_loaded, 16 * TT)
                elif v == 5:
                    pe.wait_ge(x_ready, x_version(5, 2 if c < 4 else 4))
                else:
                    pe.wait_ge(x_ready, x_version(v, 2 if c < 4 else 4))
                transposed(f"x{v}.{c}", chunks_of(x, c, 2))

            def open_pair(name):
                i = groups[name]["index"]
                if i >= 2:
                    before = group_list[i - 2]
                    if before["act"]:
                        pe.wait_ge(group_act, before["act_end"])
                    if before["dve"]:
                        pe.wait_ge(group_dve, before["dve_end"])
                return group_ps(name)

            def dense(name, slots=None):
                g = groups[name]
                ps = open_pair(name)
                hi, lo, c_at = OPERAND[g["source"]]
                ncols, last_c = g["ncols"], g["units"][-1][1] + g["units"][-1][2] - 1

                def unit(u):
                    k, c0, n = u
                    wait_source(g["source"], c0 + n - 1)
                    pe.wait_ge(lo_ready, k + 1)
                    for tt in range(TT):
                        for j in range(n):
                            c = c0 + j
                            cols = slice(j * ncols, (j + 1) * ncols)
                            rows = slice(tt * P, (tt + 1) * P)
                            last = product(ps[:, tt, 0:ncols], hi[:, c_at + c, rows], lo[:, c_at + c, rows],
                                           w_hi[:, k % RING, cols], w_lo[:, k % RING, cols], c == 0, c == last_c)
                    last.then_inc(unit_used, 1)
                run_group(name, unit, slots)

            def mlp(m, source):
                k0 = mlps[m]
                steps = FF // HALF
                h0 = m * steps * TT

                def at(value, it, per):
                    return value if it is None else it * per + value

                def up(k, it=None):
                    for u in range(4):
                        if it is None:
                            wait_source(source, 2 * u + 1)
                        pe.wait_ge(lo_ready, at(k + u + 1, it, RING))
                        for tt in range(TT):
                            for j in range(2):
                                c = 2 * u + j
                                rows, cols = slice(tt * P, (tt + 1) * P), slice(j * HALF, (j + 1) * HALF)
                                slot = (k + u) % RING
                                last = product(pair[0][:, tt, :], a_hi[:, c, rows], a_lo[:, c, rows],
                                               w_hi[:, slot, cols], w_lo[:, slot, cols], c == 0, c == DC - 1)
                        last.then_inc(unit_used, 1)

                def turn_hidden(h, it=None):
                    for tt in range(TT):
                        pe.wait_ge(hid_ready, at(h + tt + 1, it, TT))
                        for c in range(HALF // P):
                            last = pe.transpose(turn_ps[:, tt, c * P:(c + 1) * P], hid[:, tt, c * P:(c + 1) * P], ident)
                        last.then_inc(hid_turned, 1)

                def down_step(k, h, it=None, stop=False):
                    pe.wait_ge(hid_lo, at(h + TT, it, TT))
                    for u in range(4):
                        pe.wait_ge(lo_ready, at(k + u + 1, it, RING))
                        for tt in range(TT):
                            rows = slice(tt * P, (tt + 1) * P)
                            for n in range(2):
                                cols = slice(n * HALF, (n + 1) * HALF)
                                slot = (k + u) % RING
                                last = product(down[n][:, tt, :], h_hi[:, u, rows], h_lo[:, u, rows],
                                               w_hi[:, slot, cols], w_lo[:, slot, cols], False, stop and u == 3)
                        last.then_inc(unit_used, 1)

                up(k0)
                for n in range(2):
                    for tt in range(TT):
                        pe.matmul(down[n][:, tt, :], zeros[:, 0:P], zeros[:, :], start=True, stop=False)
                turn_hidden(h0)
                with pe.Fori(1, steps) as i:
                    up(k0 - 4, i)
                    down_step(k0, h0 - TT, i)
                    turn_hidden(h0, i)
                down_step(k0 + 60, h0 + TT * (steps - 1), None, True)

            pe.wait_ge(const_loaded, 16)
            pe.wait_ge(gains_loaded, 16 * len(GAIN_ROWS))
            transposed("gains", [gain_rows[:, :]])
            pe.wait_ge(set_ready, 1)
            pe.wait_ge(small_loaded, 32)
            pe.matmul(score[0:DA_H, 0, 0:3 * P - 1], table[0:BUCKETS + 1, :], onehot[0:BUCKETS + 1, :],
                      start=True, stop=True).then_inc(bias_psum, 1)

            for c in range(0, DC, 2):
                x_turn(0, c)

            def qk_turns(name, n):
                pe.wait_ge(group_act, groups[name]["act_end"])
                for half in range(2):
                    cols = [qk_sb[:, n, tt, (2 * half + j) * P:(2 * half + j + 1) * P]
                            for j in range(2) for tt in range(TT)]
                    transposed(f"{name}{'ab'[half]}", cols)

            def da_score(h):
                if h == 0:
                    pe.wait_ge(bias_rows_ready, 1)
                else:
                    pe.wait_ge(da_biased, h)
                for name in ("q0b", "k0b") if h < 4 else ("q1b", "k1b"):
                    pe.wait_ge(turn_dve, turn[name]["dve_end"])
                for m in range(2):
                    rows = slice(DA_D * m, DA_D * (m + 1))
                    pe.matmul(score[:, m, WIDE], da_q[rows, h, P:S], da_k[rows, h, :], start=True, stop=True)
                    last = pe.matmul(score[:, m, TALL], da_q[rows, h, 0:P], da_k[rows, h, 0:P], start=True, stop=True)
                last.then_inc(da_scored, 1)

            def da_probs(h):
                pe.wait_ge(da_mixed, h + 1)
                transposed(f"ap{h}", [da_p[:, h, j * P:(j + 1) * P] for j in range(3)])

            def da_value(h):
                bank = open_turn(f"av{h}")
                pe.wait_ge(turn_act, turn[f"ap{h}"]["act_end"])
                pe.wait_ge(group_act, groups[f"v{h // 4}"]["act_end"])
                cols = slice(h * P, (h + 1) * P)
                pe.matmul(bank[:, 0:P], da_pt[:, h % 2, TALL], da_v[:, 0, cols], start=True, stop=True)
                pe.matmul(bank[:, P:2 * P], da_pt[:, h % 2, 0:P], da_v[:, 0, cols], start=True, stop=False)
                pe.matmul(bank[:, P:2 * P], da_pt[:, h % 2, P:2 * P], da_v[:, 1, cols], start=False, stop=True)\
                    .then_inc(turn_filled, 1)

            def da_out_turns(half):
                pe.wait_ge(da_scaled, 2 * (half + 1))
                for c in range(0, 4, 2):
                    transposed(f"oT{half}.{c}", chunks_of(da_o, 4 * half + c, 2))

            dense("q0")
            dense("k0")
            qk_turns("q0", 0)
            dense("q1", {1: lambda: qk_turns("k0", 1)})
            dense("k1", {n: (lambda n=n: da_score(n)) for n in range(4)})
            qk_turns("q1", 0)
            dense("v0", {1: lambda: qk_turns("k1", 1)})

            def v1_slot(n):
                da_score(4 + n)
                if n:
                    da_value(n - 1)
                da_probs(n)
            dense("v1", {n: (lambda n=n: v1_slot(n)) for n in range(4)})
            for h in range(4, DA_H + 1):
                da_value(h - 1)
                if h in (6, 8):
                    da_out_turns(h // 8)
                if h < DA_H:
                    da_probs(h)
            dense("ao0")
            dense("ao1", {2: lambda: x_turn(1, 0), 3: lambda: x_turn(1, 2)})
            x_turn(1, 4)
            x_turn(1, 6)
            mlp(0, "x1")

            for c in range(0, DC, 2):
                x_turn(2, c)

            def cumulate():
                pe.wait_ge(ml_lf, 1)
                pe.matmul(score[:, 0, 0:ML_H], triu, g_lf[:, 0, :], start=True, stop=True)
                pe.matmul(score[:, 0, ML_H:2 * ML_H], ones, g_lf[:, 0, :], start=True, stop=False)
                pe.matmul(score[:, 0, ML_H:2 * ML_H], triu, g_lf[:, 1, :], start=False, stop=True).then_inc(ml_cum, 1)

            def spread(n):
                pe.wait_ge(ml_diag, n + 1)
                for j in range(2):
                    last = pe.matmul(score[:, j, :], ones, diag[:, 2 * j:2 * j + 2, :], start=True, stop=True)
                last.then_inc(ml_spread, 1)

            def conv_turn(b):
                pe.wait_ge(group_act, groups["mq" if b < 2 else "mk"]["act_end"])
                c0 = 2 * (b % 2)
                transposed(f"conv{b}", [ml_qk[:, b // 2, tt, c * P:(c + 1) * P]
                                        for c in (c0, c0 + 1) for tt in range(TT)])

            def ml_score(h):
                if h < 2:
                    pe.wait_ge(ml_wexp, ML_H)
                else:
                    pe.wait_ge(ml_weighted, h - 1)
                pe.wait_ge(ml_silu, 4)
                q, k = ml_t[:, h, :], ml_t[:, ML_H + h, :]
                pe.matmul(score[:, h % 2, WIDE], k[:, 0:P], q, start=True, stop=True)
                pe.matmul(score[:, h % 2, TALL], k[:, P:S], q[:, P:S], start=True, stop=True).then_inc(ml_scored, 1)

            def ml_value(h):
                pe.wait_ge(ml_weighted, h + 1)
                pe.wait_ge(ml_ones, 1)
                pe.wait_ge(group_act, groups["mv1"]["act_end"])
                bank = open_turn(f"mv{h}.0")
                pe.matmul(bank[:, 0:ML_V + 1], ml_s[:, h, 0:P], ml_v[:, 0, h, :], start=True, stop=True)\
                    .then_inc(turn_filled, 1)
                bank = open_turn(f"mv{h}.1")
                pe.matmul(bank[:, 0:ML_V + 1], ml_s[:, h, P:S], ml_v[:, 0, h, :], start=True, stop=False)
                pe.matmul(bank[:, 0:ML_V + 1], ml_s[:, h, TALL], ml_v[:, 1, h, :], start=False, stop=True)\
                    .then_inc(turn_filled, 1)

            dense("gate")
            dense("mq", {2: cumulate})
            dense("mk", {0: lambda: spread(0), 1: lambda: conv_turn(0), 2: lambda: conv_turn(1),
                         3: lambda: spread(1)})
            dense("mv0", {1: lambda: conv_turn(2), 3: lambda: conv_turn(3)})
            dense("mv1")
            dense("mo0", {n: (lambda n=n: ml_score(n)) for n in range(4)})
            dense("mo1", {n: (lambda n=n: ml_value(n - 1)) for n in range(1, 4)})
            ml_value(3)
            for c in range(0, DC, 2):
                pe.wait_ge(ml_y, c + 2)
                transposed(f"yT.{c}", chunks_of(ml_o, c, 2))
            dense("mw0")
            dense("mw1", {2: lambda: x_turn(3, 0), 3: lambda: x_turn(3, 2)})
            x_turn(3, 4)
            x_turn(3, 6)
            mlp(1, "x3")

            for c in range(0, DC, 2):
                x_turn(5, c)

            def lat_turn(c, n):
                pe.wait_ge(group_act, groups["ckv"]["act_end"])
                transposed(f"lat.{c}", chunks_of(lat_sb, c, n))

            def ret_turn(name, half):
                pe.wait_ge(ret_roped, ("rq0", "rq1", "rk0", "rk1").index(name) + 1)
                transposed(f"{name}{'ab'[half]}", [work[:, 1, tt, (2 * half + j) * P:(2 * half + j + 1) * P]
                                                   for j in range(2) for tt in range(TT)])

            def ret_score(h):
                if h >= 2:
                    pe.wait_ge(ret_decayed, h - 1)
                pe.wait_ge(turn_dve, turn["rk1b"]["dve_end"])
                for j in range(2):
                    c = 2 * h + j
                    pe.matmul(score[:, h % 2, WIDE], rk_t[:, c, 0:P], rq_t[:, c, :], start=j == 0, stop=j == 1)
                for j in range(2):
                    c = 2 * h + j
                    last = pe.matmul(score[:, h % 2, TALL], rk_t[:, c, P:S], rq_t[:, c, P:S],
                                     start=j == 0, stop=j == 1)
                last.then_inc(ret_scored, 1)

            def ret_value(h):
                ps = open_pair(f"ret{h}")
                pe.wait_ge(ret_decayed, h + 1)
                pe.wait_ge(group_act, groups[f"rv{h}"]["act_end"])
                v = work[:, h % 2, :, :]
                pe.matmul(ps[:, 0, :], ret_s[:, h, 0:P], v[:, 0, :], start=True, stop=True)
                pe.matmul(ps[:, 1, :], ret_s[:, h, P:S], v[:, 0, :], start=True, stop=False)
                pe.matmul(ps[:, 1, :], ret_s[:, h, TALL], v[:, 1, :], start=False, stop=True).then_inc(ret_out, 1)

            def mla_turn(which, part, b):
                tile, ready = (lq_sb, lq_ready) if which == "mq" else (kv, lk_ready)
                pe.wait_ge(ready, 1 if (which, part) == ("mk", "n") else 2)
                if part == "n":
                    src = [tile[:, tt, 2 * b + j, 0:NOPE] for j in range(2) for tt in range(TT)]
                else:
                    src = [rot[:, tt, 4 * b + 2 * j:4 * b + 2 * j + 2, :] for j in range(2) for tt in range(TT)]
                transposed(f"{which}{part}{b}", src)

            def mla_score(h):
                if h >= 2:
                    pe.wait_ge(l_masked, h - 1)
                else:
                    pe.wait_ge(ret_decayed, RET_H)
                pe.wait_ge(turn_act, turn["mkn3"]["act_end"])
                pe.wait_ge(turn_dve, turn["mkr1"]["dve_end"])
                rows = slice(ROPE * (h % 2), ROPE * (h % 2 + 1))
                for cols, q, k in ((WIDE, slice(P, S), slice(0, S)), (TALL, slice(0, P), slice(0, P))):
                    o = score[:, h % 2, cols]
                    pe.matmul(o, lq_n[:, h, q], lk_n[:, h, k], start=True, stop=False)
                    last = pe.matmul(o, lq_t[rows, h // 2, q], lk_t[rows, h // 2, k], start=False, stop=True)
                last.then_inc(l_scored, 1)

            def mla_probs(h):
                pe.wait_ge(l_exped, h + 1)
                transposed(f"lp{h}", [l_e[:, h % 2, j * P:(j + 1) * P] for j in range(3)])

            def mla_value(h):
                bank = open_turn(f"lv{h}")
                pe.wait_ge(turn_act, turn[f"lp{h}"]["act_end"])
                v = [kv[:, tt, h, NOPE:] for tt in range(TT)]
                pe.matmul(bank[:, 0:P], l_pt[:, h % 2, TALL], v[0], start=True, stop=True)
                pe.matmul(bank[:, P:S], l_pt[:, h % 2, 0:P], v[0], start=True, stop=False)
                pe.matmul(bank[:, P:S], l_pt[:, h % 2, P:S], v[1], start=False, stop=True).then_inc(turn_filled, 1)

            def mla_slot(n):
                if n < MLA_H:
                    mla_score(n)
                if n >= 2:
                    mla_value(n - 2)
                if 1 <= n <= MLA_H:
                    mla_probs(n - 1)

            dense("cq")
            dense("ckv")
            dense("rq0", {1: lambda: lat_turn(0, 2), 2: lambda: lat_turn(2, 2), 3: lambda: lat_turn(4, 1)})
            dense("rq1", {2: lambda: ret_turn("rq0", 0), 3: lambda: ret_turn("rq0", 1)})
            dense("rk0", {2: lambda: ret_turn("rq1", 0), 3: lambda: ret_turn("rq1", 1)})
            dense("rk1", {2: lambda: ret_turn("rk0", 0), 3: lambda: ret_turn("rk0", 1)})
            dense("uq0")
            dense("uq1", {1: lambda: ret_turn("rk1", 0)})
            dense("uq2", {1: lambda: ret_turn("rk1", 1)})
            for n in range(4):
                dense(f"ukv{n}")
                ret_score(n)
            dense("rv0")
            dense("rv1")
            ret_value(0)

            def turns_q(n):
                mla_turn("mq", "n", n)

            def turns_k(n):
                if n == 0:
                    mla_turn("mq", "r", 0)
                    mla_turn("mq", "r", 1)
                mla_turn("mk", "n", n)
            dense("rv2", {n: (lambda n=n: turns_q(n)) for n in range(4)})
            ret_value(1)
            dense("rv3", {n: (lambda n=n: turns_k(n)) for n in range(4)})
            ret_value(2)
            dense("rg0", {0: lambda: mla_turn("mk", "r", 0), 1: lambda: mla_turn("mk", "r", 1)})
            ret_value(3)
            dense("rg1", {n: (lambda n=n: mla_slot(n)) for n in range(4)})
            dense("rg2", {n: (lambda n=n: mla_slot(4 + n)) for n in range(4)})
            dense("rg3", {0: lambda: mla_slot(8), 1: lambda: mla_slot(9)})

            def ro_turn(c):
                pe.wait_ge(gated, c // 4 + 1)
                transposed(f"roT.{c}", chunks_of(ret, c, 2))
            dense("gm0", {n: (lambda n=n: ro_turn(2 * n)) for n in range(4)})
            dense("gm1", {n: (lambda n=n: ro_turn(8 + 2 * n)) for n in range(4)})
            dense("gr0")
            dense("gr1")

            def mo_turn(c):
                pe.wait_ge(turn_act, turn["lv7"]["act_end"])
                transposed(f"moT.{c}", chunks_of(lo_sb, c, 2))
            dense("br0", {2 * n + 1: (lambda n=n: mo_turn(2 * n)) for n in range(4)})
            dense("br1")
            dense("bm0")

            def mix_turn(c):
                pe.wait_ge(mixed, 2 * (c // 4) + 2)
                transposed(f"mixT.{c}", chunks_of(mix, c, 2))
            dense("bm1", {2: lambda: mix_turn(0), 3: lambda: mix_turn(2)})
            mix_turn(4)
            mix_turn(6)
            dense("wo0")
            dense("wo1", {2: lambda: x_turn(6, 0), 3: lambda: x_turn(6, 2)})
            x_turn(6, 4)
            x_turn(6, 6)
            mlp(2, "x6")

            pe.wait_ge(p_loaded, 16 * TT)
            transposed("pT.0", chunks_of(p_sb, 0, 2))
            for n in range(2):
                pe.wait_ge(x_ready, x_version(7, 2))
                dense(f"pl{n}")
            for c in range(0, DC, 2):
                x_turn(7, c)
            for n in range(2):
                dense(f"pg{n}")

        @block.scalar
        def _(act):
            mark, own = own_order(act, act_step)
            sizes = {item[1]: item[3] * item[4] for item in stream if item[0] == "unit"}
            split_to = [0]
            junk_free = [None]

            def square_sum(src, total, cols, done, value):
                if junk_free[0]:
                    act.wait_ge(*junk_free[0])
                junk_free[0] = (done, value)
                act.activation(junk[:, cols], src, ACT.Square, accum_out=total).then_inc(done, 1)

            def split_unit(k, it=None):
                if it is not None or k >= RING:
                    used = k - RING + 1
                    act.wait_ge(unit_used, used if it is None else it * RING + used)
                land = 16 * (k // RAW + 1)
                act.wait_ge(landed[k % RAW], land if it is None else it * (16 * RING // RAW) + land)
                n = sizes.get(k, UNIT) if it is None else UNIT
                act.activation(w_hi[:, k % RING, 0:n], raw[:, k % RAW, 0:n], ACT.Copy).then_inc(hi_ready, 1)

            def split_until(k):
                while split_to[0] <= min(k, total_units - 1):
                    split_unit(split_to[0])
                    split_to[0] += 1

            def split_turn(name):
                wait_turn(act, name)
                for src, hi, _, scale in split_parts(name):
                    if scale is None:
                        act.activation(hi, src, ACT.Copy).then_inc(turn_act, 1)
                    else:
                        act.activation(hi, src, ACT.Copy, scale=scale).then_inc(turn_act, 1)

            def x_squares(v):
                if v == 0:
                    act.wait_ge(x_loaded, 16 * TT)
                else:
                    act.wait_ge(x_ready, x_version(v))
                for tt in range(TT):
                    square_sum(x[:, tt, :], ssx[:, v, tt:tt + 1], slice(0, D), x_squared, TT * v + tt + 1)

            def dense(name, slots=None):
                run_group(name, lambda u: split_until(u[0] + AHEAD), slots)

            def empty(name, outs, func=ACT.Copy, scales=None):
                wait_group(act, name)
                for tt in range(TT):
                    ps = group_ps(name)[:, tt, 0:groups[name]["ncols"]]
                    ps = ps if len(outs[tt].shape) == 2 else ps.rearrange("p (a b) -> p a b", a=outs[tt].shape[1])
                    if scales is None:
                        act.activation(outs[tt], ps, func).then_inc(group_act, 1)
                    else:
                        act.activation(outs[tt], ps, func, scale=scales[tt]).then_inc(group_act, 1)

            def row_norm(v):
                return [rstd[:, v, tt:tt + 1] for tt in range(TT)]

            def mlp(m, v):
                k0, steps = mlps[m], FF // HALF
                h0 = m * steps * TT

                def at(value, it, per):
                    return value if it is None else it * per + value

                def step(k, h, it=None):
                    act.wait_ge(unit_used, at(k + 4, it, RING))
                    for tt in range(TT):
                        act.activation(relu[:, tt, :], pair[0][:, tt, :], ACT.Relu).then_inc(up_relu, 1)
                    for u in range(4):
                        split_unit(k + 8 + u, it)
                    for tt in range(TT):
                        act.wait_ge(hid_turned, at(h + tt + 1, it, TT))
                        act.activation(h_hi[:, :, tt * P:(tt + 1) * P],
                                       turn_ps[:, tt, :].rearrange("p (c s) -> p c s", s=P), ACT.Copy)\
                            .then_inc(hid_hi, 1)

                def step_tail(k, it=None):
                    for u in range(4):
                        split_unit(k + 12 + u, it)

                split_until(k0 + 7)
                step(k0, h0)
                with act.Fori(1, steps - 1) as i:
                    step(k0 - 4, h0, i)
                    step_tail(k0 - 4, i)
                step(k0 + 4 + RING * (steps - 2), h0 + TT * (steps - 1))
                split_to[0] = k0 + 8 * steps

            act.dma_start(square[:, :, :], w["c_square"]).then_inc(const_loaded, 16)
            at = 0
            for name, rows in GAIN_ROWS:
                src = w[name].rearrange("a b -> (a b)") if len(w[name].shape) == 2 else \
                    w[name].rearrange("a b c -> (a b c)")
                src = src[0:rows * P].rearrange("(r p) -> r p", p=P)
                act.dma_start(gain_rows[at:at + rows, :], src).then_inc(gains_loaded, 16)
                at += rows
            act.wait_ge(lam_sum, 1)
            act.activation(lam_e[:, :], lam_s[:, :], ACT.Exp).then_inc(lam_exp, 1)
            wait_turn(act, "gains")
            act.activation(gains[:, :], turn_bank("gains")[:, 0:P], ACT.Copy).then_inc(turn_act, 1)
            act.wait_ge(turn_act, 1)
            for c in range(0, DC, 2):
                split_turn(f"x0.{c}")
                split_until(c // 2)
            x_squares(0)
            split_until(4)
            act.wait_ge(angles_ready, 1)
            act.activation(trig[:, :, :, :], ang[:, :, :, :], ACT.Sin).then_inc(trig_ready, 1)

            def da_exp(h):
                act.wait_ge(da_maxed, h + 1)
                b = h % 2
                for j, cols in enumerate((WIDE, TALL)):
                    for m in range(2):
                        i = 2 * j + m
                        last = act.activation(da_e[:, b, m, cols], da_e[:, b, m, cols], ACT.Exp,
                                              bias=da_nm[:, b, i:i + 1], accum_out=da_sum[:, b, i:i + 1])
                last.then_inc(da_exped, 1)

            def da_probs(h):
                wait_turn(act, f"ap{h}")
                act.activation(da_pt[:, h % 2, :], turn_bank(f"ap{h}")[:, 0:SCORE], ACT.Copy).then_inc(turn_act, 1)

            def da_value(h):
                wait_turn(act, f"av{h}")
                for tt in range(TT):
                    square_sum(turn_bank(f"av{h}")[:, tt * P:(tt + 1) * P], da_ss[:, h // 4, tt, h % 4:h % 4 + 1],
                               slice(0, P), turn_act, turn[f"av{h}"]["act"] + tt + 1)

            empty_qk = lambda name, n: empty(name, [qk_sb[:, n, tt, :] for tt in range(TT)], scales=row_norm(0))
            act.wait_ge(rstd_ready, 1)
            dense("q0")
            empty_qk("q0", 0)
            dense("k0")
            empty_qk("k0", 1)
            dense("q1")
            wait_turn(act, "q0b")
            empty_qk("q1", 0)
            dense("k1", {n: (lambda n=n: da_exp(n - 1)) for n in range(1, 4)})
            wait_turn(act, "k0b")
            empty_qk("k1", 1)
            dense("v0", {0: lambda: da_exp(3)})
            empty("v0", [da_v[:, tt, 0:HALF] for tt in range(TT)], scales=row_norm(0))

            def v1_slot(n):
                if n:
                    da_exp(3 + n)
                    da_value(n - 1)
                da_probs(n)
            dense("v1", {n: (lambda n=n: v1_slot(n)) for n in range(4)})
            empty("v1", [da_v[:, tt, HALF:D] for tt in range(TT)], scales=row_norm(0))
            da_exp(7)
            first = groups["ao0"]["units"][0][0]
            for h in range(4, DA_H + 1):
                da_value(h - 1)
                if h in (6, 8):
                    for c in (0, 2):
                        split_turn(f"oT{h // 8}.{c}")
                if h < DA_H:
                    da_probs(h)
                    split_until(first + h - 4)
            dense("ao0")
            dense("ao1", {2: lambda: split_turn("x1.0"), 3: lambda: split_turn("x1.2")})
            split_turn("x1.4")
            split_turn("x1.6")
            x_squares(1)
            mlp(0, 1)

            first = groups["gate"]["units"][0][0]
            split_until(first + 2)
            for c in range(0, DC, 2):
                split_turn(f"x2.{c}")
            x_squares(2)
            dense("gate")
            act.wait_ge(rstd_ready, 3)
            empty("gate", [gate_in[:, tt, :] for tt in range(TT)], scales=row_norm(2))

            def gate_log():
                act.wait_ge(ml_abs, 1)
                mark(act.activation(g_exp, g_abs, ACT.Exp, scale=-1.0))
                own()
                act.activation(g_ln, g_exp, ACT.Ln, bias=1.0).then_inc(ml_ln, 1)

            def weights():
                act.wait_ge(ml_args, 2)
                for h in range(ML_H):
                    g0, g1 = g_g[:, 0, h:h + 1], g_g[:, 1, h:h + 1]
                    spread = score[:, h // 2, :].rearrange("p (h s) -> p h s", h=2)[:, h % 2, :]
                    act.activation(ml_w[:, h, 0:P], ml_w[:, h, 0:P], ACT.Exp, bias=g0)
                    act.activation(ml_w[:, h, P:S], spread[:, P:S], ACT.Exp, bias=g0, scale=-1.0)
                    act.activation(ml_w[:, h, TALL], ml_w[:, h, TALL], ACT.Exp, bias=g1).then_inc(ml_wexp, 1)
                act.activation(g_em, g_nm, ACT.Exp, scale=-1.0).then_inc(ml_em, 1)

            def silu(b):
                act.wait_ge(turn_dve, turn[f"conv{b}"]["dve_end"])
                if b >= 2:
                    act.wait_ge(ml_silu, b - 1)
                act.activation(ml_sig[:, b % 2, :, :], ml_t[:, 2 * b:2 * b + 2, :], ACT.Sigmoid).then_inc(ml_sigm, 1)

            def ml_square(h):
                for tt in range(TT):
                    name = f"mv{h}.{tt}"
                    wait_turn(act, name)
                    square_sum(turn_bank(name)[:, 0:ML_V], r_ss[:, tt, h:h + 1], slice(0, ML_V), turn_act,
                               turn[name]["act_end"])

            dense("mq", {0: gate_log})
            empty("mq", [ml_qk[:, 0, tt, :] for tt in range(TT)], scales=row_norm(2))
            dense("mk")
            empty("mk", [ml_qk[:, 1, tt, :] for tt in range(TT)], scales=row_norm(2))
            dense("mv0", {0: weights, 2: lambda: silu(0), 3: lambda: silu(1)})
            act.wait_ge(ml_ones, 1)
            half_v = lambda n: [ml_v[:, tt, 2 * n:2 * n + 2, 0:ML_V] for tt in range(TT)]
            empty("mv0", half_v(0), scales=row_norm(2))
            dense("mv1", {0: lambda: silu(2), 1: lambda: silu(3)})
            empty("mv1", half_v(1), scales=row_norm(2))
            dense("mo0")
            empty("mo0", [ml_o[:, tt, 0:HALF] for tt in range(TT)], ACT.Sigmoid, row_norm(2))
            dense("mo1", {n: (lambda n=n: ml_square(n - 1)) for n in range(1, 4)})
            empty("mo1", [ml_o[:, tt, HALF:D] for tt in range(TT)], ACT.Sigmoid, row_norm(2))
            ml_square(3)
            first = groups["mw0"]["units"][0][0]
            for c in range(0, DC, 2):
                split_turn(f"yT.{c}")
                split_until(first + c // 2)
            dense("mw0")
            dense("mw1", {2: lambda: split_turn("x3.0"), 3: lambda: split_turn("x3.2")})
            split_turn("x3.4")
            split_turn("x3.6")
            x_squares(3)
            mlp(1, 3)

            first = groups["cq"]["units"][0][0]
            split_until(first + 3)
            x_squares(4)
            for c in range(0, DC, 2):
                split_turn(f"x5.{c}")
            x_squares(5)
            dense("cq")
            act.wait_ge(rstd_ready, 6)
            empty("cq", [lat_sb[:, tt, 0:Q_LORA] for tt in range(TT)], scales=row_norm(5))
            dense("ckv")
            empty("ckv", [lat_sb[:, tt, Q_LORA:] for tt in range(TT)], scales=row_norm(5))

            def lat_squares():
                act.wait_ge(group_act, groups["ckv"]["act_end"])
                for tt in range(TT):
                    for n, cols in enumerate((slice(0, Q_LORA), slice(Q_LORA, LAT))):
                        square_sum(lat_sb[:, tt, cols], lat_ss[:, n, tt:tt + 1], cols, lat_sq, 2 * tt + n + 1)

            def empty_rope(name):
                n = ("rq0", "rq1", "rk0", "rk1").index(name)
                if n:
                    act.wait_ge(ret_roped, n)
                empty(name, [work[:, 0, tt, :] for tt in range(TT)], scales=row_norm(5))

            def mla_copy(which, b):
                name = f"{which}n{b}"
                wait_turn(act, name)
                dst = (lq_n if which == "mq" else lk_n)[:, 2 * b:2 * b + 2, :]
                act.activation(dst, turn_bank(name).rearrange("p (h s) -> p h s", h=2), ACT.Copy,
                               scale=gain("q_norm_2" if which == "mq" else "k_norm_2", 0)).then_inc(turn_act, 1)

            def ret_squares(h):
                act.wait_ge(ret_out, h + 1)
                ps = group_ps(f"ret{h}")
                for tt in range(TT):
                    square_sum(ps[:, tt, :], ret_ss[:, tt, h:h + 1], slice(0, HALF), group_act,
                               groups[f"ret{h}"]["act_end"] - 1 + tt)

            def mla_exp(h):
                act.wait_ge(l_maxed, h + 1)
                b = h % 2
                for j, cols in enumerate((WIDE, TALL)):
                    last = act.activation(l_e[:, b, cols], l_e[:, b, cols], ACT.Exp, bias=l_nm[:, b, j:j + 1],
                                          accum_out=l_sum[:, b, j:j + 1])
                last.then_inc(l_exped, 1)

            def mla_probs(h):
                wait_turn(act, f"lp{h}")
                act.activation(l_pt[:, h % 2, :], turn_bank(f"lp{h}")[:, 0:SCORE], ACT.Copy).then_inc(turn_act, 1)

            def mla_value(h):
                wait_turn(act, f"lv{h}")
                act.wait_ge(l_reced, h + 1)
                for tt in range(TT):
                    act.activation(lo_sb[:, tt, h * P:(h + 1) * P], turn_bank(f"lv{h}")[:, tt * P:(tt + 1) * P],
                                   ACT.Copy, scale=l_rec[:, h % 2, 1 - tt:2 - tt]).then_inc(turn_act, 1)

            def mla_slot(n):
                if 1 <= n <= MLA_H:
                    mla_exp(n - 1)
                if n >= 2:
                    mla_value(n - 2)
                if 1 <= n <= MLA_H:
                    mla_probs(n - 1)

            dense("rq0", {0: lat_squares, 1: lambda: split_turn("lat.0"), 2: lambda: split_turn("lat.2"),
                          3: lambda: split_turn("lat.4")})
            empty_rope("rq0")
            dense("rq1")
            empty_rope("rq1")
            dense("rk0")
            empty_rope("rk0")
            dense("rk1")
            empty_rope("rk1")
            act.wait_ge(lat_norm, 1)
            for n in range(3):
                dense(f"uq{n}")
                empty(f"uq{n}", [flat_q[:, tt * MLA_H * MLA_QK + n * HALF:tt * MLA_H * MLA_QK + (n + 1) * HALF]
                                 for tt in range(TT)], scales=[lat_r[:, 0, tt:tt + 1] for tt in range(TT)])
            for n in range(4):
                dense(f"ukv{n}")
                empty(f"ukv{n}", [kv[:, tt, 2 * n:2 * n + 2, :] for tt in range(TT)],
                      scales=[lat_r[:, 1, tt:tt + 1] for tt in range(TT)])

            def empty_value(n):
                if n == 0:
                    wait_turn(act, "rk1b")
                elif n >= 2:
                    act.wait_ge(ret_out, n - 1)
                else:
                    wait_turn(act, "rk1b")
                empty(f"rv{n}", [work[:, n % 2, tt, :] for tt in range(TT)], scales=row_norm(5))

            def empty_gate(n):
                act.wait_ge(ret_out, 3 if n == 0 else 4)
                if n >= 2:
                    act.wait_ge(gated, n - 1)
                empty(f"rg{n}", [work[:, n % 2, tt, :] for tt in range(TT)], ACT.Sigmoid, row_norm(5))

            dense("rv0")
            empty_value(0)
            dense("rv1")
            empty_value(1)
            ret_squares(0)

            dense("rv2", {n: (lambda n=n: mla_copy("mq", n)) for n in range(4)})
            empty_value(2)
            ret_squares(1)
            dense("rv3", {n: (lambda n=n: mla_copy("mk", n)) for n in range(4)})
            empty_value(3)
            ret_squares(2)
            dense("rg0")
            empty_gate(0)
            ret_squares(3)
            dense("rg1", {n: (lambda n=n: mla_slot(n)) for n in range(4)})
            empty_gate(1)
            dense("rg2", {n: (lambda n=n: mla_slot(4 + n)) for n in range(4)})
            empty_gate(2)
            dense("rg3", {0: lambda: mla_slot(8), 1: lambda: mla_slot(9)})
            empty_gate(3)
            dense("gm0", {n: (lambda n=n: split_turn(f"roT.{2 * n}")) for n in range(4)})
            empty("gm0", [gm[:, tt, 0:HALF] for tt in range(TT)], ACT.Sigmoid, row_norm(5))
            dense("gm1", {n: (lambda n=n: split_turn(f"roT.{8 + 2 * n}")) for n in range(4)})
            empty("gm1", [gm[:, tt, HALF:D] for tt in range(TT)], ACT.Sigmoid, row_norm(5))
            dense("gr0")
            empty("gr0", [gr[:, tt, 0:HALF] for tt in range(TT)], ACT.Sigmoid, row_norm(5))
            dense("gr1")
            empty("gr1", [gr[:, tt, HALF:D] for tt in range(TT)], ACT.Sigmoid, row_norm(5))
            dense("br0", {2 * n + 1: (lambda n=n: split_turn(f"moT.{2 * n}")) for n in range(4)})
            dense("br1")
            dense("bm0")
            dense("bm1", {2: lambda: split_turn("mixT.0"), 3: lambda: split_turn("mixT.2")})
            split_turn("mixT.4")
            split_turn("mixT.6")
            dense("wo0")
            dense("wo1", {2: lambda: split_turn("x6.0"), 3: lambda: split_turn("x6.2")})
            split_turn("x6.4")
            split_turn("x6.6")
            x_squares(6)
            mlp(2, 6)

            split_until(groups["pl0"]["units"][0][0] + 3)
            split_turn("pT.0")
            for n in range(2):
                cols = slice(n * HALF, (n + 1) * HALF)
                dense(f"pl{n}")
                empty(f"pl{n}", [ple[:, tt, cols] for tt in range(TT)])
            for c in range(0, DC, 2):
                split_turn(f"x7.{c}")
            x_squares(7)
            act.wait_ge(rstd_ready, 8)
            for n in range(2):
                cols = slice(n * HALF, (n + 1) * HALF)
                dense(f"pg{n}")
                empty(f"pg{n}", [gate[:, tt, cols] for tt in range(TT)], ACT.Sigmoid, row_norm(7))

        @block.vector
        def _(dve):
            mark, own = own_order(dve, dve_step)
            sizes = {item[1]: item[3] * item[4] for item in stream if item[0] == "unit"}
            split_to = [0]

            def split_unit(k, it=None):
                dve.wait_ge(hi_ready, k + 1 if it is None else it * RING + (k + 1))
                n = sizes.get(k, UNIT) if it is None else UNIT
                dve.tensor_tensor(w_lo[:, k % RING, 0:n], raw[:, k % RAW, 0:n], w_hi[:, k % RING, 0:n],
                                  ALU.subtract).then_inc(lo_ready, 1)

            def split_until(k):
                while split_to[0] <= min(k, total_units - 1):
                    split_unit(split_to[0])
                    split_to[0] += 1

            def dense(name, slots=None):
                run_group(name, lambda u: split_until(u[0] + AHEAD), slots)

            def split_turn(name):
                dve.wait_ge(turn_act, turn[name]["act_end"])
                for src, hi, lo, scale in split_parts(name):
                    if scale is None:
                        dve.tensor_tensor(lo, src, hi, ALU.subtract).then_inc(turn_dve, 1)
                    else:
                        dve.scalar_tensor_tensor(lo, src, scale, hi.bitcast(F32), ALU.mult, ALU.subtract)\
                            .then_inc(turn_dve, 1)

            def copy_turn(name, dst, src):
                if turn[name]["act_end"] > turn[name]["act"]:
                    dve.wait_ge(turn_act, turn[name]["act_end"])
                else:
                    wait_turn(dve, name)
                dve.tensor_copy(dst, src).then_inc(turn_dve, 1)

            def invert(v):
                dve.wait_ge(rstd_ready, v + 1)
                dve.reciprocal(inv_ms[:, v, :], msx[:, v, :]).then_inc(inv_ready, 1)

            def mlp(m, v):
                k0, steps = mlps[m], FF // HALF
                h0 = m * steps * TT

                def at(value, it, per):
                    return value if it is None else it * per + value

                def step(k, h, it=None):
                    for tt in range(TT):
                        dve.wait_ge(up_relu, at(h + tt + 1, it, TT))
                        dve.scalar_tensor_tensor(hid[:, tt, :], pair[0][:, tt, :], 0.0, relu[:, tt, :],
                                                 ALU.max, ALU.mult).then_inc(hid_ready, 1)
                    for u in range(4):
                        split_unit(k + 8 + u, it)
                    for tt in range(TT):
                        dve.wait_ge(hid_hi, at(h + tt + 1, it, TT))
                        rows = slice(tt * P, (tt + 1) * P)
                        dve.tensor_tensor(h_lo[:, :, rows], turn_ps[:, tt, :].rearrange("p (c s) -> p c s", s=P),
                                          h_hi[:, :, rows], ALU.subtract).then_inc(hid_lo, 1)

                def step_tail(k, it=None):
                    for u in range(4):
                        split_unit(k + 12 + u, it)

                split_until(k0 + 7)
                invert(v)
                step(k0, h0)
                with dve.Fori(1, steps - 1) as i:
                    step(k0 - 4, h0, i)
                    step_tail(k0 - 4, i)
                step(k0 + 4 + RING * (steps - 2), h0 + TT * (steps - 1))
                split_to[0] = k0 + 8 * steps
                split_until(k0 + 8 * steps + 2)
                dve.wait_ge(unit_used, k0 + 8 * steps)
                dve.wait_ge(inv_ready, m + 1)
                for n in range(2):
                    cols = slice(n * HALF, (n + 1) * HALF)
                    for tt in range(TT):
                        dve.scalar_tensor_tensor(x[:, tt, cols], down[n][:, tt, :], inv_ms[:, v, tt:tt + 1],
                                                 x[:, tt, cols], ALU.mult, ALU.add).then_inc(x_ready, 1)

            def add_to_x(name, n):
                wait_group(dve, name)
                cols = slice(n * HALF, (n + 1) * HALF)
                for tt in range(TT):
                    dve.tensor_tensor(x[:, tt, cols], x[:, tt, cols], group_ps(name)[:, tt, :], ALU.add)\
                        .then_inc(x_ready, 1)

            def rotate(o1, o2, t1, t2, x1, x2, cos, sin):
                mark(dve.tensor_tensor(o1, x1, cos, ALU.mult))
                n = mark(dve.tensor_tensor(t1, x2, sin, ALU.mult))
                mark(dve.tensor_tensor(o2, x2, cos, ALU.mult))
                mark(dve.tensor_tensor(t2, x1, sin, ALU.mult))
                own(n)
                mark(dve.tensor_tensor(o1, o1, t1, ALU.subtract))
                own()
                return dve.tensor_tensor(o2, o2, t2, ALU.add)

            def spread_to(ap, axis, shape):
                return ap.unsqueeze(axis).to_broadcast([P, *shape])

            dve.wait_ge(lam_loaded, 64)
            mark(dve.tensor_tensor(lam_prod[:, :, :], lam_in[:, 0::2, :], lam_in[:, 1::2, :], ALU.mult))
            own()
            dve.tensor_reduce(lam_s[:, :], lam_prod[:, :, :], AXIS, ALU.add).then_inc(lam_sum, 1)
            dve.wait_ge(bias_psum, 1)
            dve.tensor_copy(bias_rows[0:DA_H, :], score[0:DA_H, 0, 0:3 * P - 1]).then_inc(bias_rows_ready, 1)
            dve.wait_ge(lam_exp, 1)
            mark(dve.scalar_tensor_tensor(neg_lam[:, :], lam_e[:, 1:2], LAMBDA_INIT, lam_e[:, 0:1],
                                          ALU.subtract, ALU.subtract))
            for c in range(0, DC, 2):
                split_turn(f"x0.{c}")
                split_until(c // 2)
            dve.wait_ge(pos_loaded, 32)
            mark(dve.tensor_copy(pos_f[:, :], pos_i[:, :]))
            own()
            for a in range(2):
                for tt in range(TT):
                    mark(dve.tensor_scalar(ang[:, a, tt, :], inv[:, :], pos_f[:, tt:tt + 1], None, ALU.mult))
            own()
            for a in range(2):
                mark(dve.tensor_scalar(turns_k[:, a, :, :], ang[:, a, :, :], 1 / TWO_PI, 0.25 * a, ALU.mult, ALU.add))
            for step in (ROUND, -ROUND):
                own()
                mark(dve.tensor_scalar(turns_k[:, :, :, :], turns_k[:, :, :, :], step, None, ALU.add))
            split_until(4)
            k_flat = turns_k[:, :, :, :].rearrange("p a t n -> p (a t n)")
            a_flat = ang[:, :, :, :].rearrange("p a t n -> p (a t n)")
            for part in (PI_A, PI_B, PI_C):
                own()
                mark(dve.scalar_tensor_tensor(a_flat, k_flat, -part, a_flat, ALU.mult, ALU.add))
            own()
            mark(dve.tensor_scalar(ang[:, 1, :, :], ang[:, 1, :, :], TWO_PI / 4, None, ALU.add))
            own()
            dve.tensor_scalar(a_flat, a_flat, PI_SAFE, -PI_SAFE, ALU.min, ALU.max).then_inc(angles_ready, 1)

            def da_logits(h):
                dve.wait_ge(da_scored, h + 1)
                b = h % 2
                if h >= 2:
                    dve.wait_ge(da_mixed, h - 1)
                dve.scalar_tensor_tensor(da_e[:, b, :, :], score[:, :, 0:SCORE], DA_D ** -0.5,
                                         spread_to(bias[:, h, :], 1, [2, SCORE]), ALU.mult, ALU.add)\
                    .then_inc(da_biased, 1)
                dve.wait_ge(da_biased, h + 1)
                for j, cols in enumerate((WIDE, TALL)):
                    last = dve.tensor_reduce(da_nm[:, b, 2 * j:2 * j + 2], da_e[:, b, :, cols], AXIS, ALU.max,
                                             negate=True)
                last.then_inc(da_maxed, 1)

            def da_mix(h):
                dve.wait_ge(da_exped, h + 1)
                b = h % 2
                mark(dve.reciprocal(da_rec[:, b, :], da_sum[:, b, :]))
                own()
                mark(dve.tensor_scalar(da_nl[:, b, :], da_rec[:, b, 1::2], neg_lam[:, 0:1], None, ALU.mult))
                own()
                for j, cols in enumerate((WIDE, TALL)):
                    mark(dve.tensor_scalar(da_e[:, b, 1, cols], da_e[:, b, 1, cols], da_nl[:, b, j:j + 1], None,
                                           ALU.mult))
                own()
                for j, cols in enumerate((WIDE, TALL)):
                    last = dve.scalar_tensor_tensor(da_p[:, h, cols], da_e[:, b, 0, cols],
                                                    da_rec[:, b, 2 * j:2 * j + 1], da_e[:, b, 1, cols],
                                                    ALU.mult, ALU.add)
                last.then_inc(da_mixed, 1)

            def da_value(h):
                copy_turn(f"av{h}", da_o[:, :, h * P:(h + 1) * P],
                          turn_bank(f"av{h}")[:, 0:2 * P].rearrange("p (t d) -> p t d", t=TT))

            def da_scale(half):
                dve.wait_ge(da_norm, half + 1)
                dve.wait_ge(turn_dve, turn[f"av{4 * half + 3}"]["dve_end"])
                for tt in range(TT):
                    o = da_o[:, tt, half * HALF:(half + 1) * HALF].rearrange("p (h d) -> p h d", d=P)
                    dve.tensor_tensor(o, o, spread_to(da_r[:, half, tt, :], 2, [4, P]), ALU.mult)\
                        .then_inc(da_scaled, 1)

            def copy_heads(name, dst, h0):
                for half in range(2):
                    turn_name = f"{name}{'ab'[half]}"
                    copy_turn(turn_name, dst[:, h0 + 2 * half:h0 + 2 * half + 2, :],
                              turn_bank(turn_name).rearrange("p (h s) -> p h s", h=2))

            dense("q0")
            dense("k0")
            copy_heads("q0", da_q, 0)
            dense("q1", {1: lambda: copy_heads("k0", da_k, 0)})
            dve.wait_ge(bias_loaded, 32)

            def k1_slot(n):
                da_logits(n)
                if n:
                    da_mix(n - 1)
            dense("k1", {n: (lambda n=n: k1_slot(n)) for n in range(4)})
            copy_heads("q1", da_q, 4)
            dense("v0", {0: lambda: da_mix(3), 1: lambda: copy_heads("k1", da_k, 4)})

            def v1_slot(n):
                da_logits(4 + n)
                if n:
                    da_value(n - 1)
                    da_mix(3 + n)
            dense("v1", {n: (lambda n=n: v1_slot(n)) for n in range(4)})
            da_value(3)
            da_mix(7)
            first = groups["ao0"]["units"][0][0]
            for h in range(4, DA_H + 1):
                if h > 4:
                    da_value(h - 1)
                if h in (4, 8):
                    da_scale(h // 8)
                if h in (6, 8):
                    for c in (0, 2):
                        split_turn(f"oT{h // 8}.{c}")
                if h < DA_H:
                    split_until(first + h - 4)
            dense("ao0")
            add_to_x("ao0", 0)
            dense("ao1", {2: lambda: split_turn("x1.0"), 3: lambda: split_turn("x1.2")})
            add_to_x("ao1", 1)
            split_turn("x1.4")
            split_turn("x1.6")
            mlp(0, 1)

            def ml_gates():
                dve.wait_ge(group_act, groups["gate"]["act_end"])
                dve.wait_ge(ml_loaded, 32)
                mark(dve.tensor_tensor(g_i, gate_in[:, :, 0:ML_H], spread_to(gate_b[:, 0:ML_H], 1, [TT, ML_H]), ALU.add))
                mark(dve.tensor_tensor(g_fz, gate_in[:, :, ML_H:], spread_to(gate_b[:, ML_H:], 1, [TT, ML_H]), ALU.add))
                own()
                mark(dve.tensor_scalar(g_nfz, g_fz, -1.0, None, ALU.mult))
                own()
                dve.tensor_tensor(g_abs, g_fz, g_nfz, ALU.max).then_inc(ml_abs, 1)

            def ml_log_forget():
                dve.wait_ge(ml_ln, 1)
                last = None
                for tt in range(TT):
                    last = dve.scalar_tensor_tensor(g_lf[:, tt, :], g_fz[:, tt, :], 0.0, g_ln[:, tt, :],
                                                    ALU.min, ALU.subtract)
                last.then_inc(ml_lf, 1)

            def diagonals(values):
                for h in range(ML_H):
                    for tt in range(TT):
                        last = dve.tensor_scalar(diag[:, h, tt * P:(tt + 1) * P], ident, values[:, tt, h:h + 1], None,
                                                 ALU.mult)
                last.then_inc(ml_diag, 1)

            def ml_cumulated():
                dve.wait_ge(ml_cum, 1)
                mark(dve.tensor_copy(g_F, score[:, 0, 0:2 * ML_H].rearrange("p (t h) -> p t h", t=TT)))
                own()
                mark(dve.tensor_tensor(g_g, g_i, g_F, ALU.subtract))
                own()
                diagonals(g_g)

            spread = score[:, :, :].rearrange("p b (h s) -> p (b h) s", h=2)

            def ml_maxima():
                dve.wait_ge(ml_spread, 1)
                for tt in range(TT):
                    mark(dve.tensor_tensor(maxed[:, :, :], spread[:, :, tt * P:(tt + 1) * P],
                                           spread_to(causal, 1, [ML_H, P]), ALU.add))
                    own()
                    mark(dve.tensor_reduce(g_max[:, tt, :], maxed[:, :, :], AXIS, ALU.max))
                    own()
                mark(dve.tensor_reduce(g_max2[:, 1, :], spread[:, :, 0:P], AXIS, ALU.max))
                own()
                mark(dve.tensor_tensor(g_max[:, 1, :], g_max[:, 1, :], g_max2[:, 1, :], ALU.max))
                own()
                mark(dve.tensor_scalar(g_max, g_max, 0.0, None, ALU.max))
                own()
                mark(dve.tensor_tensor(g_nm, g_F, g_max, ALU.add))
                diagonals(g_max)

            def ml_arguments():
                dve.wait_ge(ml_spread, 2)
                for src, dst in ((slice(0, P), slice(0, P)), (slice(P, S), TALL)):
                    dve.tensor_tensor(ml_w[:, :, dst], spread_to(causal_t, 1, [ML_H, P]), spread[:, :, src],
                                      ALU.subtract).then_inc(ml_args, 1)

            def convolve(b):
                name = f"conv{b}"
                wait_turn(dve, name)
                done = [0, 0]
                for shift in range(CONV):
                    for j in range(2):
                        c = 2 * b + j
                        tap = gain("mlstm_conv_w", (CONV - 1 - shift) * DC + c)
                        src = turn_bank(name)[:, j * S:(j + 1) * S - shift]
                        dst = ml_t[:, c, shift:]
                        if shift == 0:
                            ins = dve.tensor_scalar(dst, src, tap, gain("mlstm_conv_b", c), ALU.mult, ALU.add)
                        else:
                            own(done[j])
                            ins = dve.scalar_tensor_tensor(dst, src, tap, dst, ALU.mult, ALU.add)
                        if shift == CONV - 1 and j == 1:
                            ins.then_inc(turn_dve, 1)
                        else:
                            done[j] = mark(ins)

            def silu(b):
                dve.wait_ge(ml_sigm, b + 1)
                two = ml_t[:, 2 * b:2 * b + 2, :]
                dve.tensor_tensor(two, two, ml_sig[:, b % 2, :, :], ALU.mult).then_inc(ml_silu, 1)

            def ml_weigh(h):
                dve.wait_ge(ml_scored, h + 1)
                dve.wait_ge(ml_wexp, h + 1)
                dve.scalar_tensor_tensor(ml_s[:, h, :], score[:, h % 2, 0:SCORE], ML_QK ** -0.5, ml_w[:, h, :],
                                         ALU.mult, ALU.mult).then_inc(ml_weighted, 1)

            def ml_value(h):
                for tt in range(TT):
                    copy_turn(f"mv{h}.{tt}", ml_n[:, tt, h, :], turn_bank(f"mv{h}.{tt}")[:, 0:ML_V + 1])

            def ml_finish():
                dve.wait_ge(turn_dve, turn["mv3.1"]["dve_end"])
                dve.wait_ge(ml_em, 1)
                den = ml_n[:, :, :, ML_V]
                mark(dve.scalar_tensor_tensor(r_abs, den, -1.0, den, ALU.mult, ALU.max))
                own()
                mark(dve.tensor_tensor(r_dmax, r_abs, g_em, ALU.max))
                own()
                mark(dve.reciprocal(r_dinv, r_dmax))
                own()
                dve.wait_ge(turn_act, turn["mv3.1"]["act_end"])
                mark(dve.tensor_tensor(r_t, r_ss, r_dinv, ALU.mult))
                own()
                dve.tensor_tensor(r_ms, r_t, r_dinv, ALU.mult).then_inc(ml_ms, 1)
                dve.wait_ge(ml_norm, 1)
                mark(dve.tensor_tensor(r_sc, r_dinv, r_r, ALU.mult))
                own()
                dve.wait_ge(group_act, groups["mo1"]["act_end"])
                for h in range(ML_H):
                    cols = slice(h * ML_V, (h + 1) * ML_V)
                    for tt in range(TT):
                        dve.scalar_tensor_tensor(ml_o[:, tt, cols], ml_n[:, tt, h, 0:ML_V], r_sc[:, tt, h:h + 1],
                                                 ml_o[:, tt, cols], ALU.mult, ALU.mult).then_inc(ml_y, 1)

            for c in range(0, DC, 2):
                split_turn(f"x2.{c}")
            dense("gate")
            ml_gates()
            dense("mq", {1: ml_log_forget, 3: ml_cumulated})
            dense("mk", {0: ml_maxima, 1: lambda: convolve(0), 2: lambda: convolve(1), 3: ml_arguments})
            dense("mv0", {1: lambda: convolve(2), 3: lambda: convolve(3)})
            dense("mv1", {n: (lambda n=n: silu(n)) for n in range(4)})
            dense("mo0", {n: (lambda n=n: ml_weigh(n)) for n in range(4)})
            dense("mo1", {n: (lambda n=n: ml_value(n - 1)) for n in range(1, 4)})
            ml_value(3)
            ml_finish()
            for c in range(0, DC, 2):
                split_turn(f"yT.{c}")
            dense("mw0")
            add_to_x("mw0", 0)
            dense("mw1", {2: lambda: split_turn("x3.0"), 3: lambda: split_turn("x3.2")})
            add_to_x("mw1", 1)
            split_turn("x3.4")
            split_turn("x3.6")
            mlp(1, 3)

            dve.wait_ge(rstd_ready, 5)
            dve.wait_ge(fgain_loaded, 16)
            for n in range(2):
                cols = slice(n * HALF, (n + 1) * HALF)
                for tt in range(TT):
                    dve.scalar_tensor_tensor(x[:, tt, cols], x[:, tt, cols], rstd[:, 4, tt:tt + 1],
                                             final_gain[:, cols], ALU.mult, ALU.mult).then_inc(x_ready, 1)

            def shared_key():
                dve.wait_ge(group_act, groups["ckv"]["act_end"])
                dve.wait_ge(b2_loaded, 64)
                dve.wait_ge(trig_ready, 1)
                kr = lat_sb[:, :, LAT:]
                mark(dve.tensor_tensor(kr_sb[:, 1, :, :], kr, kr, ALU.mult))
                mark(dve.tensor_tensor(kr_sb[:, 0, :, :], kr, spread_to(rope_gain[:, 1, :], 1, [TT, ROPE]), ALU.mult))
                own()
                mark(dve.tensor_reduce(kr_ss[:, :], kr_sb[:, 1, :, :], AXIS, ALU.add))
                own()
                lo_half, hi_half = slice(0, ROPE // 2), slice(ROPE // 2, ROPE)
                mark(rotate(kr_sb[:, 3, :, lo_half], kr_sb[:, 3, :, hi_half], kr_sb[:, 1, :, lo_half],
                            kr_sb[:, 2, :, lo_half], kr_sb[:, 0, :, lo_half], kr_sb[:, 0, :, hi_half],
                            trig[:, 1, :, P:], trig[:, 0, :, P:]))

            def ret_rotate(name):
                n = ("rq0", "rq1", "rk0", "rk1").index(name)
                dve.wait_ge(group_act, groups[name]["act_end"])
                if n:
                    wait_turn(dve, ("rq0", "rq1", "rk0")[n - 1] + "b")
                    dve.wait_ge(ret_roped, n)
                src, dst = (work[:, i, :, :].rearrange("p t (h d) -> p t h d", h=2) for i in range(2))
                tmp = [l_work[:, i * HALF:(i + 1) * HALF].rearrange("p (t h d) -> p t h d", t=TT, h=2)
                       for i in range(2)]
                cos, sin = (spread_to(trig[:, i, :, 0:P], 2, [TT, 2, P]) for i in (1, 0))
                rotate(dst[:, :, :, 0:P], dst[:, :, :, P:], tmp[0], tmp[1], src[:, :, :, 0:P], src[:, :, :, P:],
                       cos, sin).then_inc(ret_roped, 1)

            def ret_copy(name, half):
                n = ("rq0", "rq1", "rk0", "rk1").index(name)
                turn_name = f"{name}{'ab'[half]}"
                c = 4 * (n % 2) + 2 * half
                copy_turn(turn_name, (rq_t if n < 2 else rk_t)[:, c:c + 2, :],
                          turn_bank(turn_name).rearrange("p (c s) -> p c s", c=2))

            def ret_decay(h):
                dve.wait_ge(ret_scored, h + 1)
                dve.scalar_tensor_tensor(ret_s[:, h, :], score[:, h % 2, 0:SCORE], RET_QK ** -0.5, ret_s[:, h, :],
                                         ALU.mult, ALU.mult).then_inc(ret_decayed, 1)

            def ret_value(h):
                dve.wait_ge(group_act, groups[f"ret{h}"]["act_end"])
                for tt in range(TT):
                    dve.tensor_copy(ret[:, tt, h * HALF:(h + 1) * HALF], group_ps(f"ret{h}")[:, tt, :])\
                        .then_inc(group_dve, 1)

            def gate_sigma(n):
                dve.wait_ge(group_act, groups[f"rg{n}"]["act_end"])
                for tt in range(TT):
                    dve.scalar_tensor_tensor(work[:, n % 2, tt, :], group_ps(f"rg{n}")[:, tt, :],
                                             rstd[:, 5, tt:tt + 1], work[:, n % 2, tt, :], ALU.mult, ALU.mult)\
                        .then_inc(group_dve, 1)

            def gate_out(n):
                dve.wait_ge(ret_norm, 1)
                dve.wait_ge(group_dve, max(groups[f"rg{n}"]["dve_end"], groups["ret3"]["dve_end"]))
                cols = slice(n * HALF, (n + 1) * HALF)
                for tt in range(TT):
                    last = dve.scalar_tensor_tensor(ret[:, tt, cols], ret[:, tt, cols], ret_r[:, tt, n:n + 1],
                                                    work[:, n % 2, tt, :], ALU.mult, ALU.mult)
                last.then_inc(gated, 1)

            def mla_sums_q():
                for tt in range(TT):
                    dve.wait_ge(l_squares, tt + 1)
                    scratch = l_work[:, 0:MLA_H * MLA_QK] if tt == 0 else lk_flat[:, 0:MLA_H * MLA_QK]
                    dve.tensor_reduce(lq_ss[:, tt, :], scratch.rearrange("p (h d) -> p h d", d=MLA_QK), AXIS, ALU.add)\
                        .then_inc(l_sq, 1)

            def mla_sums_k():
                for tt in range(TT):
                    dve.wait_ge(l_squares, TT + tt + 1)
                    scratch = l_work[:, 0:MLA_H * NOPE] if tt == 0 else lk_flat[:, 0:MLA_H * NOPE]
                    dve.tensor_reduce(lk_ss[:, tt, :], scratch.rearrange("p (h d) -> p h d", d=NOPE), AXIS, ALU.add)\
                        .then_inc(l_sq, 1)
                dve.wait_ge(l_sq, 4)
                for tt in range(TT):
                    dve.tensor_scalar(lk_ss[:, tt, :], lk_ss[:, tt, :], kr_ss[:, tt:tt + 1], None, ALU.add)\
                        .then_inc(l_sq, 1)

            def mla_q(tt):
                dve.wait_ge(l_norm, 1)
                q = lq_sb[:, tt, :, :]
                mark(dve.tensor_tensor(q, q, spread_to(lq_r[:, tt, :], 2, [MLA_H, MLA_QK]), ALU.mult))
                own()
                part = lq_sb[:, tt, :, NOPE:]
                mark(dve.tensor_tensor(part, part, spread_to(rope_gain[:, 0, :], 1, [MLA_H, ROPE]), ALU.mult))
                own()
                half = ROPE // 2
                cos, sin = (spread_to(trig[:, i, tt, P:], 1, [MLA_H, half]) for i in (1, 0))
                rotate(rot[:, tt, :, 0:half], rot[:, tt, :, half:], prod[:, tt, :, 0:half], prod[:, tt, :, half:],
                       part[:, :, 0:half], part[:, :, half:], cos, sin).then_inc(lq_ready, 1)

            def mla_k():
                dve.wait_ge(l_norm, 2)
                for tt in range(TT):
                    k = kv[:, tt, :, 0:NOPE]
                    last = dve.tensor_tensor(k, k, spread_to(lk_r[:, tt, :], 2, [MLA_H, NOPE]), ALU.mult)
                last.then_inc(lk_ready, 1)

            def mla_k_rot():
                wait_turn(dve, "mqr1")
                for tt in range(TT):
                    last = dve.tensor_tensor(rot[:, tt, :, :], spread_to(kr_sb[:, 3, tt, :], 1, [MLA_H, ROPE]),
                                             spread_to(lk_r[:, tt, :], 2, [MLA_H, ROPE]), ALU.mult)
                last.then_inc(lk_ready, 1)

            def mla_rot_copy(which, b):
                name = f"{which}r{b}"
                copy_turn(name, (lq_t if which == "mq" else lk_t)[:, 2 * b:2 * b + 2, :],
                          turn_bank(name).rearrange("p (h s) -> p h s", h=2))

            def mla_logits(h):
                dve.wait_ge(l_scored, h + 1)
                b = h % 2
                if h >= 2:
                    wait_turn(dve, f"lp{h - 2}")
                dve.tensor_tensor(l_e[:, b, :], score[:, b, 0:SCORE], mask[:, :], ALU.add).then_inc(l_masked, 1)
                dve.wait_ge(l_masked, h + 1)
                for j, cols in enumerate((WIDE, TALL)):
                    last = dve.tensor_reduce(l_nm[:, b, j:j + 1], l_e[:, b, cols], AXIS, ALU.max, negate=True)
                last.then_inc(l_maxed, 1)

            def mla_recip(h):
                dve.wait_ge(l_exped, h + 1)
                if h >= 2:
                    dve.wait_ge(turn_act, turn[f"lv{h - 2}"]["act_end"])
                dve.reciprocal(l_rec[:, h % 2, :], l_sum[:, h % 2, :]).then_inc(l_reced, 1)

            def mla_slot(n):
                if n < MLA_H:
                    mla_logits(n)
                if 1 <= n <= MLA_H:
                    mla_recip(n - 1)

            for c in range(0, DC, 2):
                split_turn(f"x5.{c}")
            dense("cq")
            dense("ckv")
            dense("rq0", {0: shared_key, 1: lambda: split_turn("lat.0"), 2: lambda: split_turn("lat.2"),
                          3: lambda: split_turn("lat.4")})
            for name, before in (("rq1", "rq0"), ("rk0", "rq1"), ("rk1", "rk0")):
                dense(name, {0: lambda before=before: ret_rotate(before), 2: lambda before=before: ret_copy(before, 0),
                             3: lambda before=before: ret_copy(before, 1)})
            dense("uq0", {0: lambda: ret_rotate("rk1")})
            dense("uq1", {1: lambda: ret_copy("rk1", 0)})
            dense("uq2", {1: lambda: ret_copy("rk1", 1)})
            for n in range(4):
                dense(f"ukv{n}")
                ret_decay(n)
            dense("rv0", {0: mla_sums_q, 3: mla_sums_k})
            dense("rv1", {0: lambda: mla_q(0), 1: lambda: mla_q(1), 2: mla_k})
            ret_value(0)
            dense("rv2")
            ret_value(1)

            def rv3_slot(n):
                if n == 0:
                    mla_rot_copy("mq", 0)
                    mla_rot_copy("mq", 1)
                    mla_k_rot()
            dense("rv3", {n: (lambda n=n: rv3_slot(n)) for n in range(4)})
            ret_value(2)
            dense("rg0", {n: (lambda n=n: mla_rot_copy("mk", n)) for n in range(2)})
            gate_sigma(0)
            ret_value(3)
            dense("rg1", {n: (lambda n=n: mla_slot(n)) for n in range(4)})
            gate_out(0)
            gate_sigma(1)
            dense("rg2", {n: (lambda n=n: mla_slot(4 + n)) for n in range(4)})
            gate_out(1)
            gate_sigma(2)
            dense("rg3", {0: lambda: mla_slot(8)})
            gate_out(2)
            gate_sigma(3)
            gate_out(3)
            dense("gm0", {n: (lambda n=n: split_turn(f"roT.{2 * n}")) for n in range(4)})
            dense("gm1", {n: (lambda n=n: split_turn(f"roT.{8 + 2 * n}")) for n in range(4)})
            dense("gr0")
            dense("gr1")

            def mix_ret(n):
                wait_group(dve, f"br{n}")
                dve.wait_ge(group_act, groups["gr1"]["act_end"])
                cols = slice(n * HALF, (n + 1) * HALF)
                for tt in range(TT):
                    dve.tensor_tensor(mix[:, tt, cols], group_ps(f"br{n}")[:, tt, :], gr[:, tt, cols], ALU.mult)\
                        .then_inc(group_dve, 1)

            def mix_mla(n):
                wait_group(dve, f"bm{n}")
                cols = slice(n * HALF, (n + 1) * HALF)
                for tt in range(TT):
                    dve.tensor_tensor(gm[:, tt, cols], group_ps(f"bm{n}")[:, tt, :], gm[:, tt, cols], ALU.mult)\
                        .then_inc(group_dve, 1)
                for tt in range(TT):
                    dve.wait_ge(group_dve, groups[f"bm{n}"]["dve_end"] - 1 + tt)
                    dve.tensor_tensor(mix[:, tt, cols], mix[:, tt, cols], gm[:, tt, cols], ALU.add)\
                        .then_inc(mixed, 1)

            dense("br0", {2 * n + 1: (lambda n=n: split_turn(f"moT.{2 * n}")) for n in range(4)})
            mix_ret(0)
            dense("br1")
            mix_ret(1)
            dense("bm0")
            mix_mla(0)
            dense("bm1", {2: lambda: split_turn("mixT.0"), 3: lambda: split_turn("mixT.2")})
            mix_mla(1)
            split_turn("mixT.4")
            split_turn("mixT.6")
            dense("wo0")
            add_to_x("wo0", 0)
            dense("wo1", {2: lambda: split_turn("x6.0"), 3: lambda: split_turn("x6.2")})
            add_to_x("wo1", 1)
            split_turn("x6.4")
            split_turn("x6.6")
            mlp(2, 6)

            split_turn("pT.0")
            dense("pl0")
            dense("pl1")
            for c in range(0, DC, 2):
                split_turn(f"x7.{c}")
            for n in range(2):
                dense(f"pg{n}")
                dve.wait_ge(group_act, groups[f"pg{n}"]["act_end"])
                cols = slice(n * HALF, (n + 1) * HALF)
                for tt in range(TT):
                    mark(dve.tensor_tensor(gate[:, tt, cols], gate[:, tt, cols], ple[:, tt, cols], ALU.mult))
                    own()
                    dve.tensor_tensor(gate[:, tt, cols], gate[:, tt, cols], x[:, tt, cols], ALU.add)\
                        .then_inc(out_ready, 1)

        @block.gpsimd
        def _(pool):
            mark, own = own_order(pool, pool_step)

            def factor(dst, means, sums, scale, eps, done):
                mark(pool.tensor_scalar(means, sums, scale, eps, ALU.mult, ALU.add))
                own()
                shape = dst.shape[1:]
                half = mhalf[:, 0:math.prod(shape)]
                if len(shape) == 2:
                    half = half.rearrange("p (a b) -> p a b", a=shape[0])
                pool.tensor_tensor(dst, means, half, ALU.pow).then_inc(done, 1)

            def x_factor(v):
                pool.wait_ge(x_squared, TT * (v + 1))
                factor(rstd[:, v, :], msx[:, v, :], ssx[:, v, :], 1 / D, EPS, rstd_ready)

            pool.dma_start(onehot[0:BUCKETS + 1, :], w["c_onehot"]).then_inc(small_loaded, 16)
            pool.dma_start(table[0:BUCKETS, :], w["rel_bias"]).then_inc(small_loaded, 16)
            mark(pool.memset(table[BUCKETS:BUCKETS + 1, :], NEG))
            own()
            mark(pool.memset(zeros[:, :], 0.0))
            own()
            pool.memset(mhalf[:, :], -0.5).then_inc(set_ready, 1)
            for i, name in enumerate(("attn_lambda_q1", "attn_lambda_k1", "attn_lambda_q2", "attn_lambda_k2")):
                pool.dma_start(lam_in[:, i, :], w[name][0, :].partition_broadcast(P)).then_inc(lam_loaded, 16)
            pool.dma_start(inv[:, :], w["c_inv"][0, :].partition_broadcast(P)).then_inc(pos_loaded, 16)
            with nc.allow_non_contiguous_dma(reason="256 positions"):
                pool.dma_start(pos_i[:, :], w["positions_2"][0, :].rearrange("(t p) -> p t", p=P))\
                    .then_inc(pos_loaded, 16)
            pool.wait_ge(bias_rows_ready, 1)
            pool.dma_start(bias_dram[:, 0:3 * P - 1], bias_rows[0:DA_H, :]).then_inc(bias_stored, 16)
            pool.wait_ge(bias_stored, 16)
            rows = bass.AP(bias_dram.tensor, 0, [[0, P], [SCORE, DA_H], [1, 3 * P - 1]])
            pool.dma_start(bias_rep[:, :, 0:3 * P - 1], rows).then_inc(bias_stored, 16)
            pool.wait_ge(bias_stored, 32)
            for cols, at in ((WIDE, P - 1), (TALL, 2 * P - 1)):
                n = cols.stop - cols.start
                skewed = bass.AP(bias_rep.tensor, at, [[DA_H * SCORE - 1, P], [SCORE, DA_H], [1, n]])
                pool.dma_start(bias[:, :, cols], skewed).then_inc(bias_loaded, 16)
            pool.wait_ge(set_ready, 1)
            x_factor(0)
            for half in range(2):
                pool.wait_ge(turn_act, turn[f"av{4 * half + 3}"]["act_end"])
                keep = (1.0 - LAMBDA_INIT) ** -2
                factor(da_r[:, half, :, :], da_ms[:, half, :, :], da_ss[:, half, :, :], keep / P, keep * EPS, da_norm)
            x_factor(1)
            pool.wait_ge(x_ready, x_version(2))
            pool.dma_start(gate_b[:, 0:ML_H], w["mlstm_b_i"][0, :].partition_broadcast(P)).then_inc(ml_loaded, 16)
            pool.dma_start(gate_b[:, ML_H:], w["mlstm_b_f"][0, :].partition_broadcast(P)).then_inc(ml_loaded, 16)
            pool.memset(ml_v[:, :, :, ML_V:], 1.0).then_inc(ml_ones, 1)
            x_factor(2)
            pool.wait_ge(ml_ms, 1)
            factor(r_r, r_t, r_ms, 1 / ML_V, EPS, ml_norm)
            pool.wait_ge(x_ready, x_version(3))
            pool.dma_start(final_gain[:, :], w["final_norm"].partition_broadcast(P)).then_inc(fgain_loaded, 16)
            x_factor(3)
            x_factor(4)
            pool.wait_ge(x_ready, x_version(5))
            pool.dma_start(rope_gain[:, 0, :], w["q_norm_2"][0, NOPE:].partition_broadcast(P)).then_inc(b2_loaded, 16)
            pool.dma_start(rope_gain[:, 1, :], w["k_norm_2"][0, NOPE:].partition_broadcast(P)).then_inc(b2_loaded, 16)
            pool.dma_start(mask[:, :], w["c_mask"]).then_inc(b2_loaded, 16)
            pool.dma_start(ret_s[:, :, :], w["c_decay"]).then_inc(b2_loaded, 16)
            x_factor(5)
            pool.wait_ge(lat_sq, 2 * TT)
            mark(pool.tensor_scalar(lat_ms[:, 0, :], lat_ss[:, 0, :], 1 / Q_LORA, EPS, ALU.mult, ALU.add))
            mark(pool.tensor_scalar(lat_ms[:, 1, :], lat_ss[:, 1, :], 1 / KV_LORA, EPS, ALU.mult, ALU.add))
            own()
            pool.tensor_tensor(lat_r[:, :, :], lat_ms[:, :, :], mhalf[:, 0:4].rearrange("p (a b) -> p a b", a=2),
                               ALU.pow).then_inc(lat_norm, 1)
            pool.wait_ge(group_act, groups["uq2"]["act_end"])
            pool.wait_ge(ret_roped, 4)
            for tt in range(TT):
                q = flat_q[:, tt * MLA_H * MLA_QK:(tt + 1) * MLA_H * MLA_QK]
                scratch = (l_work if tt == 0 else lk_flat)[:, 0:MLA_H * MLA_QK]
                pool.tensor_tensor(scratch, q, q, ALU.mult).then_inc(l_squares, 1)
            pool.wait_ge(group_act, groups["ukv3"]["act_end"])
            for tt in range(TT):
                pool.wait_ge(l_sq, tt + 1)
                k = kv[:, tt, :, 0:NOPE]
                scratch = (l_work if tt == 0 else lk_flat)[:, 0:MLA_H * NOPE].rearrange("p (h d) -> p h d", d=NOPE)
                pool.tensor_tensor(scratch, k, k, ALU.mult).then_inc(l_squares, 1)
            factor(lq_r[:, :, :], lq_ms[:, :, :], lq_ss[:, :, :], 1.0, MLA_QK * EPS, l_norm)
            pool.wait_ge(l_sq, 6)
            factor(lk_r[:, :, :], lk_ms[:, :, :], lk_ss[:, :, :], 1 / MLA_QK, EPS, l_norm)
            pool.wait_ge(group_act, groups["ret3"]["act_end"])
            factor(ret_r[:, :, :], ret_ms[:, :, :], ret_ss[:, :, :], 1 / RET_V, EPS, ret_norm)
            pool.wait_ge(x_ready, x_version(6))
            for tt in range(TT):
                pool.dma_start(p_sb[:, tt, :], w["p_2"][0, 0, tt * P:(tt + 1) * P, :]).then_inc(p_loaded, 16)
            x_factor(6)
            x_factor(7)


_INS = ["x", "rel_bias", "attn_norm", "attn_w_in", "attn_lambda_q1", "attn_lambda_k1", "attn_lambda_q2",
        "attn_lambda_k2", "attn_subln", "attn_w_out", "mlstm_norm", "mlstm_w_in", "mlstm_b_i", "mlstm_b_f",
        "mlstm_conv_w", "mlstm_conv_b", "mlstm_head_norm", "mlstm_w_out", "mlp_norm", "mlp_w1", "mlp_w2",
        "final_norm", "p_2", "positions_2", "norm_mix_2", "w_in_2", "ret_norm_2", "q_lat_norm_2", "kv_lat_norm_2",
        "w_uq_2", "w_ukv_2", "q_norm_2", "k_norm_2", "w_br_2", "w_bm_2", "w_o_2", "norm_mlp_2", "w_up_2",
        "w_down_2", "norm_ple_2", "w_ple_gate_2", "w_ple_2"]
_ONE_LAYER = ["attn_w_in", "attn_w_out", "mlstm_w_in", "mlstm_w_out", "w_in_2", "w_uq_2", "w_ukv_2", "w_br_2",
              "w_bm_2", "w_o_2", "w_up_2", "w_down_2", "w_ple_gate_2", "w_ple_2"]


def kernel(**inputs):
    import concourse.bacc as bacc
    from concourse.bass_utils import run_bass_kernel_spmd

    nc = bacc.Bacc("TRN2", target_bir_lowering=False, num_devices=1)
    arrays, w = {}, {}
    for name, a in [(n, np.ascontiguousarray(inputs[n])) for n in _INS] + list(constants().items()):
        arrays[f"in_{name}"] = a
        w[name] = nc.dram_tensor(f"in_{name}", a.shape, mybir.dt.from_np(a.dtype), kind="ExternalInput").ap()
    for name in _ONE_LAYER:
        w[name] = w[name][0]
    out = nc.dram_tensor("out_0", (1, S, D), F32, kind="ExternalOutput").ap()
    build(nc, w, out)
    r = run_bass_kernel_spmd(nc, [arrays], core_ids=[0])
    return r.results[0]["out_0"]
```

```python
import math
from contextlib import ExitStack

import numpy as np

import concourse.bass as bass
from concourse import mybir

F32 = mybir.dt.float32
F32R = mybir.dt.float32r
BF16 = mybir.dt.bfloat16
I32 = mybir.dt.int32
ALU = mybir.AluOpType
ACT = mybir.ActivationFunctionType
AXIS = mybir.AxisListType.X

P = 128
S = 256
TT = S // P
D = 1024
DC = D // P
FF = 4 * D
HALF = 512
EPS = 1e-6
NEG = -1e30

UNIT = 1024
RAW = 4
RING = 8
AHEAD = 5

DA_H, DA_D = 8, 64
ML_H, ML_QK, ML_V = 4, 128, 256
CONV = 4
RET_H, RET_QK, RET_V = 4, 256, 512
MLA_H, NOPE, ROPE = 8, 128, 64
MLA_QK = NOPE + ROPE
Q_LORA, KV_LORA = 384, 256
LAT = Q_LORA + KV_LORA
BUCKETS = 32
LAMBDA_INIT = 0.8 - 0.6 * math.exp(-0.3 * 0)

WIDE, TALL = slice(0, 2 * P), slice(2 * P, 3 * P)
SCORE = 3 * P

GAIN_ROWS = [("attn_norm", 8), ("mlp_norm", 16), ("mlstm_norm", 8), ("mlstm_head_norm", 8), ("norm_mix_2", 8),
             ("ret_norm_2", 16), ("q_lat_norm_2", 3), ("kv_lat_norm_2", 2), ("norm_mlp_2", 8), ("norm_ple_2", 8),
             ("attn_subln", 1), ("mlstm_conv_w", 32), ("mlstm_conv_b", 8), ("q_norm_2", 1), ("k_norm_2", 1)]
GAIN = {}
for _name, _rows in GAIN_ROWS:
    GAIN[_name] = sum(r for n, r in GAIN_ROWS[:len(GAIN)])
assert sum(r for _, r in GAIN_ROWS) == P

TWO_PI = 2 * math.pi
PI_A = 6.28125
PI_B = float(np.float32(math.floor((TWO_PI - PI_A) * 2**20) / 2**20))
PI_C = TWO_PI - PI_A - PI_B
ROUND = 1.5 * 2**23
PI_SAFE = 3.1415925


def constants():
    i = np.arange(P)
    causal = np.where(i[:, None] >= i[None, :], 0.0, NEG)
    dist = S - 1 - np.arange(3 * P - 1)
    d = np.maximum(dist, 1).astype(np.float32)
    exact = BUCKETS // 2
    large = exact + (np.log(d / exact) / math.log(128 / exact) * (BUCKETS - exact)).astype(np.int32)
    bucket = np.where(dist < exact, dist, np.minimum(large, BUCKETS - 1))
    bucket = np.where(dist < 0, BUCKETS, bucket)
    onehot = bucket[None, :] == np.arange(BUCKETS + 1)[:, None]
    log_g = np.log1p(-np.exp2(-5.0 - np.arange(RET_H)))
    diff = np.arange(S)[None, :] - i[:, None]
    wide = np.where(diff[:, None, :] >= 0, np.exp(np.maximum(diff, 0)[:, None, :] * log_g[None, :, None]), 0.0)
    decay = np.concatenate([wide, wide[:, :, 0:P]], axis=2)
    inv = [10000.0 ** (-np.arange(n, dtype=np.float32) / np.float32(n)) for n in (RET_QK // 2, ROPE // 2)]
    square = np.stack([np.eye(P), np.ones((P, P)), i[:, None] <= i[None, :], causal, causal.T], axis=1)
    mask = np.concatenate([np.zeros((P, P)), causal, causal], axis=1)
    out = {"c_square": square, "c_onehot": onehot, "c_decay": decay, "c_inv": np.concatenate(inv)[None, :],
           "c_mask": mask}
    return {k: np.ascontiguousarray(v, dtype=np.float32) for k, v in out.items()}


NINV = RET_QK // 2 + ROPE // 2


def schedule(w):
    groups, stream = {}, []
    count = [0]

    def group(name, weight, col, ncols, source, nchunks, act, dve, rows=0, per=2, last=None):
        groups[name] = dict(index=len(groups), units=[], ncols=ncols, source=source, act=act, dve=dve,
                            weight=weight, col=col, nchunks=nchunks, rows=rows, per=per)
        if weight is not None:
            chunks(name, 0, nchunks if last is None else last)

    def chunks(name, first, last):
        g, c = groups[name], first
        while c < last:
            n = min(g["per"], last - c)
            src = g["weight"][g["rows"] + c * P:g["rows"] + (c + n) * P, g["col"]:g["col"] + g["ncols"]]
            g["units"].append((count[0], c, n))
            stream.append(("unit", count[0], src.rearrange("(c p) n -> p c n", p=P), n, g["ncols"]))
            count[0] += 1
            c += n

    def swap_pairs():
        group(f"none{len(groups)}", None, 0, 0, None, 0, 0, 0)

    def mlp(which, w1, w2):
        stream.append(("mlp", count[0], w1, w2, which))
        mlps.append(count[0])
        count[0] += 2 * 4 * (FF // HALF)

    mlps = []
    qkv = w["attn_w_in"]
    for name, col in (("q0", 0), ("k0", D), ("q1", HALF), ("k1", D + HALF), ("v0", 2 * D), ("v1", 2 * D + HALF)):
        group(name, qkv, col, HALF, "x0", DC, 2, 0)
    for n in range(2):
        group(f"ao{n}", w["attn_w_out"], n * HALF, HALF, "oT", DC, 0, 0, last=DC // 2)
    for n in range(2):
        chunks(f"ao{n}", DC // 2, DC)
    mlp(0, w["mlp_w1"][0], w["mlp_w2"][0])
    swap_pairs()
    ml = w["mlstm_w_in"]
    group("gate", ml, 3 * D, 2 * ML_H, "x2", DC, 2, 0, per=8, last=0)
    group("mq", ml, 0, HALF, "x2", DC, 2, 0, last=DC // 2)
    chunks("gate", 0, DC)
    chunks("mq", DC // 2, DC)
    for name, col in (("mk", HALF), ("mv0", D), ("mv1", D + HALF), ("mo0", 2 * D), ("mo1", 2 * D + HALF)):
        group(name, ml, col, HALF, "x2", DC, 2, 0)
    for n in range(2):
        group(f"mw{n}", w["mlstm_w_out"], n * HALF, HALF, "yT", DC, 0, 0, last=DC // 2)
    for n in range(2):
        chunks(f"mw{n}", DC // 2, DC)
    mlp(1, w["mlp_w1"][1], w["mlp_w2"][1])
    swap_pairs()
    win = w["w_in_2"]
    at = np.cumsum([0, D, D, 2 * D, 2 * D, Q_LORA, KV_LORA + ROPE, D, D]).tolist()
    group("cq", win, at[4], Q_LORA, "x5", DC, 2, 0)
    group("ckv", win, at[5], KV_LORA + ROPE, "x5", DC, 2, 0)
    for name, col in (("rq0", at[0]), ("rq1", at[0] + HALF), ("rk0", at[1]), ("rk1", at[1] + HALF)):
        group(name, win, col, HALF, "x5", DC, 2, 0)
    for n in range(3):
        group(f"uq{n}", w["w_uq_2"], n * HALF, HALF, "latq", Q_LORA // P, 2, 0)
    for n in range(4):
        group(f"ukv{n}", w["w_ukv_2"], n * HALF, HALF, "latkv", KV_LORA // P, 2, 0)
    for n in range(4):
        group(f"rv{n}", win, at[2] + n * HALF, HALF, "x5", DC, 2, 0)
        if n:
            group(f"ret{n - 1}", None, 0, HALF, None, 0, 2, 2)
    group("rg0", win, at[3], HALF, "x5", DC, 2, 0)
    group("ret3", None, 0, HALF, None, 0, 2, 2)
    for n in range(1, 4):
        group(f"rg{n}", win, at[3] + n * HALF, HALF, "x5", DC, 2, 0)
    for name, col in (("gm0", at[7]), ("gm1", at[7] + HALF), ("gr0", at[6]), ("gr1", at[6] + HALF)):
        group(name, win, col, HALF, "x5", DC, 2, 0)
    for n in range(2):
        group(f"br{n}", w["w_br_2"], n * HALF, HALF, "roT", 2 * DC, 0, 2)
    for n in range(2):
        group(f"bm{n}", w["w_bm_2"], n * HALF, HALF, "moT", DC, 0, 2)
    for n in range(2):
        group(f"wo{n}", w["w_o_2"], n * HALF, HALF, "mixT", DC, 0, 0)
    mlp(2, w["w_up_2"], w["w_down_2"])
    assert groups["ao1"]["index"] % 2 and groups["mw1"]["index"] % 2 and groups["wo1"]["index"] % 2
    for n in range(2):
        group(f"pl{n}", w["w_ple_2"], n * HALF, HALF, "pT", 2, 2, 0)
    for n in range(2):
        group(f"pg{n}", w["w_ple_gate_2"], n * HALF, HALF, "x7", DC, 2, 0)

    act = dve = 0
    by_index = []
    for g in groups.values():
        act, dve = act + g["act"], dve + g["dve"]
        g["act_end"], g["dve_end"] = act, dve
        by_index.append(g)
    return groups, by_index, stream, mlps


def turns():
    order = [("gains", 1, 0)]

    def split(name, chunks, c=0):
        for n in chunks:
            order.append((f"{name}.{c}", n, n))
            c += n

    pairs = [2] * (DC // 2)
    split("x0", pairs)
    for name in ("q0", "k0", "q1", "k1"):
        order.extend([(f"{name}a", 0, 1), (f"{name}b", 0, 1)])
    order.extend([("ap0", 1, 0), ("ap1", 1, 0)])
    for h in range(DA_H):
        if h == 4:
            split("oT0", [2, 2])
        order.append((f"av{h}", 2, 1))
        if h < 6:
            order.append((f"ap{h + 2}", 1, 0))
    split("oT1", [2, 2])
    split("x1", pairs)
    split("x2", pairs)
    for b in range(4):
        order.append((f"conv{b}", 2, 1))
    for h in range(ML_H):
        order.extend([(f"mv{h}.0", 2, 0), (f"mv{h}.1", 2, 0)])
    split("yT", pairs)
    split("x3", pairs)
    split("x5", pairs)
    split("lat", [2, 2, 1])
    for name in ("rq0", "rq1", "rk0", "rk1"):
        order.extend([(f"{name}a", 0, 1), (f"{name}b", 0, 1)])
    for name in ("mq", "mk"):
        order.extend([(f"{name}n{b}", 1, 0) for b in range(4)])
        order.extend([(f"{name}r{b}", 0, 1) for b in range(2)])
    for h in range(MLA_H + 1):
        if h:
            order.append((f"lv{h - 1}", 2, 0))
        if h < MLA_H:
            order.append((f"lp{h}", 1, 0))
    split("roT", pairs + pairs)
    split("moT", pairs)
    split("mixT", pairs)
    split("x6", pairs)
    split("pT", [2])
    split("x7", pairs)
    table, act, dve = {}, 0, 0
    for i, (name, a, d) in enumerate(order):
        table[name] = dict(index=i, act=act, dve=dve, act_end=act + a, dve_end=dve + d)
        act, dve = act + a, dve + d
    by_index = [table[name] for name, _, _ in order]
    return table, by_index


def turn_of(source, c):
    if source == "oT":
        name, c = f"oT{c // 4}", c % 4
    elif source == "latq":
        name = "lat"
    elif source == "latkv":
        name, c = "lat", c + Q_LORA // P
    else:
        name = source
    return f"{name}.{c // 2 * 2}", c % 2


def build(nc, w, out):
    groups, group_list, stream, mlps = schedule(w)
    turn, turn_list = turns()
    total_units = stream[-1][1] + 1
    NX = 8

    with ExitStack() as ctx:
        def sb(name, shape, dt=F32, scope=ctx):
            return scope.enter_context(nc.sbuf_tensor(name, [P, *shape], dt))

        def sem(name):
            return ctx.enter_context(nc.semaphore(name))

        x = sb("x", [TT, D])
        raw = sb("raw", [RAW, UNIT])
        w_hi = sb("w_hi", [RING, UNIT], F32R)
        w_lo = sb("w_lo", [RING, UNIT], F32R)
        a_hi = sb("a_hi", [DC, S], F32R)
        a_lo = sb("a_lo", [DC, S], F32R)
        junk = sb("junk", [D], BF16)
        square = sb("square", [5, P])
        ident, ones, triu, causal, causal_t = (square[:, i, :] for i in range(5))
        gains = sb("gains", [P])
        trig = sb("trig", [2, TT, NINV])
        zeros = sb("zeros", [HALF], BF16)
        mhalf = sb("mhalf", [2 * DA_H])
        ssx = sb("ssx", [NX, TT])
        msx = sb("msx", [NX, TT])
        rstd = sb("rstd", [NX, TT])
        inv_ms = sb("inv_ms", [NX, TT])
        lam_s = sb("lam_s", [2])
        lam_e = sb("lam_e", [2])
        neg_lam = sb("neg_lam", [1])

        with ExitStack() as ph:
            qk_sb = sb("qk_sb", [2, TT, HALF], scope=ph)
            da_q = sb("da_q", [DA_H, S], scope=ph)
            da_k = sb("da_k", [DA_H, S], scope=ph)
            da_v = sb("da_v", [TT, D], scope=ph)
            bias = sb("bias", [DA_H, SCORE], scope=ph)
            da_e = sb("da_e", [2, 2, SCORE], scope=ph)
            da_p = sb("da_p", [DA_H, SCORE], scope=ph)
            da_pt = sb("da_pt", [2, SCORE], scope=ph)
            da_o = sb("da_o", [TT, D], scope=ph)
            o_hi = sb("o_hi", [DC, S], F32R, scope=ph)
            o_lo = sb("o_lo", [DC, S], F32R, scope=ph)
            da_nm = sb("da_nm", [2, 4], scope=ph)
            da_sum = sb("da_sum", [2, 4], scope=ph)
            da_rec = sb("da_rec", [2, 4], scope=ph)
            da_nl = sb("da_nl", [2, 2], scope=ph)
            da_ss = sb("da_ss", [2, TT, DA_H // 2], scope=ph)
            da_ms = sb("da_ms", [2, TT, DA_H // 2], scope=ph)
            da_r = sb("da_r", [2, TT, DA_H // 2], scope=ph)
        with ExitStack() as ph:
            sb("below_setup", [2 * TT * HALF + 2 * DA_H * S], scope=ph)
            gain_rows = sb("gain_rows", [P], scope=ph)
            onehot = sb("onehot", [3 * P - 1], scope=ph)
            table = sb("table", [DA_H], scope=ph)
            bias_rows = sb("bias_rows", [3 * P - 1], scope=ph)
            lam_in = sb("lam_in", [4, DA_D], scope=ph)
            lam_prod = sb("lam_prod", [2, DA_D], scope=ph)
            pos_i = sb("pos_i", [TT], I32, scope=ph)
            pos_f = sb("pos_f", [TT], scope=ph)
            inv = sb("inv", [NINV], scope=ph)
        with ExitStack() as ph:
            sb("below_angles", [2 * TT * HALF + 2 * DA_H * S + TT * D + DA_H * SCORE + 4 * SCORE + DA_H * SCORE
                                + 2 * SCORE], scope=ph)
            ang = sb("ang", [2, TT, NINV], scope=ph)
            turns_k = sb("turns_k", [2, TT, NINV], scope=ph)

        with ExitStack() as ph:
            relu = sb("relu", [TT, HALF], scope=ph)
            hid = sb("hid", [TT, HALF], scope=ph)
            h_hi = sb("h_hi", [HALF // P, S], F32R, scope=ph)
            h_lo = sb("h_lo", [HALF // P, S], F32R, scope=ph)
            final_gain = sb("final_gain", [D], scope=ph)
            p_sb = sb("p_sb", [TT, 2 * P], scope=ph)
            p_hi = sb("p_hi", [2, S], F32R, scope=ph)
            p_lo = sb("p_lo", [2, S], F32R, scope=ph)
            ple = sb("ple", [TT, D], scope=ph)
            gate = sb("gate", [TT, D], scope=ph)
            gained = gate

        with ExitStack() as ph:
            ml_qk = sb("ml_qk", [2, TT, HALF], scope=ph)
            ml_t = sb("ml_t", [2 * ML_H, S], scope=ph)
            ml_v = sb("ml_v", [TT, ML_H, ML_V + 1], scope=ph)
            ml_o = sb("ml_o", [TT, D], scope=ph)
            ml_n = sb("ml_n", [TT, ML_H, ML_V + 1], scope=ph)
            ml_w = sb("ml_w", [ML_H, SCORE], scope=ph)
            ml_s = sb("ml_s", [ML_H, SCORE], scope=ph)
            diag = sb("diag", [ML_H, S], scope=ph)
            maxed = sb("maxed", [ML_H, P], scope=ph)
            y_hi = sb("y_hi", [DC, S], F32R, scope=ph)
            y_lo = sb("y_lo", [DC, S], F32R, scope=ph)
            gate_b = sb("gate_b", [2 * ML_H], scope=ph)
            ml_g = sb("ml_g", [14, TT, ML_H], scope=ph)
            (g_fz, g_nfz, g_abs, g_exp, g_ln, g_lf, g_i, g_F, g_g, g_max, g_max2, g_nm, g_em, g_den) = (
                ml_g[:, i, :, :] for i in range(14))
            ml_r = sb("ml_r", [8, TT, ML_H], scope=ph)
            (r_abs, r_dmax, r_dinv, r_ss, r_t, r_ms, r_r, r_sc) = (ml_r[:, i, :, :] for i in range(8))
            gate_in = sb("gate_in", [TT, 2 * ML_H], scope=ph)

        ph = ctx
        lq_sb = sb("lq_sb", [TT, MLA_H, MLA_QK], scope=ph)
        ret = sb("ret", [TT, RET_H * RET_V], scope=ph)
        ret_s = sb("ret_s", [RET_H, SCORE], scope=ph)
        work = sb("work", [2, TT, HALF], scope=ph)
        mask = sb("mask", [SCORE], scope=ph)
        rope_gain = sb("rope_gain", [2, ROPE], scope=ph)
        lat_ss = sb("lat_ss", [2, TT], scope=ph)
        lat_ms = sb("lat_ms", [2, TT], scope=ph)
        lat_r = sb("lat_r", [2, TT], scope=ph)
        lq_ss = sb("lq_ss", [TT, MLA_H], scope=ph)
        lq_ms = sb("lq_ms", [TT, MLA_H], scope=ph)
        lq_r = sb("lq_r", [TT, MLA_H], scope=ph)
        lk_ss = sb("lk_ss", [TT, MLA_H], scope=ph)
        lk_ms = sb("lk_ms", [TT, MLA_H], scope=ph)
        lk_r = sb("lk_r", [TT, MLA_H], scope=ph)
        kr_ss = sb("kr_ss", [TT], scope=ph)
        l_nm = sb("l_nm", [2, TT], scope=ph)
        l_sum = sb("l_sum", [2, TT], scope=ph)
        l_rec = sb("l_rec", [2, TT], scope=ph)
        ret_ss = sb("ret_ss", [TT, RET_H], scope=ph)
        ret_ms = sb("ret_ms", [TT, RET_H], scope=ph)
        ret_r = sb("ret_r", [TT, RET_H], scope=ph)
        kr_sb = sb("kr_sb", [4, TT, ROPE], scope=ph)
        ret_t = ret[:, :, :].rearrange("p t n -> p (t n)").rearrange("p (c s) -> p c s", s=S)
        rq_t, rk_t = ret_t[:, 0:DC, :], ret_t[:, DC:2 * DC, :]
        flat_q = lq_sb[:, :, :, :].rearrange("p t h d -> p (t h d)")
        lo_sb = flat_q[:, 0:TT * D].rearrange("p (t n) -> p t n", t=TT)
        mix = lo_sb
        KV = TT * MLA_H * (NOPE + P)
        with ExitStack() as ph:
            lat_sb = sb("lat_sb", [TT, LAT + ROPE], scope=ph)
            sb("below_lat", [KV - TT * (LAT + ROPE)], scope=ph)
            lat_hi = sb("lat_hi", [LAT // P, S], F32R, scope=ph)
            lat_lo = sb("lat_lo", [LAT // P, S], F32R, scope=ph)
        with ExitStack() as ph:
            kv = sb("kv", [TT, MLA_H, NOPE + P], scope=ph)
            lq_n = sb("lq_n", [MLA_H, S], scope=ph)
            lq_t = sb("lq_t", [MLA_H // 2, S], scope=ph)
            lk_n = sb("lk_n", [MLA_H, S], scope=ph)
            lk_t = sb("lk_t", [MLA_H // 2, S], scope=ph)
            l_work = sb("l_work", [2048], scope=ph)
        lk_flat = lk_n[:, :, :].rearrange("p h s -> p (h s)")
        rot = l_work[:, 0:TT * MLA_H * ROPE].rearrange("p (t h d) -> p t h d", t=TT, h=MLA_H)
        prod = l_work[:, 1024:2048].rearrange("p (t h d) -> p t h d", t=TT, h=MLA_H)
        l_e = l_work[:, 0:2 * SCORE].rearrange("p (b n) -> p b n", b=2)
        l_pt = l_work[:, 2 * SCORE:4 * SCORE].rearrange("p (b n) -> p b n", b=2)
        with ExitStack() as ph:
            gm = sb("gm", [TT, D], scope=ph)
            gr = sb("gr", [TT, D], scope=ph)
            b_hi = sb("b_hi", [2 * DC, S], F32R, scope=ph)
            b_lo = sb("b_lo", [2 * DC, S], F32R, scope=ph)

        pair = [ctx.enter_context(nc.psum_tensor(f"pair{i}", [P, TT, HALF], F32)) for i in range(2)]
        turn_ps = ctx.enter_context(nc.psum_tensor("turn_ps", [P, 2, HALF], F32))
        score = ctx.enter_context(nc.psum_tensor("score", [P, 2, HALF], F32))
        down = [pair[1], score]

        landed = [sem(f"landed{i}") for i in range(RAW)]
        hi_ready = sem("hi_ready")
        lo_ready = sem("lo_ready")
        unit_used = sem("unit_used")
        group_act = sem("group_act")
        group_dve = sem("group_dve")
        turn_filled = sem("turn_filled")
        turn_act = sem("turn_act")
        turn_dve = sem("turn_dve")
        x_loaded = sem("x_loaded")
        gained_ready = sem("gained_ready")
        x_ready = sem("x_ready")
        x_squared = sem("x_squared")
        rstd_ready = sem("rstd_ready")
        inv_ready = sem("inv_ready")
        act_step = sem("act_step")
        dve_step = sem("dve_step")
        pool_step = sem("pool_step")
        const_loaded = sem("const_loaded")
        gains_loaded = sem("gains_loaded")
        small_loaded = sem("small_loaded")
        pos_loaded = sem("pos_loaded")
        set_ready = sem("set_ready")
        table_ready = sem("table_ready")
        bias_psum = sem("bias_psum")
        bias_rows_ready = sem("bias_rows_ready")
        bias_stored = sem("bias_stored")
        bias_loaded = sem("bias_loaded")
        lam_loaded = sem("lam_loaded")
        lam_sum = sem("lam_sum")
        lam_exp = sem("lam_exp")
        angles_ready = sem("angles_ready")
        trig_ready = sem("trig_ready")
        da_scored = sem("da_scored")
        da_biased = sem("da_biased")
        da_maxed = sem("da_maxed")
        da_exped = sem("da_exped")
        da_mixed = sem("da_mixed")
        da_norm = sem("da_norm")
        da_scaled = sem("da_scaled")
        up_relu = sem("up_relu")
        hid_ready = sem("hid_ready")
        hid_turned = sem("hid_turned")
        hid_hi = sem("hid_hi")
        hid_lo = sem("hid_lo")
        down_half = sem("down_half")
        fgain_loaded = sem("fgain_loaded")
        ml_loaded = sem("ml_loaded")
        ml_abs = sem("ml_abs")
        ml_ln = sem("ml_ln")
        ml_lf = sem("ml_lf")
        ml_cum = sem("ml_cum")
        ml_diag = sem("ml_diag")
        ml_spread = sem("ml_spread")
        ml_args = sem("ml_args")
        ml_wexp = sem("ml_wexp")
        ml_em = sem("ml_em")
        ml_ones = sem("ml_ones")
        ml_silu = sem("ml_silu")
        ml_scored = sem("ml_scored")
        ml_weighted = sem("ml_weighted")
        ml_ms = sem("ml_ms")
        ml_norm = sem("ml_norm")
        ml_y = sem("ml_y")
        b2_loaded = sem("b2_loaded")
        ret_roped = sem("ret_roped")
        lat_sq = sem("lat_sq")
        lat_norm = sem("lat_norm")
        ret_scored = sem("ret_scored")
        ret_decayed = sem("ret_decayed")
        ret_out = sem("ret_out")
        ret_norm = sem("ret_norm")
        l_squares = sem("l_squares")
        l_sq = sem("l_sq")
        l_norm = sem("l_norm")
        lq_ready = sem("lq_ready")
        lk_ready = sem("lk_ready")
        l_scored = sem("l_scored")
        l_masked = sem("l_masked")
        l_maxed = sem("l_maxed")
        l_exped = sem("l_exped")
        l_reced = sem("l_reced")
        gated = sem("gated")
        mixed = sem("mixed")
        p_loaded = sem("p_loaded")
        out_ready = sem("out_ready")
        out_stored = sem("out_stored")

        bias_dram = nc.dram_tensor("bias_scratch", (DA_H, SCORE), F32, kind="Internal").ap()
        bias_rep = nc.dram_tensor("bias_replicas", (P, DA_H, SCORE), F32, kind="Internal").ap()

        def own_order(eng, step):
            count = [0]

            def mark(ins):
                ins.then_inc(step, 1)
                count[0] += 1
                return count[0]

            def wait(n=None):
                eng.wait_ge(step, count[0] if n is None else n)
            return mark, wait

        def gain(name, c):
            i = GAIN[name] + c
            return gains[:, i:i + 1]

        def wait_group(eng, name):
            eng.wait_ge(unit_used, groups[name]["units"][-1][0] + 1)

        def group_ps(name):
            return pair[groups[name]["index"] % 2]

        def turn_bank(name):
            return turn_ps[:, turn[name]["index"] % 2, :]

        def wait_turn(eng, name):
            eng.wait_ge(turn_filled, turn[name]["index"] + 1)

        OPERAND = {"x0": (a_hi, a_lo, 0), "x2": (a_hi, a_lo, 0), "x5": (a_hi, a_lo, 0), "x7": (a_hi, a_lo, 0),
                   "oT": (o_hi, o_lo, 0), "yT": (y_hi, y_lo, 0), "latq": (lat_hi, lat_lo, 0),
                   "latkv": (lat_hi, lat_lo, Q_LORA // P), "roT": (b_hi, b_lo, 0), "moT": (a_hi, a_lo, 0),
                   "mixT": (b_hi, b_lo, 0), "pT": (p_hi, p_lo, 0)}
        SPLIT = {"x0": (a_hi, a_lo, "attn_norm", 0), "x1": (a_hi, a_lo, "mlp_norm", 0),
                 "x2": (a_hi, a_lo, "mlstm_norm", 0), "x3": (a_hi, a_lo, "mlp_norm", DC),
                 "x5": (a_hi, a_lo, "norm_mix_2", 0), "x6": (a_hi, a_lo, "norm_mlp_2", 0),
                 "x7": (a_hi, a_lo, "norm_ple_2", 0), "oT0": (o_hi, o_lo, "attn_subln", None),
                 "oT1": (o_hi, o_lo, "attn_subln", None), "yT": (y_hi, y_lo, "mlstm_head_norm", 0),
                 "lat": (lat_hi, lat_lo, "q_lat_norm_2", 0), "roT": (b_hi, b_lo, "ret_norm_2", 0),
                 "moT": (a_hi, a_lo, None, 0), "mixT": (b_hi, b_lo, None, 0), "pT": (p_hi, p_lo, None, 0)}

        def split_parts(name):
            base, c0 = name.split(".")
            hi, lo, g, at = SPLIT[base]
            c0 = int(c0)
            n = turn[name]["act_end"] - turn[name]["act"]
            for j in range(n):
                c = c0 + j + (4 if base == "oT1" else 0)
                scale = None if g is None else gain(g, 0 if at is None else at + c)
                yield turn_bank(name)[:, j * S:(j + 1) * S], hi[:, c, :], lo[:, c, :], scale

        def run_group(name, each, slots=None, part=slice(None)):
            for n, unit in list(enumerate(groups[name]["units"]))[part]:
                each(unit)
                if slots and n in slots:
                    slots[n]()

        def x_version(v, nblocks=4):
            return 4 * (v - 1) + nblocks

        block = ctx.enter_context(nc.Block())

        @block.sync
        def _(sp):
            for tt in range(TT):
                sp.dma_start(x[:, tt, :], w["x"][0, tt * P:(tt + 1) * P, :]).then_inc(x_loaded, 16)

            def load(k, src, chunks, ncols, it=None):
                if it is not None or k >= RAW:
                    used = k - RAW + 1
                    sp.wait_ge(lo_ready, used if it is None else it * RING + used)
                dst = raw[:, k % RAW, 0:chunks * ncols].rearrange("p (c n) -> p c n", n=ncols)
                sp.dma_start(dst, src).then_inc(landed[k % RAW], 16)

            def load_up(w1, k, i, it=None):
                cols = slice(i * HALF, (i + 1) * HALF) if it is None else bass.ds(it * HALF, HALF)
                rows = w1.rearrange("(c p) n -> p c n", p=P)
                for u in range(4):
                    load(k + u, rows[:, 2 * u:2 * u + 2, cols], 2, HALF, it)

            def load_down(w2, k, i, it=None):
                for u in range(4):
                    at = i * HALF + u * P if it is None else it * HALF + (u * P - HALF)
                    src = w2[at:at + P, :] if it is None else w2[bass.ds(at, P), :]
                    load(k + u, src.rearrange("p (c n) -> p c n", c=1), 1, D, it)

            for item in stream:
                if item[0] == "unit":
                    _, k, src, chunks, ncols = item
                    load(k, src, chunks, ncols)
                else:
                    _, k, w1, w2, _ = item
                    load_up(w1, k, 0)
                    with sp.Fori(1, FF // HALF) as i:
                        load_up(w1, k - 4, None, i)
                        load_down(w2, k, None, i)
                    load_down(w2, k + 60, FF // HALF - 1)
            for n in range(2):
                for tt in range(TT):
                    sp.wait_ge(out_ready, 2 * n + tt + 1)
                    sp.dma_start(out[0, tt * P:(tt + 1) * P, n * HALF:(n + 1) * HALF],
                                 gate[:, tt, n * HALF:(n + 1) * HALF]).then_inc(out_stored, 16)
            sp.wait_ge(out_stored, 64)

        @block.tensor
        def _(pe):
            seen = {"source": 0}
            next_turn = [0]

            def product(o, hi, lo, whi, wlo, start, stop):
                pe.matmul(o, hi, whi, start=start, stop=False)
                pe.matmul(o, hi, wlo, start=False, stop=False)
                return pe.matmul(o, lo, whi, start=False, stop=stop)

            def wait_source(source, c):
                name, j = turn_of(source, c)
                value = turn[name]["dve"] + j + 1
                if value > seen["source"]:
                    pe.wait_ge(turn_dve, value)
                    seen["source"] = value

            def open_turn(name):
                assert turn[name]["index"] == next_turn[0], name
                next_turn[0] += 1
                if turn[name]["index"] >= 2:
                    before = turn_list[turn[name]["index"] - 2]
                    if before["act_end"] > before["act"]:
                        pe.wait_ge(turn_act, before["act_end"])
                    if before["dve_end"] > before["dve"]:
                        pe.wait_ge(turn_dve, before["dve_end"])
                return turn_bank(name)

            def transposed(name, sources):
                bank = open_turn(name)
                for j, src in enumerate(sources):
                    last = pe.transpose(bank[:, j * P:(j + 1) * P], src, ident)
                last.then_inc(turn_filled, 1)

            def chunks_of(tile, c0, n):
                return [tile[:, tt, c * P:(c + 1) * P] for c in range(c0, c0 + n) for tt in range(TT)]

            def x_turn(v, c):
                if v == 0:
                    pe.wait_ge(x_loaded, 16 * TT)
                elif v == 5:
                    pe.wait_ge(gained_ready, 2 if c < 4 else 4)
                else:
                    pe.wait_ge(x_ready, x_version(v, 2 if c < 4 else 4))
                transposed(f"x{v}.{c}", chunks_of(gained if v == 5 else x, c, 2))

            def open_pair(name):
                i = groups[name]["index"]
                if i >= 2:
                    before = group_list[i - 2]
                    if before["act"]:
                        pe.wait_ge(group_act, before["act_end"])
                    if before["dve"]:
                        pe.wait_ge(group_dve, before["dve_end"])
                return group_ps(name)

            def dense(name, slots=None, part=slice(None)):
                g = groups[name]
                ps = group_ps(name) if part.start else open_pair(name)
                hi, lo, c_at = OPERAND[g["source"]]
                ncols, last_c = g["ncols"], g["units"][-1][1] + g["units"][-1][2] - 1

                def unit(u):
                    k, c0, n = u
                    wait_source(g["source"], c0 + n - 1)
                    pe.wait_ge(lo_ready, k + 1)
                    for tt in range(TT):
                        for j in range(n):
                            c = c0 + j
                            cols = slice(j * ncols, (j + 1) * ncols)
                            rows = slice(tt * P, (tt + 1) * P)
                            last = product(ps[:, tt, 0:ncols], hi[:, c_at + c, rows], lo[:, c_at + c, rows],
                                           w_hi[:, k % RING, cols], w_lo[:, k % RING, cols], c == 0, c == last_c)
                    last.then_inc(unit_used, 1)
                run_group(name, unit, slots, part)

            def mlp(m, source, slots, last_slots):
                k0 = mlps[m]
                steps = FF // HALF
                h0 = m * steps * TT

                def at(value, it, per):
                    return value if it is None else it * per + value

                def up(k, it=None):
                    for u in range(4):
                        if it is None:
                            wait_source(source, 2 * u + 1)
                        pe.wait_ge(lo_ready, at(k + u + 1, it, RING))
                        for tt in range(TT):
                            for j in range(2):
                                c = 2 * u + j
                                rows, cols = slice(tt * P, (tt + 1) * P), slice(j * HALF, (j + 1) * HALF)
                                slot = (k + u) % RING
                                last = product(pair[0][:, tt, :], a_hi[:, c, rows], a_lo[:, c, rows],
                                               w_hi[:, slot, cols], w_lo[:, slot, cols], c == 0, c == DC - 1)
                        last.then_inc(unit_used, 1)
                        if it is None and u in slots:
                            slots[u]()

                def turn_hidden(h, it=None):
                    for tt in range(TT):
                        pe.wait_ge(hid_ready, at(h + tt + 1, it, TT))
                        for c in range(HALF // P):
                            last = pe.transpose(turn_ps[:, tt, c * P:(c + 1) * P], hid[:, tt, c * P:(c + 1) * P], ident)
                        last.then_inc(hid_turned, 1)

                def down_last(k, h):
                    pe.wait_ge(lo_ready, k + 4)
                    for n in range(2):
                        cols = slice(n * HALF, (n + 1) * HALF)
                        for tt in range(TT):
                            rows = slice(tt * P, (tt + 1) * P)
                            if n == 0:
                                pe.wait_ge(hid_lo, h + tt + 1)
                            for u in range(4):
                                slot = (k + u) % RING
                                last = product(down[n][:, tt, :], h_hi[:, u, rows], h_lo[:, u, rows],
                                               w_hi[:, slot, cols], w_lo[:, slot, cols], False, u == 3)
                                if n == 1 and tt == 1:
                                    last.then_inc(unit_used, 1)
                            if n == 0 and tt == 1:
                                last.then_inc(down_half, 1)
                            if n == 1:
                                last_slots[tt]()

                def down_step(k, h, it=None):
                    pe.wait_ge(hid_lo, at(h + TT, it, TT))
                    for u in range(4):
                        pe.wait_ge(lo_ready, at(k + u + 1, it, RING))
                        for tt in range(TT):
                            rows = slice(tt * P, (tt + 1) * P)
                            for n in range(2):
                                cols = slice(n * HALF, (n + 1) * HALF)
                                slot = (k + u) % RING
                                last = product(down[n][:, tt, :], h_hi[:, u, rows], h_lo[:, u, rows],
                                               w_hi[:, slot, cols], w_lo[:, slot, cols], False, False)
                        last.then_inc(unit_used, 1)

                up(k0)
                for n in range(2):
                    for tt in range(TT):
                        pe.matmul(down[n][:, tt, :], zeros[:, 0:P], zeros[:, :], start=True, stop=False)
                turn_hidden(h0)
                with pe.Fori(1, steps) as i:
                    up(k0 - 4, i)
                    down_step(k0, h0 - TT, i)
                    turn_hidden(h0, i)
                down_last(k0 + 60, h0 + TT * (steps - 1))

            pe.wait_ge(const_loaded, 16)
            pe.wait_ge(gains_loaded, 16 * len(GAIN_ROWS))
            transposed("gains", [gain_rows[:, :]])
            pe.wait_ge(set_ready, 1)
            pe.wait_ge(small_loaded, 32)
            pe.matmul(score[0:DA_H, 0, 0:3 * P - 1], table[0:BUCKETS + 1, :], onehot[0:BUCKETS + 1, :],
                      start=True, stop=True).then_inc(bias_psum, 1)

            for c in range(0, DC, 2):
                x_turn(0, c)

            def qk_turns(name, n):
                pe.wait_ge(group_act, groups[name]["act_end"])
                for half in range(2):
                    cols = [qk_sb[:, n, tt, (2 * half + j) * P:(2 * half + j + 1) * P]
                            for j in range(2) for tt in range(TT)]
                    transposed(f"{name}{'ab'[half]}", cols)

            def da_score(h):
                if h == 0:
                    pe.wait_ge(bias_rows_ready, 1)
                else:
                    pe.wait_ge(da_biased, h)
                for name in ("q0b", "k0b") if h < 4 else ("q1b", "k1b"):
                    pe.wait_ge(turn_dve, turn[name]["dve_end"])
                for m in range(2):
                    rows = slice(DA_D * m, DA_D * (m + 1))
                    pe.matmul(score[:, m, WIDE], da_q[rows, h, P:S], da_k[rows, h, :], start=True, stop=True)
                    last = pe.matmul(score[:, m, TALL], da_q[rows, h, 0:P], da_k[rows, h, 0:P], start=True, stop=True)
                last.then_inc(da_scored, 1)

            def da_probs(h):
                pe.wait_ge(da_mixed, h + 1)
                transposed(f"ap{h}", [da_p[:, h, j * P:(j + 1) * P] for j in range(3)])

            def da_value(h):
                bank = open_turn(f"av{h}")
                pe.wait_ge(turn_act, turn[f"ap{h}"]["act_end"])
                pe.wait_ge(group_act, groups[f"v{h // 4}"]["act_end"])
                cols = slice(h * P, (h + 1) * P)
                pe.matmul(bank[:, 0:P], da_pt[:, h % 2, TALL], da_v[:, 0, cols], start=True, stop=True)
                pe.matmul(bank[:, P:2 * P], da_pt[:, h % 2, 0:P], da_v[:, 0, cols], start=True, stop=False)
                pe.matmul(bank[:, P:2 * P], da_pt[:, h % 2, P:2 * P], da_v[:, 1, cols], start=False, stop=True)\
                    .then_inc(turn_filled, 1)

            def da_out_turns(half):
                pe.wait_ge(da_scaled, 2 * (half + 1))
                for c in range(0, 4, 2):
                    transposed(f"oT{half}.{c}", chunks_of(da_o, 4 * half + c, 2))

            dense("q0")
            dense("k0")
            qk_turns("q0", 0)
            dense("q1", {1: lambda: qk_turns("k0", 1)})
            dense("k1", {n: (lambda n=n: da_score(n)) for n in range(4)})
            qk_turns("q1", 0)

            def v0_slot(n):
                if n == 1:
                    qk_turns("k1", 1)
                if n >= 2:
                    da_probs(n - 2)
                    da_score(n + 2)
            dense("v0", {n: (lambda n=n: v0_slot(n)) for n in range(4)})

            def v1_slot(n):
                if n < 2:
                    da_score(6 + n)
                da_value(n)
                da_probs(n + 2)
            dense("v1", {n: (lambda n=n: v1_slot(n)) for n in range(4)})
            da_out_turns(0)

            def ao0_slot(n):
                da_value(4 + n)
                da_probs(6 + n)
            first, second = slice(0, 2), slice(2, 4)
            dense("ao0", {n: (lambda n=n: ao0_slot(n)) for n in range(2)}, first)
            da_value(6)
            dense("ao1", {0: lambda: da_value(7)}, first)
            da_out_turns(1)
            dense("ao0", None, second)
            dense("ao1", {2: lambda: x_turn(1, 0), 3: lambda: x_turn(1, 2)}, second)
            mlp(0, "x1", {0: lambda: x_turn(1, 4), 1: lambda: x_turn(1, 6)},
                [lambda: x_turn(2, 0), lambda: x_turn(2, 2)])


            def cumulate():
                pe.wait_ge(ml_lf, 1)
                pe.matmul(score[:, 0, 0:ML_H], triu, g_lf[:, 0, :], start=True, stop=True)
                pe.matmul(score[:, 0, ML_H:2 * ML_H], ones, g_lf[:, 0, :], start=True, stop=False)
                pe.matmul(score[:, 0, ML_H:2 * ML_H], triu, g_lf[:, 1, :], start=False, stop=True).then_inc(ml_cum, 1)

            def spread(n):
                pe.wait_ge(ml_diag, n + 1)
                for j in range(2):
                    last = pe.matmul(score[:, j, :], ones, diag[:, 2 * j:2 * j + 2, :], start=True, stop=True)
                last.then_inc(ml_spread, 1)

            def conv_turn(b):
                pe.wait_ge(group_act, groups["mq" if b < 2 else "mk"]["act_end"])
                c0 = 2 * (b % 2)
                transposed(f"conv{b}", [ml_qk[:, b // 2, tt, c * P:(c + 1) * P]
                                        for c in (c0, c0 + 1) for tt in range(TT)])

            def ml_score(h):
                if h < 2:
                    pe.wait_ge(ml_wexp, ML_H)
                else:
                    pe.wait_ge(ml_weighted, h - 1)
                pe.wait_ge(ml_silu, 4)
                q, k = ml_t[:, h, :], ml_t[:, ML_H + h, :]
                pe.matmul(score[:, h % 2, WIDE], k[:, 0:P], q, start=True, stop=True)
                pe.matmul(score[:, h % 2, TALL], k[:, P:S], q[:, P:S], start=True, stop=True).then_inc(ml_scored, 1)

            def ml_value(h):
                pe.wait_ge(ml_weighted, h + 1)
                pe.wait_ge(ml_ones, 1)
                pe.wait_ge(group_act, groups["mv1"]["act_end"])
                bank = open_turn(f"mv{h}.0")
                pe.matmul(bank[:, 0:ML_V + 1], ml_s[:, h, 0:P], ml_v[:, 0, h, :], start=True, stop=True)\
                    .then_inc(turn_filled, 1)
                bank = open_turn(f"mv{h}.1")
                pe.matmul(bank[:, 0:ML_V + 1], ml_s[:, h, P:S], ml_v[:, 0, h, :], start=True, stop=False)
                pe.matmul(bank[:, 0:ML_V + 1], ml_s[:, h, TALL], ml_v[:, 1, h, :], start=False, stop=True)\
                    .then_inc(turn_filled, 1)

            dense("mq", {0: lambda: x_turn(2, 4), 1: lambda: x_turn(2, 6)}, first)
            dense("gate")
            dense("mq", {3: cumulate}, second)
            dense("mk", {1: lambda: spread(0), 2: lambda: conv_turn(0), 3: lambda: conv_turn(1)})
            dense("mv0", {0: lambda: spread(1), 1: lambda: conv_turn(2), 3: lambda: conv_turn(3)})
            dense("mv1")
            dense("mo0", {n: (lambda n=n: ml_score(n)) for n in range(4)})
            dense("mo1", {n: (lambda n=n: ml_value(n)) for n in range(4)})

            def y_turn(c):
                pe.wait_ge(ml_y, c + 2)
                transposed(f"yT.{c}", chunks_of(ml_o, c, 2))
            y_turn(0)
            y_turn(2)
            dense("mw0", None, first)
            dense("mw1", None, first)
            y_turn(4)
            y_turn(6)
            dense("mw0", None, second)
            dense("mw1", {2: lambda: x_turn(3, 0), 3: lambda: x_turn(3, 2)}, second)
            mlp(1, "x3", {0: lambda: x_turn(3, 4), 1: lambda: x_turn(3, 6)},
                [lambda: x_turn(5, 0), lambda: x_turn(5, 2)])


            def lat_turn(c, n):
                pe.wait_ge(group_act, groups["ckv"]["act_end"])
                transposed(f"lat.{c}", chunks_of(lat_sb, c, n))

            def ret_turn(name, half):
                pe.wait_ge(ret_roped, ("rq0", "rq1", "rk0", "rk1").index(name) + 1)
                transposed(f"{name}{'ab'[half]}", [work[:, 1, tt, (2 * half + j) * P:(2 * half + j + 1) * P]
                                                   for j in range(2) for tt in range(TT)])

            def ret_score(h):
                if h >= 2:
                    pe.wait_ge(ret_decayed, h - 1)
                pe.wait_ge(turn_dve, turn["rk1b"]["dve_end"])
                for j in range(2):
                    c = 2 * h + j
                    pe.matmul(score[:, h % 2, WIDE], rk_t[:, c, 0:P], rq_t[:, c, :], start=j == 0, stop=j == 1)
                for j in range(2):
                    c = 2 * h + j
                    last = pe.matmul(score[:, h % 2, TALL], rk_t[:, c, P:S], rq_t[:, c, P:S],
                                     start=j == 0, stop=j == 1)
                last.then_inc(ret_scored, 1)

            def ret_value(h):
                ps = open_pair(f"ret{h}")
                pe.wait_ge(ret_decayed, h + 1)
                pe.wait_ge(group_act, groups[f"rv{h}"]["act_end"])
                v = work[:, h % 2, :, :]
                pe.matmul(ps[:, 0, :], ret_s[:, h, 0:P], v[:, 0, :], start=True, stop=True)
                pe.matmul(ps[:, 1, :], ret_s[:, h, P:S], v[:, 0, :], start=True, stop=False)
                pe.matmul(ps[:, 1, :], ret_s[:, h, TALL], v[:, 1, :], start=False, stop=True).then_inc(ret_out, 1)

            def mla_turn(which, part, b):
                tile, ready = (lq_sb, lq_ready) if which == "mq" else (kv, lk_ready)
                pe.wait_ge(ready, 1 if (which, part) == ("mk", "n") else 2)
                if part == "n":
                    src = [tile[:, tt, 2 * b + j, 0:NOPE] for j in range(2) for tt in range(TT)]
                else:
                    src = [rot[:, tt, 4 * b + 2 * j:4 * b + 2 * j + 2, :] for j in range(2) for tt in range(TT)]
                transposed(f"{which}{part}{b}", src)

            def mla_score(h):
                if h >= 2:
                    pe.wait_ge(l_masked, h - 1)
                else:
                    pe.wait_ge(ret_decayed, RET_H)
                pe.wait_ge(turn_act, turn["mkn3"]["act_end"])
                pe.wait_ge(turn_dve, turn["mkr1"]["dve_end"])
                rows = slice(ROPE * (h % 2), ROPE * (h % 2 + 1))
                for cols, q, k in ((WIDE, slice(P, S), slice(0, S)), (TALL, slice(0, P), slice(0, P))):
                    o = score[:, h % 2, cols]
                    pe.matmul(o, lq_n[:, h, q], lk_n[:, h, k], start=True, stop=False)
                    last = pe.matmul(o, lq_t[rows, h // 2, q], lk_t[rows, h // 2, k], start=False, stop=True)
                last.then_inc(l_scored, 1)

            def mla_probs(h):
                pe.wait_ge(l_exped, h + 1)
                transposed(f"lp{h}", [l_e[:, h % 2, j * P:(j + 1) * P] for j in range(3)])

            def mla_value(h):
                bank = open_turn(f"lv{h}")
                pe.wait_ge(turn_act, turn[f"lp{h}"]["act_end"])
                v = [kv[:, tt, h, NOPE:] for tt in range(TT)]
                pe.matmul(bank[:, 0:P], l_pt[:, h % 2, TALL], v[0], start=True, stop=True)
                pe.matmul(bank[:, P:S], l_pt[:, h % 2, 0:P], v[0], start=True, stop=False)
                pe.matmul(bank[:, P:S], l_pt[:, h % 2, P:S], v[1], start=False, stop=True).then_inc(turn_filled, 1)

            def mla_slot(n):
                if n < MLA_H:
                    mla_score(n)
                if n >= 2:
                    mla_value(n - 2)
                if 1 <= n <= MLA_H:
                    mla_probs(n - 1)

            dense("cq", {0: lambda: x_turn(5, 4), 1: lambda: x_turn(5, 6)})
            dense("ckv")
            dense("rq0", {1: lambda: lat_turn(0, 2), 2: lambda: lat_turn(2, 2), 3: lambda: lat_turn(4, 1)})
            dense("rq1", {2: lambda: ret_turn("rq0", 0), 3: lambda: ret_turn("rq0", 1)})
            dense("rk0", {2: lambda: ret_turn("rq1", 0), 3: lambda: ret_turn("rq1", 1)})
            dense("rk1", {2: lambda: ret_turn("rk0", 0), 3: lambda: ret_turn("rk0", 1)})
            dense("uq0")
            dense("uq1", {1: lambda: ret_turn("rk1", 0)})
            dense("uq2", {1: lambda: ret_turn("rk1", 1)})
            for n in range(4):
                dense(f"ukv{n}")
                ret_score(n)
            dense("rv0")
            dense("rv1")
            ret_value(0)

            def turns_q(n):
                mla_turn("mq", "n", n)

            def turns_k(n):
                if n == 0:
                    mla_turn("mq", "r", 0)
                    mla_turn("mq", "r", 1)
                mla_turn("mk", "n", n)
            dense("rv2", {n: (lambda n=n: turns_q(n)) for n in range(4)})
            ret_value(1)
            dense("rv3", {n: (lambda n=n: turns_k(n)) for n in range(4)})
            ret_value(2)
            dense("rg0", {0: lambda: mla_turn("mk", "r", 0), 1: lambda: mla_turn("mk", "r", 1)})
            ret_value(3)
            dense("rg1", {n: (lambda n=n: mla_slot(n)) for n in range(4)})
            dense("rg2", {n: (lambda n=n: mla_slot(4 + n)) for n in range(4)})
            dense("rg3", {0: lambda: mla_slot(8), 1: lambda: mla_slot(9)})

            def ro_turn(c):
                pe.wait_ge(gated, c // 4 + 1)
                transposed(f"roT.{c}", chunks_of(ret, c, 2))
            dense("gm0", {n: (lambda n=n: ro_turn(2 * n)) for n in range(4)})
            dense("gm1", {n: (lambda n=n: ro_turn(8 + 2 * n)) for n in range(4)})
            dense("gr0")
            dense("gr1")

            def mo_turn(c):
                pe.wait_ge(turn_act, turn["lv7"]["act_end"])
                transposed(f"moT.{c}", chunks_of(lo_sb, c, 2))
            dense("br0", {2 * n + 1: (lambda n=n: mo_turn(2 * n)) for n in range(4)})
            dense("br1")
            dense("bm0")

            def mix_turn(c):
                pe.wait_ge(mixed, 2 * (c // 4) + 2)
                transposed(f"mixT.{c}", chunks_of(mix, c, 2))
            dense("bm1", {2: lambda: mix_turn(0), 3: lambda: mix_turn(2)})
            dense("wo0", {0: lambda: mix_turn(4), 1: lambda: mix_turn(6)})
            dense("wo1", {2: lambda: x_turn(6, 0), 3: lambda: x_turn(6, 2)})

            def p_turn():
                pe.wait_ge(p_loaded, 16 * TT)
                transposed("pT.0", chunks_of(p_sb, 0, 2))
            mlp(2, "x6", {0: lambda: x_turn(6, 4), 1: lambda: x_turn(6, 6), 3: p_turn},
                [lambda: x_turn(7, 0), lambda: x_turn(7, 2)])

            for n in range(2):
                pe.wait_ge(x_ready, x_version(7, 2))
                dense(f"pl{n}")
            dense("pg0", {0: lambda: x_turn(7, 4), 1: lambda: x_turn(7, 6)})
            dense("pg1")

        @block.scalar
        def _(act):
            mark, own = own_order(act, act_step)
            sizes = {item[1]: item[3] * item[4] for item in stream if item[0] == "unit"}
            split_to = [0]
            junk_free = [None]

            def square_sum(src, total, cols, done, value):
                if junk_free[0]:
                    act.wait_ge(*junk_free[0])
                junk_free[0] = (done, value)
                act.activation(junk[:, cols], src, ACT.Square, accum_out=total).then_inc(done, 1)

            def split_unit(k, it=None):
                if it is not None or k >= RING:
                    used = k - RING + 1
                    act.wait_ge(unit_used, used if it is None else it * RING + used)
                land = 16 * (k // RAW + 1)
                act.wait_ge(landed[k % RAW], land if it is None else it * (16 * RING // RAW) + land)
                n = sizes.get(k, UNIT) if it is None else UNIT
                act.activation(w_hi[:, k % RING, 0:n], raw[:, k % RAW, 0:n], ACT.Copy).then_inc(hi_ready, 1)

            def split_until(k):
                while split_to[0] <= min(k, total_units - 1):
                    split_unit(split_to[0])
                    split_to[0] += 1

            def split_turn(name):
                wait_turn(act, name)
                for src, hi, _, scale in split_parts(name):
                    if scale is None:
                        act.activation(hi, src, ACT.Copy).then_inc(turn_act, 1)
                    else:
                        act.activation(hi, src, ACT.Copy, scale=scale).then_inc(turn_act, 1)

            first, second = slice(0, 2), slice(2, 4)

            def x_squares(v):
                if v == 0:
                    act.wait_ge(x_loaded, 16 * TT)
                elif v == 5:
                    act.wait_ge(gained_ready, 4)
                else:
                    act.wait_ge(x_ready, x_version(v))
                for tt in range(TT):
                    square_sum((gained if v == 5 else x)[:, tt, :], ssx[:, v, tt:tt + 1], slice(0, D), x_squared, TT * v + tt + 1)

            def dense(name, slots=None, part=slice(None)):
                run_group(name, lambda u: split_until(u[0] + AHEAD), slots, part)

            def empty(name, outs, func=ACT.Copy, scales=None):
                wait_group(act, name)
                for tt in range(TT):
                    ps = group_ps(name)[:, tt, 0:groups[name]["ncols"]]
                    ps = ps if len(outs[tt].shape) == 2 else ps.rearrange("p (a b) -> p a b", a=outs[tt].shape[1])
                    if scales is None:
                        act.activation(outs[tt], ps, func).then_inc(group_act, 1)
                    else:
                        act.activation(outs[tt], ps, func, scale=scales[tt]).then_inc(group_act, 1)

            def row_norm(v):
                return [rstd[:, v, tt:tt + 1] for tt in range(TT)]

            def mlp(m, meanwhile=None):
                k0, steps = mlps[m], FF // HALF
                h0 = m * steps * TT

                def at(value, it, per):
                    return value if it is None else it * per + value

                def step(k, h, it=None):
                    act.wait_ge(unit_used, at(k + 4, it, RING))
                    for tt in range(TT):
                        act.activation(relu[:, tt, :], pair[0][:, tt, :], ACT.Relu).then_inc(up_relu, 1)
                    for u in range(4):
                        split_unit(k + 8 + u, it)
                    for tt in range(TT):
                        act.wait_ge(hid_turned, at(h + tt + 1, it, TT))
                        act.activation(h_hi[:, :, tt * P:(tt + 1) * P],
                                       turn_ps[:, tt, :].rearrange("p (c s) -> p c s", s=P), ACT.Copy)\
                            .then_inc(hid_hi, 1)

                def step_tail(k, it=None):
                    for u in range(4):
                        split_unit(k + 12 + u, it)

                split_until(k0 + 7)
                if meanwhile:
                    meanwhile()
                step(k0, h0)
                with act.Fori(1, steps - 1) as i:
                    step(k0 - 4, h0, i)
                    step_tail(k0 - 4, i)
                step(k0 + 4 + RING * (steps - 2), h0 + TT * (steps - 1))
                split_to[0] = k0 + 8 * steps

            act.dma_start(square[:, :, :], w["c_square"]).then_inc(const_loaded, 16)
            at = 0
            for name, rows in GAIN_ROWS:
                src = w[name].rearrange("a b -> (a b)") if len(w[name].shape) == 2 else \
                    w[name].rearrange("a b c -> (a b c)")
                src = src[0:rows * P].rearrange("(r p) -> r p", p=P)
                act.dma_start(gain_rows[at:at + rows, :], src).then_inc(gains_loaded, 16)
                at += rows
            act.wait_ge(lam_sum, 1)
            act.activation(lam_e[:, :], lam_s[:, :], ACT.Exp).then_inc(lam_exp, 1)
            wait_turn(act, "gains")
            act.activation(gains[:, :], turn_bank("gains")[:, 0:P], ACT.Copy).then_inc(turn_act, 1)
            act.wait_ge(turn_act, 1)
            for c in range(0, DC, 2):
                split_turn(f"x0.{c}")
                split_until(c // 2)
            x_squares(0)
            split_until(4)
            act.wait_ge(angles_ready, 1)
            act.activation(trig[:, :, :, :], ang[:, :, :, :], ACT.Sin).then_inc(trig_ready, 1)

            def da_exp(h):
                act.wait_ge(da_maxed, h + 1)
                b = h % 2
                for j, cols in enumerate((WIDE, TALL)):
                    for m in range(2):
                        i = 2 * j + m
                        last = act.activation(da_e[:, b, m, cols], da_e[:, b, m, cols], ACT.Exp,
                                              bias=da_nm[:, b, i:i + 1], accum_out=da_sum[:, b, i:i + 1])
                last.then_inc(da_exped, 1)

            def da_probs(h):
                wait_turn(act, f"ap{h}")
                act.activation(da_pt[:, h % 2, :], turn_bank(f"ap{h}")[:, 0:SCORE], ACT.Copy).then_inc(turn_act, 1)

            def da_value(h):
                wait_turn(act, f"av{h}")
                for tt in range(TT):
                    square_sum(turn_bank(f"av{h}")[:, tt * P:(tt + 1) * P], da_ss[:, h // 4, tt, h % 4:h % 4 + 1],
                               slice(0, P), turn_act, turn[f"av{h}"]["act"] + tt + 1)

            empty_qk = lambda name, n: empty(name, [qk_sb[:, n, tt, :] for tt in range(TT)], scales=row_norm(0))
            act.wait_ge(rstd_ready, 1)
            dense("q0")
            empty_qk("q0", 0)
            dense("k0")
            empty_qk("k0", 1)
            dense("q1")
            wait_turn(act, "q0b")
            empty_qk("q1", 0)
            dense("k1", {n: (lambda n=n: da_exp(n - 1)) for n in range(1, 4)})
            wait_turn(act, "k0b")
            empty_qk("k1", 1)
            dense("v0", {0: lambda: da_exp(3), 2: lambda: da_probs(0), 3: lambda: (da_exp(4), da_probs(1))})
            empty("v0", [da_v[:, tt, 0:HALF] for tt in range(TT)], scales=row_norm(0))

            def v1_slot(n):
                if n < 3:
                    da_exp(5 + n)
                da_value(n)
                da_probs(n + 2)
            dense("v1", {n: (lambda n=n: v1_slot(n)) for n in range(4)})
            empty("v1", [da_v[:, tt, HALF:D] for tt in range(TT)], scales=row_norm(0))
            split_turn("oT0.0")
            split_turn("oT0.2")

            def ao0_slot(n):
                da_value(4 + n)
                da_probs(6 + n)
            dense("ao0", {n: (lambda n=n: ao0_slot(n)) for n in range(2)}, first)
            da_value(6)
            dense("ao1", {0: lambda: da_value(7)}, first)
            split_turn("oT1.0")
            split_turn("oT1.2")
            dense("ao0", None, second)
            dense("ao1", {2: lambda: split_turn("x1.0"), 3: lambda: split_turn("x1.2")}, second)
            split_turn("x1.4")
            split_turn("x1.6")
            x_squares(1)
            mlp(0)

            split_until(groups["mq"]["units"][0][0] + 2)
            split_turn("x2.0")
            split_turn("x2.2")
            dense("mq", {0: lambda: split_turn("x2.4"), 1: lambda: split_turn("x2.6")}, first)
            x_squares(2)
            dense("gate")
            act.wait_ge(rstd_ready, 3)
            empty("gate", [gate_in[:, tt, :] for tt in range(TT)], scales=row_norm(2))

            def gate_log():
                act.wait_ge(ml_abs, 1)
                mark(act.activation(g_exp, g_abs, ACT.Exp, scale=-1.0))
                own()
                act.activation(g_ln, g_exp, ACT.Ln, bias=1.0).then_inc(ml_ln, 1)

            def weights():
                act.wait_ge(ml_args, 2)
                for h in range(ML_H):
                    g0, g1 = g_g[:, 0, h:h + 1], g_g[:, 1, h:h + 1]
                    spread = score[:, h // 2, :].rearrange("p (h s) -> p h s", h=2)[:, h % 2, :]
                    act.activation(ml_w[:, h, 0:P], ml_w[:, h, 0:P], ACT.Exp, bias=g0)
                    act.activation(ml_w[:, h, P:S], spread[:, P:S], ACT.Exp, bias=g0, scale=-1.0)
                    act.activation(ml_w[:, h, TALL], ml_w[:, h, TALL], ACT.Exp, bias=g1).then_inc(ml_wexp, 1)
                act.activation(g_em, g_nm, ACT.Exp, scale=-1.0).then_inc(ml_em, 1)

            def convolve(b):
                wait_turn(act, f"conv{b}")
                for j in range(2):
                    c = 2 * b + j
                    act.activation(ml_t[:, c, :], turn_bank(f"conv{b}")[:, j * S:(j + 1) * S], ACT.Identity,
                                   scale=gain("mlstm_conv_w", (CONV - 1) * DC + c), bias=gain("mlstm_conv_b", c))\
                        .then_inc(turn_act, 1)

            def silu(b):
                act.wait_ge(turn_dve, turn[f"conv{b}"]["dve_end"])
                two = ml_t[:, 2 * b:2 * b + 2, :]
                act.activation(two, two, ACT.Silu).then_inc(ml_silu, 1)

            def ml_square(h):
                for tt in range(TT):
                    name = f"mv{h}.{tt}"
                    wait_turn(act, name)
                    act.activation(ml_n[:, tt, h, :], turn_bank(name)[:, 0:ML_V + 1], ACT.Copy).then_inc(turn_act, 1)
                    square_sum(turn_bank(name)[:, 0:ML_V], r_ss[:, tt, h:h + 1], slice(0, ML_V), turn_act,
                               turn[name]["act_end"])

            dense("mq", {2: gate_log}, second)
            empty("mq", [ml_qk[:, 0, tt, :] for tt in range(TT)], scales=row_norm(2))
            dense("mk", {2: lambda: convolve(0), 3: lambda: convolve(1)})
            empty("mk", [ml_qk[:, 1, tt, :] for tt in range(TT)], scales=row_norm(2))
            dense("mv0", {1: lambda: (convolve(2), weights()), 3: lambda: (convolve(3), silu(0), silu(1))})
            act.wait_ge(ml_ones, 1)
            half_v = lambda n: [ml_v[:, tt, 2 * n:2 * n + 2, 0:ML_V] for tt in range(TT)]
            empty("mv0", half_v(0), scales=row_norm(2))
            dense("mv1", {0: lambda: silu(2), 1: lambda: silu(3)})
            empty("mv1", half_v(1), scales=row_norm(2))
            dense("mo0")
            empty("mo0", [ml_o[:, tt, 0:HALF] for tt in range(TT)], ACT.Sigmoid, row_norm(2))
            dense("mo1", {n: (lambda n=n: ml_square(n)) for n in range(4)})
            empty("mo1", [ml_o[:, tt, HALF:D] for tt in range(TT)], ACT.Sigmoid, row_norm(2))
            split_turn("yT.0")
            split_turn("yT.2")
            dense("mw0", None, first)
            dense("mw1", None, first)
            split_turn("yT.4")
            split_turn("yT.6")
            dense("mw0", None, second)
            dense("mw1", {2: lambda: split_turn("x3.0"), 3: lambda: split_turn("x3.2")}, second)
            split_turn("x3.4")
            split_turn("x3.6")
            x_squares(3)
            mlp(1)

            split_until(groups["cq"]["units"][0][0] + 3)
            split_turn("x5.0")
            split_turn("x5.2")
            dense("cq", {0: lambda: split_turn("x5.4"), 1: lambda: split_turn("x5.6"), 2: lambda: x_squares(4)})
            x_squares(5)
            act.wait_ge(rstd_ready, 6)
            empty("cq", [lat_sb[:, tt, 0:Q_LORA] for tt in range(TT)], scales=row_norm(5))
            dense("ckv")
            empty("ckv", [lat_sb[:, tt, Q_LORA:] for tt in range(TT)], scales=row_norm(5))

            def lat_squares():
                act.wait_ge(group_act, groups["ckv"]["act_end"])
                for tt in range(TT):
                    for n, cols in enumerate((slice(0, Q_LORA), slice(Q_LORA, LAT))):
                        square_sum(lat_sb[:, tt, cols], lat_ss[:, n, tt:tt + 1], cols, lat_sq, 2 * tt + n + 1)

            def empty_rope(name):
                n = ("rq0", "rq1", "rk0", "rk1").index(name)
                if n:
                    act.wait_ge(ret_roped, n)
                empty(name, [work[:, 0, tt, :] for tt in range(TT)], scales=row_norm(5))

            def mla_copy(which, b):
                name = f"{which}n{b}"
                wait_turn(act, name)
                dst = (lq_n if which == "mq" else lk_n)[:, 2 * b:2 * b + 2, :]
                act.activation(dst, turn_bank(name).rearrange("p (h s) -> p h s", h=2), ACT.Copy,
                               scale=gain("q_norm_2" if which == "mq" else "k_norm_2", 0)).then_inc(turn_act, 1)

            def ret_squares(h):
                act.wait_ge(ret_out, h + 1)
                ps = group_ps(f"ret{h}")
                for tt in range(TT):
                    square_sum(ps[:, tt, :], ret_ss[:, tt, h:h + 1], slice(0, HALF), group_act,
                               groups[f"ret{h}"]["act_end"] - 1 + tt)

            def mla_exp(h):
                act.wait_ge(l_maxed, h + 1)
                b = h % 2
                for j, cols in enumerate((WIDE, TALL)):
                    last = act.activation(l_e[:, b, cols], l_e[:, b, cols], ACT.Exp, bias=l_nm[:, b, j:j + 1],
                                          accum_out=l_sum[:, b, j:j + 1])
                last.then_inc(l_exped, 1)

            def mla_probs(h):
                wait_turn(act, f"lp{h}")
                act.activation(l_pt[:, h % 2, :], turn_bank(f"lp{h}")[:, 0:SCORE], ACT.Copy).then_inc(turn_act, 1)

            def mla_value(h):
                wait_turn(act, f"lv{h}")
                act.wait_ge(l_reced, h + 1)
                for tt in range(TT):
                    act.activation(lo_sb[:, tt, h * P:(h + 1) * P], turn_bank(f"lv{h}")[:, tt * P:(tt + 1) * P],
                                   ACT.Copy, scale=l_rec[:, h % 2, 1 - tt:2 - tt]).then_inc(turn_act, 1)

            def mla_slot(n):
                if 1 <= n <= MLA_H:
                    mla_exp(n - 1)
                if n >= 2:
                    mla_value(n - 2)
                if 1 <= n <= MLA_H:
                    mla_probs(n - 1)

            dense("rq0", {0: lat_squares, 1: lambda: split_turn("lat.0"), 2: lambda: split_turn("lat.2"),
                          3: lambda: split_turn("lat.4")})
            empty_rope("rq0")
            dense("rq1")
            empty_rope("rq1")
            dense("rk0")
            empty_rope("rk0")
            dense("rk1")
            empty_rope("rk1")
            act.wait_ge(lat_norm, 1)
            for n in range(3):
                dense(f"uq{n}")
                empty(f"uq{n}", [flat_q[:, tt * MLA_H * MLA_QK + n * HALF:tt * MLA_H * MLA_QK + (n + 1) * HALF]
                                 for tt in range(TT)], scales=[lat_r[:, 0, tt:tt + 1] for tt in range(TT)])
            for n in range(4):
                dense(f"ukv{n}")
                empty(f"ukv{n}", [kv[:, tt, 2 * n:2 * n + 2, :] for tt in range(TT)],
                      scales=[lat_r[:, 1, tt:tt + 1] for tt in range(TT)])

            def empty_value(n):
                if n == 0:
                    wait_turn(act, "rk1b")
                elif n >= 2:
                    act.wait_ge(ret_out, n - 1)
                else:
                    wait_turn(act, "rk1b")
                empty(f"rv{n}", [work[:, n % 2, tt, :] for tt in range(TT)], scales=row_norm(5))

            def empty_gate(n):
                act.wait_ge(ret_out, 3 if n == 0 else 4)
                if n >= 2:
                    act.wait_ge(gated, n - 1)
                empty(f"rg{n}", [work[:, n % 2, tt, :] for tt in range(TT)], ACT.Silu, row_norm(5))

            dense("rv0")
            empty_value(0)
            dense("rv1")
            empty_value(1)
            ret_squares(0)

            dense("rv2", {n: (lambda n=n: mla_copy("mq", n)) for n in range(4)})
            empty_value(2)
            ret_squares(1)
            dense("rv3", {n: (lambda n=n: mla_copy("mk", n)) for n in range(4)})
            empty_value(3)
            ret_squares(2)
            dense("rg0")
            empty_gate(0)
            ret_squares(3)
            dense("rg1", {n: (lambda n=n: mla_slot(n)) for n in range(4)})
            empty_gate(1)
            dense("rg2", {n: (lambda n=n: mla_slot(4 + n)) for n in range(4)})
            empty_gate(2)
            dense("rg3", {0: lambda: mla_slot(8), 1: lambda: mla_slot(9)})
            empty_gate(3)
            dense("gm0", {n: (lambda n=n: split_turn(f"roT.{2 * n}")) for n in range(4)})
            empty("gm0", [gm[:, tt, 0:HALF] for tt in range(TT)], ACT.Sigmoid, row_norm(5))
            dense("gm1", {n: (lambda n=n: split_turn(f"roT.{8 + 2 * n}")) for n in range(4)})
            empty("gm1", [gm[:, tt, HALF:D] for tt in range(TT)], ACT.Sigmoid, row_norm(5))
            dense("gr0")
            empty("gr0", [gr[:, tt, 0:HALF] for tt in range(TT)], ACT.Sigmoid, row_norm(5))
            dense("gr1")
            empty("gr1", [gr[:, tt, HALF:D] for tt in range(TT)], ACT.Sigmoid, row_norm(5))
            dense("br0", {2 * n + 1: (lambda n=n: split_turn(f"moT.{2 * n}")) for n in range(4)})
            dense("br1")
            dense("bm0")
            dense("bm1", {2: lambda: split_turn("mixT.0"), 3: lambda: split_turn("mixT.2")})
            dense("wo0", {0: lambda: split_turn("mixT.4"), 1: lambda: split_turn("mixT.6")})
            dense("wo1", {2: lambda: split_turn("x6.0"), 3: lambda: split_turn("x6.2")})
            split_turn("x6.4")
            split_turn("x6.6")
            x_squares(6)
            mlp(2, lambda: split_turn("pT.0"))

            split_until(groups["pl0"]["units"][0][0] + 3)
            split_turn("x7.0")
            split_turn("x7.2")
            for n in range(2):
                cols = slice(n * HALF, (n + 1) * HALF)
                dense(f"pl{n}")
                empty(f"pl{n}", [ple[:, tt, cols] for tt in range(TT)])
            for n in range(2):
                cols = slice(n * HALF, (n + 1) * HALF)
                if n == 0:
                    dense("pg0", {0: lambda: split_turn("x7.4"), 1: lambda: split_turn("x7.6"), 2: lambda: x_squares(7)})
                    act.wait_ge(rstd_ready, 8)
                else:
                    dense("pg1")
                empty(f"pg{n}", [gate[:, tt, cols] for tt in range(TT)], ACT.Sigmoid, row_norm(7))

        @block.vector
        def _(dve):
            mark, own = own_order(dve, dve_step)
            sizes = {item[1]: item[3] * item[4] for item in stream if item[0] == "unit"}
            split_to = [0]

            def split_unit(k, it=None):
                dve.wait_ge(hi_ready, k + 1 if it is None else it * RING + (k + 1))
                n = sizes.get(k, UNIT) if it is None else UNIT
                dve.tensor_tensor(w_lo[:, k % RING, 0:n], raw[:, k % RAW, 0:n], w_hi[:, k % RING, 0:n],
                                  ALU.subtract).then_inc(lo_ready, 1)

            def split_until(k):
                while split_to[0] <= min(k, total_units - 1):
                    split_unit(split_to[0])
                    split_to[0] += 1

            def dense(name, slots=None, part=slice(None)):
                run_group(name, lambda u: split_until(u[0] + AHEAD), slots, part)

            def split_turn(name):
                dve.wait_ge(turn_act, turn[name]["act_end"])
                for src, hi, lo, scale in split_parts(name):
                    if scale is None:
                        dve.tensor_tensor(lo, src, hi, ALU.subtract).then_inc(turn_dve, 1)
                    else:
                        dve.scalar_tensor_tensor(lo, src, scale, hi.bitcast(F32), ALU.mult, ALU.subtract)\
                            .then_inc(turn_dve, 1)

            def copy_turn(name, dst, src):
                if turn[name]["act_end"] > turn[name]["act"]:
                    dve.wait_ge(turn_act, turn[name]["act_end"])
                else:
                    wait_turn(dve, name)
                dve.tensor_copy(dst, src).then_inc(turn_dve, 1)

            def invert(v):
                dve.wait_ge(rstd_ready, v + 1)
                dve.reciprocal(inv_ms[:, v, :], msx[:, v, :]).then_inc(inv_ready, 1)

            first, second = slice(0, 2), slice(2, 4)

            def mlp(m, v, meanwhile=None):
                k0, steps = mlps[m], FF // HALF
                h0 = m * steps * TT

                def at(value, it, per):
                    return value if it is None else it * per + value

                def step(k, h, it=None):
                    for tt in range(TT):
                        dve.wait_ge(up_relu, at(h + tt + 1, it, TT))
                        dve.scalar_tensor_tensor(hid[:, tt, :], pair[0][:, tt, :], 0.0, relu[:, tt, :],
                                                 ALU.max, ALU.mult).then_inc(hid_ready, 1)
                    for u in range(4):
                        split_unit(k + 8 + u, it)
                    for tt in range(TT):
                        dve.wait_ge(hid_hi, at(h + tt + 1, it, TT))
                        rows = slice(tt * P, (tt + 1) * P)
                        dve.tensor_tensor(h_lo[:, :, rows], turn_ps[:, tt, :].rearrange("p (c s) -> p c s", s=P),
                                          h_hi[:, :, rows], ALU.subtract).then_inc(hid_lo, 1)

                def step_tail(k, it=None):
                    for u in range(4):
                        split_unit(k + 12 + u, it)

                split_until(k0 + 7)
                if meanwhile:
                    meanwhile()
                invert(v)
                step(k0, h0)
                with dve.Fori(1, steps - 1) as i:
                    step(k0 - 4, h0, i)
                    step_tail(k0 - 4, i)
                step(k0 + 4 + RING * (steps - 2), h0 + TT * (steps - 1))
                split_to[0] = k0 + 8 * steps
                split_until(k0 + 8 * steps + 2)
                dve.wait_ge(inv_ready, m + 1)

            def mlp_out(m, v, n):
                if n == 0:
                    dve.wait_ge(down_half, m + 1)
                else:
                    dve.wait_ge(unit_used, mlps[m] + 8 * (FF // HALF))
                cols = slice(n * HALF, (n + 1) * HALF)
                for tt in range(TT):
                    dve.scalar_tensor_tensor(x[:, tt, cols], down[n][:, tt, :], inv_ms[:, v, tt:tt + 1],
                                             x[:, tt, cols], ALU.mult, ALU.add).then_inc(x_ready, 1)

            def mlp_end(m, v, turns_of):
                for n in range(2):
                    mlp_out(m, v, n)
                    if n == 0:
                        split_turn(f"{turns_of}.0")
                        split_turn(f"{turns_of}.2")

            def add_to_x(name, n):
                wait_group(dve, name)
                cols = slice(n * HALF, (n + 1) * HALF)
                for tt in range(TT):
                    dve.tensor_tensor(x[:, tt, cols], x[:, tt, cols], group_ps(name)[:, tt, :], ALU.add)\
                        .then_inc(x_ready, 1)

            def rotate(o1, o2, t1, t2, x1, x2, cos, sin):
                mark(dve.tensor_tensor(o1, x1, cos, ALU.mult))
                n = mark(dve.tensor_tensor(t1, x2, sin, ALU.mult))
                mark(dve.tensor_tensor(o2, x2, cos, ALU.mult))
                mark(dve.tensor_tensor(t2, x1, sin, ALU.mult))
                own(n)
                mark(dve.tensor_tensor(o1, o1, t1, ALU.subtract))
                own()
                return dve.tensor_tensor(o2, o2, t2, ALU.add)

            def spread_to(ap, axis, shape):
                return ap.unsqueeze(axis).to_broadcast([P, *shape])

            dve.wait_ge(lam_loaded, 64)
            mark(dve.tensor_tensor(lam_prod[:, :, :], lam_in[:, 0::2, :], lam_in[:, 1::2, :], ALU.mult))
            own()
            dve.tensor_reduce(lam_s[:, :], lam_prod[:, :, :], AXIS, ALU.add).then_inc(lam_sum, 1)
            dve.wait_ge(bias_psum, 1)
            dve.tensor_copy(bias_rows[0:DA_H, :], score[0:DA_H, 0, 0:3 * P - 1]).then_inc(bias_rows_ready, 1)
            dve.wait_ge(lam_exp, 1)
            mark(dve.scalar_tensor_tensor(neg_lam[:, :], lam_e[:, 1:2], LAMBDA_INIT, lam_e[:, 0:1],
                                          ALU.subtract, ALU.subtract))
            for c in range(0, DC, 2):
                split_turn(f"x0.{c}")
                split_until(c // 2)
            dve.wait_ge(pos_loaded, 32)
            mark(dve.tensor_copy(pos_f[:, :], pos_i[:, :]))
            own()
            for a in range(2):
                for tt in range(TT):
                    mark(dve.tensor_scalar(ang[:, a, tt, :], inv[:, :], pos_f[:, tt:tt + 1], None, ALU.mult))
            own()
            for a in range(2):
                mark(dve.tensor_scalar(turns_k[:, a, :, :], ang[:, a, :, :], 1 / TWO_PI, 0.25 * a, ALU.mult, ALU.add))
            for step in (ROUND, -ROUND):
                own()
                mark(dve.tensor_scalar(turns_k[:, :, :, :], turns_k[:, :, :, :], step, None, ALU.add))
            split_until(4)
            k_flat = turns_k[:, :, :, :].rearrange("p a t n -> p (a t n)")
            a_flat = ang[:, :, :, :].rearrange("p a t n -> p (a t n)")
            for part in (PI_A, PI_B, PI_C):
                own()
                mark(dve.scalar_tensor_tensor(a_flat, k_flat, -part, a_flat, ALU.mult, ALU.add))
            own()
            mark(dve.tensor_scalar(ang[:, 1, :, :], ang[:, 1, :, :], TWO_PI / 4, None, ALU.add))
            own()
            dve.tensor_scalar(a_flat, a_flat, PI_SAFE, -PI_SAFE, ALU.min, ALU.max).then_inc(angles_ready, 1)

            def da_logits(h):
                dve.wait_ge(da_scored, h + 1)
                b = h % 2
                if h >= 2:
                    dve.wait_ge(da_mixed, h - 1)
                dve.scalar_tensor_tensor(da_e[:, b, :, :], score[:, :, 0:SCORE], DA_D ** -0.5,
                                         spread_to(bias[:, h, :], 1, [2, SCORE]), ALU.mult, ALU.add)\
                    .then_inc(da_biased, 1)
                dve.wait_ge(da_biased, h + 1)
                for j, cols in enumerate((WIDE, TALL)):
                    last = dve.tensor_reduce(da_nm[:, b, 2 * j:2 * j + 2], da_e[:, b, :, cols], AXIS, ALU.max,
                                             negate=True)
                last.then_inc(da_maxed, 1)

            def da_mix(h):
                dve.wait_ge(da_exped, h + 1)
                b = h % 2
                mark(dve.reciprocal(da_rec[:, b, :], da_sum[:, b, :]))
                own()
                mark(dve.tensor_scalar(da_nl[:, b, :], da_rec[:, b, 1::2], neg_lam[:, 0:1], None, ALU.mult))
                own()
                for j, cols in enumerate((WIDE, TALL)):
                    mark(dve.tensor_scalar(da_e[:, b, 1, cols], da_e[:, b, 1, cols], da_nl[:, b, j:j + 1], None,
                                           ALU.mult))
                own()
                for j, cols in enumerate((WIDE, TALL)):
                    last = dve.scalar_tensor_tensor(da_p[:, h, cols], da_e[:, b, 0, cols],
                                                    da_rec[:, b, 2 * j:2 * j + 1], da_e[:, b, 1, cols],
                                                    ALU.mult, ALU.add)
                last.then_inc(da_mixed, 1)

            def da_value(h):
                copy_turn(f"av{h}", da_o[:, :, h * P:(h + 1) * P],
                          turn_bank(f"av{h}")[:, 0:2 * P].rearrange("p (t d) -> p t d", t=TT))

            def da_scale(half):
                dve.wait_ge(da_norm, half + 1)
                dve.wait_ge(turn_dve, turn[f"av{4 * half + 3}"]["dve_end"])
                for tt in range(TT):
                    o = da_o[:, tt, half * HALF:(half + 1) * HALF].rearrange("p (h d) -> p h d", d=P)
                    dve.tensor_tensor(o, o, spread_to(da_r[:, half, tt, :], 2, [4, P]), ALU.mult)\
                        .then_inc(da_scaled, 1)

            def copy_heads(name, dst, h0):
                for half in range(2):
                    turn_name = f"{name}{'ab'[half]}"
                    copy_turn(turn_name, dst[:, h0 + 2 * half:h0 + 2 * half + 2, :],
                              turn_bank(turn_name).rearrange("p (h s) -> p h s", h=2))

            dense("q0")
            dense("k0")
            copy_heads("q0", da_q, 0)
            dense("q1", {1: lambda: copy_heads("k0", da_k, 0)})
            dve.wait_ge(bias_loaded, 32)

            def k1_slot(n):
                da_logits(n)
                if n:
                    da_mix(n - 1)
            dense("k1", {n: (lambda n=n: k1_slot(n)) for n in range(4)})
            copy_heads("q1", da_q, 4)
            dense("v0", {0: lambda: da_mix(3), 1: lambda: copy_heads("k1", da_k, 4), 2: lambda: da_logits(4),
                         3: lambda: (da_logits(5), da_mix(4))})

            def v1_slot(n):
                if n < 2:
                    da_logits(6 + n)
                da_value(n)
                if n < 3:
                    da_mix(5 + n)
            dense("v1", {n: (lambda n=n: v1_slot(n)) for n in range(4)})
            da_scale(0)
            split_turn("oT0.0")
            split_turn("oT0.2")
            dense("ao0", {n: (lambda n=n: da_value(4 + n)) for n in range(2)}, first)
            da_value(6)
            dense("ao1", {0: lambda: da_value(7)}, first)
            da_scale(1)
            split_turn("oT1.0")
            split_turn("oT1.2")
            dense("ao0", None, second)
            add_to_x("ao0", 0)
            dense("ao1", {2: lambda: split_turn("x1.0"), 3: lambda: split_turn("x1.2")}, second)
            add_to_x("ao1", 1)
            split_turn("x1.4")
            split_turn("x1.6")
            mlp(0, 1)
            mlp_end(0, 1, "x2")

            def ml_gates():
                dve.wait_ge(group_act, groups["gate"]["act_end"])
                dve.wait_ge(ml_loaded, 32)
                mark(dve.tensor_tensor(g_i, gate_in[:, :, 0:ML_H], spread_to(gate_b[:, 0:ML_H], 1, [TT, ML_H]), ALU.add))
                mark(dve.tensor_tensor(g_fz, gate_in[:, :, ML_H:], spread_to(gate_b[:, ML_H:], 1, [TT, ML_H]), ALU.add))
                own()
                mark(dve.tensor_scalar(g_nfz, g_fz, -1.0, None, ALU.mult))
                own()
                dve.tensor_tensor(g_abs, g_fz, g_nfz, ALU.max).then_inc(ml_abs, 1)

            def ml_log_forget():
                dve.wait_ge(ml_ln, 1)
                last = None
                for tt in range(TT):
                    last = dve.scalar_tensor_tensor(g_lf[:, tt, :], g_fz[:, tt, :], 0.0, g_ln[:, tt, :],
                                                    ALU.min, ALU.subtract)
                last.then_inc(ml_lf, 1)

            def diagonals(values):
                for h in range(ML_H):
                    for tt in range(TT):
                        last = dve.tensor_scalar(diag[:, h, tt * P:(tt + 1) * P], ident, values[:, tt, h:h + 1], None,
                                                 ALU.mult)
                last.then_inc(ml_diag, 1)

            def ml_cumulated():
                dve.wait_ge(ml_cum, 1)
                mark(dve.tensor_copy(g_F, score[:, 0, 0:2 * ML_H].rearrange("p (t h) -> p t h", t=TT)))
                own()
                mark(dve.tensor_tensor(g_g, g_i, g_F, ALU.subtract))
                own()
                diagonals(g_g)

            spread = score[:, :, :].rearrange("p b (h s) -> p (b h) s", h=2)

            def ml_maxima():
                dve.wait_ge(ml_spread, 1)
                for tt in range(TT):
                    mark(dve.tensor_tensor(maxed[:, :, :], spread[:, :, tt * P:(tt + 1) * P],
                                           spread_to(causal, 1, [ML_H, P]), ALU.add))
                    own()
                    mark(dve.tensor_reduce(g_max[:, tt, :], maxed[:, :, :], AXIS, ALU.max))
                    own()
                mark(dve.tensor_reduce(g_max2[:, 1, :], spread[:, :, 0:P], AXIS, ALU.max))
                own()
                mark(dve.tensor_tensor(g_max[:, 1, :], g_max[:, 1, :], g_max2[:, 1, :], ALU.max))
                own()
                mark(dve.tensor_scalar(g_max, g_max, 0.0, None, ALU.max))
                own()
                mark(dve.tensor_tensor(g_nm, g_F, g_max, ALU.add))
                diagonals(g_max)

            def ml_arguments():
                dve.wait_ge(ml_spread, 2)
                for src, dst in ((slice(0, P), slice(0, P)), (slice(P, S), TALL)):
                    dve.tensor_tensor(ml_w[:, :, dst], spread_to(causal_t, 1, [ML_H, P]), spread[:, :, src],
                                      ALU.subtract).then_inc(ml_args, 1)

            def convolve(b):
                name = f"conv{b}"
                dve.wait_ge(turn_act, turn[name]["act_end"])
                done = [0, 0]
                for shift in range(1, CONV):
                    for j in range(2):
                        c = 2 * b + j
                        tap = gain("mlstm_conv_w", (CONV - 1 - shift) * DC + c)
                        src = turn_bank(name)[:, j * S:(j + 1) * S - shift]
                        dst = ml_t[:, c, shift:]
                        if shift > 1:
                            own(done[j])
                        ins = dve.scalar_tensor_tensor(dst, src, tap, dst, ALU.mult, ALU.add)
                        if shift == CONV - 1 and j == 1:
                            ins.then_inc(turn_dve, 1)
                        else:
                            done[j] = mark(ins)

            def ml_weigh(h):
                dve.wait_ge(ml_scored, h + 1)
                dve.wait_ge(ml_wexp, h + 1)
                dve.scalar_tensor_tensor(ml_s[:, h, :], score[:, h % 2, 0:SCORE], ML_QK ** -0.5, ml_w[:, h, :],
                                         ALU.mult, ALU.mult).then_inc(ml_weighted, 1)

            def ml_denominators(half):
                two = slice(2 * half, 2 * half + 2)
                dve.wait_ge(turn_act, turn[f"mv{2 * half + 1}.1"]["act_end"])
                dve.wait_ge(ml_em, 1)
                den = ml_n[:, :, two, ML_V]
                mark(dve.scalar_tensor_tensor(r_abs[:, :, two], den, -1.0, den, ALU.mult, ALU.max))
                own()
                mark(dve.tensor_tensor(r_dmax[:, :, two], r_abs[:, :, two], g_em[:, :, two], ALU.max))
                own()
                mark(dve.reciprocal(r_dinv[:, :, two], r_dmax[:, :, two]))
                own()
                mark(dve.tensor_tensor(r_t[:, :, two], r_ss[:, :, two], r_dinv[:, :, two], ALU.mult))
                own()
                dve.tensor_tensor(r_ms[:, :, two], r_t[:, :, two], r_dinv[:, :, two], ALU.mult).then_inc(ml_ms, 1)

            def ml_finish(half):
                two = slice(2 * half, 2 * half + 2)
                dve.wait_ge(ml_norm, half + 1)
                mark(dve.tensor_tensor(r_sc[:, :, two], r_dinv[:, :, two], r_r[:, :, two], ALU.mult))
                own()
                dve.wait_ge(group_act, groups[f"mo{half}"]["act_end"])
                for h in range(2 * half, 2 * half + 2):
                    cols = slice(h * ML_V, (h + 1) * ML_V)
                    for tt in range(TT):
                        dve.scalar_tensor_tensor(ml_o[:, tt, cols], ml_n[:, tt, h, 0:ML_V], r_sc[:, tt, h:h + 1],
                                                 ml_o[:, tt, cols], ALU.mult, ALU.mult).then_inc(ml_y, 1)

            dense("mq", {0: lambda: split_turn("x2.4"), 1: lambda: split_turn("x2.6")}, first)
            dense("gate")
            ml_gates()
            dense("mq", {2: ml_log_forget}, second)
            dense("mk", {0: ml_cumulated, 1: ml_maxima, 2: lambda: convolve(0), 3: lambda: convolve(1)})
            dense("mv0", {0: ml_arguments, 1: lambda: convolve(2), 3: lambda: convolve(3)})
            dense("mv1")
            dense("mo0", {n: (lambda n=n: ml_weigh(n)) for n in range(4)})
            dense("mo1", {2: lambda: ml_denominators(0), 3: lambda: ml_finish(0)})
            ml_denominators(1)
            split_turn("yT.0")
            split_turn("yT.2")
            dense("mw0", None, first)
            ml_finish(1)
            dense("mw1", None, first)
            split_turn("yT.4")
            split_turn("yT.6")
            dense("mw0", None, second)
            add_to_x("mw0", 0)
            dense("mw1", {2: lambda: split_turn("x3.0"), 3: lambda: split_turn("x3.2")}, second)
            add_to_x("mw1", 1)
            split_turn("x3.4")
            split_turn("x3.6")
            mlp(1, 3)

            dve.wait_ge(fgain_loaded, 16)
            for n in range(2):
                mlp_out(1, 3, n)
                cols = slice(n * HALF, (n + 1) * HALF)
                for tt in range(TT):
                    dve.wait_ge(x_ready, x_version(4, 2 * n + tt + 1))
                    dve.tensor_tensor(gained[:, tt, cols], x[:, tt, cols], final_gain[:, cols], ALU.mult)\
                        .then_inc(gained_ready, 1)
                if n == 0:
                    split_turn("x5.0")
                    split_turn("x5.2")

            def normed(n):
                dve.wait_ge(rstd_ready, 5)
                tt, cols = n % 2, slice(n // 2 * HALF, (n // 2 + 1) * HALF)
                dve.tensor_scalar(x[:, tt, cols], gained[:, tt, cols], rstd[:, 4, tt:tt + 1], None, ALU.mult)\
                    .then_inc(x_ready, 1)

            def shared_key():
                dve.wait_ge(group_act, groups["ckv"]["act_end"])
                dve.wait_ge(b2_loaded, 64)
                dve.wait_ge(trig_ready, 1)
                kr = lat_sb[:, :, LAT:]
                mark(dve.tensor_tensor(kr_sb[:, 1, :, :], kr, kr, ALU.mult))
                mark(dve.tensor_tensor(kr_sb[:, 0, :, :], kr, spread_to(rope_gain[:, 1, :], 1, [TT, ROPE]), ALU.mult))
                own()
                mark(dve.tensor_reduce(kr_ss[:, :], kr_sb[:, 1, :, :], AXIS, ALU.add))
                own()
                lo_half, hi_half = slice(0, ROPE // 2), slice(ROPE // 2, ROPE)
                mark(rotate(kr_sb[:, 3, :, lo_half], kr_sb[:, 3, :, hi_half], kr_sb[:, 1, :, lo_half],
                            kr_sb[:, 2, :, lo_half], kr_sb[:, 0, :, lo_half], kr_sb[:, 0, :, hi_half],
                            trig[:, 1, :, P:], trig[:, 0, :, P:]))

            def ret_rotate(name):
                n = ("rq0", "rq1", "rk0", "rk1").index(name)
                dve.wait_ge(group_act, groups[name]["act_end"])
                if n:
                    wait_turn(dve, ("rq0", "rq1", "rk0")[n - 1] + "b")
                    dve.wait_ge(ret_roped, n)
                src, dst = (work[:, i, :, :].rearrange("p t (h d) -> p t h d", h=2) for i in range(2))
                tmp = [l_work[:, i * HALF:(i + 1) * HALF].rearrange("p (t h d) -> p t h d", t=TT, h=2)
                       for i in range(2)]
                cos, sin = (spread_to(trig[:, i, :, 0:P], 2, [TT, 2, P]) for i in (1, 0))
                rotate(dst[:, :, :, 0:P], dst[:, :, :, P:], tmp[0], tmp[1], src[:, :, :, 0:P], src[:, :, :, P:],
                       cos, sin).then_inc(ret_roped, 1)

            def ret_copy(name, half):
                n = ("rq0", "rq1", "rk0", "rk1").index(name)
                turn_name = f"{name}{'ab'[half]}"
                c = 4 * (n % 2) + 2 * half
                copy_turn(turn_name, (rq_t if n < 2 else rk_t)[:, c:c + 2, :],
                          turn_bank(turn_name).rearrange("p (c s) -> p c s", c=2))

            def ret_decay(h):
                dve.wait_ge(ret_scored, h + 1)
                dve.scalar_tensor_tensor(ret_s[:, h, :], score[:, h % 2, 0:SCORE], RET_QK ** -0.5, ret_s[:, h, :],
                                         ALU.mult, ALU.mult).then_inc(ret_decayed, 1)

            def ret_value(h):
                dve.wait_ge(group_act, groups[f"ret{h}"]["act_end"])
                for tt in range(TT):
                    dve.tensor_copy(ret[:, tt, h * HALF:(h + 1) * HALF], group_ps(f"ret{h}")[:, tt, :])\
                        .then_inc(group_dve, 1)

            def gate_out(n):
                dve.wait_ge(ret_norm, 1)
                dve.wait_ge(group_act, groups[f"rg{n}"]["act_end"])
                dve.wait_ge(group_dve, groups["ret3"]["dve_end"])
                cols = slice(n * HALF, (n + 1) * HALF)
                for tt in range(TT):
                    last = dve.scalar_tensor_tensor(ret[:, tt, cols], ret[:, tt, cols], ret_r[:, tt, n:n + 1],
                                                    work[:, n % 2, tt, :], ALU.mult, ALU.mult)
                last.then_inc(gated, 1)

            def mla_sums_q():
                for tt in range(TT):
                    dve.wait_ge(l_squares, tt + 1)
                    scratch = l_work[:, 0:MLA_H * MLA_QK] if tt == 0 else lk_flat[:, 0:MLA_H * MLA_QK]
                    dve.tensor_reduce(lq_ss[:, tt, :], scratch.rearrange("p (h d) -> p h d", d=MLA_QK), AXIS, ALU.add)\
                        .then_inc(l_sq, 1)

            def mla_sums_k():
                for tt in range(TT):
                    dve.wait_ge(l_squares, TT + tt + 1)
                    scratch = l_work[:, 0:MLA_H * NOPE] if tt == 0 else lk_flat[:, 0:MLA_H * NOPE]
                    dve.tensor_reduce(lk_ss[:, tt, :], scratch.rearrange("p (h d) -> p h d", d=NOPE), AXIS, ALU.add)\
                        .then_inc(l_sq, 1)
                dve.wait_ge(l_sq, 4)
                for tt in range(TT):
                    dve.tensor_scalar(lk_ss[:, tt, :], lk_ss[:, tt, :], kr_ss[:, tt:tt + 1], None, ALU.add)\
                        .then_inc(l_sq, 1)

            def mla_q(tt):
                dve.wait_ge(l_norm, 1)
                q = lq_sb[:, tt, :, :]
                mark(dve.tensor_tensor(q, q, spread_to(lq_r[:, tt, :], 2, [MLA_H, MLA_QK]), ALU.mult))
                own()
                part = lq_sb[:, tt, :, NOPE:]
                mark(dve.tensor_tensor(part, part, spread_to(rope_gain[:, 0, :], 1, [MLA_H, ROPE]), ALU.mult))
                own()
                half = ROPE // 2
                cos, sin = (spread_to(trig[:, i, tt, P:], 1, [MLA_H, half]) for i in (1, 0))
                rotate(rot[:, tt, :, 0:half], rot[:, tt, :, half:], prod[:, tt, :, 0:half], prod[:, tt, :, half:],
                       part[:, :, 0:half], part[:, :, half:], cos, sin).then_inc(lq_ready, 1)

            def mla_k():
                dve.wait_ge(l_norm, 2)
                for tt in range(TT):
                    k = kv[:, tt, :, 0:NOPE]
                    last = dve.tensor_tensor(k, k, spread_to(lk_r[:, tt, :], 2, [MLA_H, NOPE]), ALU.mult)
                last.then_inc(lk_ready, 1)

            def mla_k_rot():
                wait_turn(dve, "mqr1")
                for tt in range(TT):
                    last = dve.tensor_tensor(rot[:, tt, :, :], spread_to(kr_sb[:, 3, tt, :], 1, [MLA_H, ROPE]),
                                             spread_to(lk_r[:, tt, :], 2, [MLA_H, ROPE]), ALU.mult)
                last.then_inc(lk_ready, 1)

            def mla_rot_copy(which, b):
                name = f"{which}r{b}"
                copy_turn(name, (lq_t if which == "mq" else lk_t)[:, 2 * b:2 * b + 2, :],
                          turn_bank(name).rearrange("p (h s) -> p h s", h=2))

            def mla_logits(h):
                dve.wait_ge(l_scored, h + 1)
                b = h % 2
                if h >= 2:
                    wait_turn(dve, f"lp{h - 2}")
                dve.tensor_tensor(l_e[:, b, :], score[:, b, 0:SCORE], mask[:, :], ALU.add).then_inc(l_masked, 1)
                dve.wait_ge(l_masked, h + 1)
                for j, cols in enumerate((WIDE, TALL)):
                    last = dve.tensor_reduce(l_nm[:, b, j:j + 1], l_e[:, b, cols], AXIS, ALU.max, negate=True)
                last.then_inc(l_maxed, 1)

            def mla_recip(h):
                dve.wait_ge(l_exped, h + 1)
                if h >= 2:
                    dve.wait_ge(turn_act, turn[f"lv{h - 2}"]["act_end"])
                dve.reciprocal(l_rec[:, h % 2, :], l_sum[:, h % 2, :]).then_inc(l_reced, 1)

            def mla_slot(n):
                if n < MLA_H:
                    mla_logits(n)
                if 1 <= n <= MLA_H:
                    mla_recip(n - 1)

            dense("cq", {0: lambda: split_turn("x5.4"), 1: lambda: split_turn("x5.6")})
            dense("ckv", {n: (lambda n=n: normed(n)) for n in range(4)})
            dense("rq0", {0: shared_key, 1: lambda: split_turn("lat.0"), 2: lambda: split_turn("lat.2"),
                          3: lambda: split_turn("lat.4")})
            for name, before in (("rq1", "rq0"), ("rk0", "rq1"), ("rk1", "rk0")):
                dense(name, {0: lambda before=before: ret_rotate(before), 2: lambda before=before: ret_copy(before, 0),
                             3: lambda before=before: ret_copy(before, 1)})
            dense("uq0", {0: lambda: ret_rotate("rk1")})
            dense("uq1", {1: lambda: ret_copy("rk1", 0)})
            dense("uq2", {1: lambda: ret_copy("rk1", 1)})
            for n in range(4):
                dense(f"ukv{n}")
                ret_decay(n)
            dense("rv0", {0: mla_sums_q, 3: mla_sums_k})
            dense("rv1", {0: lambda: mla_q(0), 1: lambda: mla_q(1), 2: mla_k})
            ret_value(0)
            dense("rv2")
            ret_value(1)

            def rv3_slot(n):
                if n == 0:
                    mla_rot_copy("mq", 0)
                    mla_rot_copy("mq", 1)
                    mla_k_rot()
            dense("rv3", {n: (lambda n=n: rv3_slot(n)) for n in range(4)})
            ret_value(2)
            dense("rg0", {n: (lambda n=n: mla_rot_copy("mk", n)) for n in range(2)})
            ret_value(3)
            dense("rg1", {n: (lambda n=n: mla_slot(n)) for n in range(4)})
            gate_out(0)
            dense("rg2", {n: (lambda n=n: mla_slot(4 + n)) for n in range(4)})
            gate_out(1)
            dense("rg3", {0: lambda: mla_slot(8)})
            gate_out(2)
            gate_out(3)
            dense("gm0", {n: (lambda n=n: split_turn(f"roT.{2 * n}")) for n in range(4)})
            dense("gm1", {n: (lambda n=n: split_turn(f"roT.{8 + 2 * n}")) for n in range(4)})
            dense("gr0")
            dense("gr1")

            def mix_ret(n):
                wait_group(dve, f"br{n}")
                dve.wait_ge(group_act, groups["gr1"]["act_end"])
                cols = slice(n * HALF, (n + 1) * HALF)
                for tt in range(TT):
                    dve.tensor_tensor(mix[:, tt, cols], group_ps(f"br{n}")[:, tt, :], gr[:, tt, cols], ALU.mult)\
                        .then_inc(group_dve, 1)

            def mix_mla(n):
                wait_group(dve, f"bm{n}")
                cols = slice(n * HALF, (n + 1) * HALF)
                for tt in range(TT):
                    dve.tensor_tensor(gm[:, tt, cols], group_ps(f"bm{n}")[:, tt, :], gm[:, tt, cols], ALU.mult)\
                        .then_inc(group_dve, 1)
                for tt in range(TT):
                    dve.wait_ge(group_dve, groups[f"bm{n}"]["dve_end"] - 1 + tt)
                    dve.tensor_tensor(mix[:, tt, cols], mix[:, tt, cols], gm[:, tt, cols], ALU.add)\
                        .then_inc(mixed, 1)

            dense("br0", {2 * n + 1: (lambda n=n: split_turn(f"moT.{2 * n}")) for n in range(4)})
            mix_ret(0)
            dense("br1")
            mix_ret(1)
            dense("bm0")
            mix_mla(0)
            dense("bm1", {2: lambda: split_turn("mixT.0"), 3: lambda: split_turn("mixT.2")})
            mix_mla(1)
            dense("wo0", {0: lambda: split_turn("mixT.4"), 1: lambda: split_turn("mixT.6")})
            add_to_x("wo0", 0)
            dense("wo1", {2: lambda: split_turn("x6.0"), 3: lambda: split_turn("x6.2")})
            add_to_x("wo1", 1)
            split_turn("x6.4")
            split_turn("x6.6")
            mlp(2, 6, lambda: split_turn("pT.0"))
            mlp_end(2, 6, "x7")

            dense("pl0")
            dense("pl1")
            for n in range(2):
                dense(f"pg{n}", {0: lambda: split_turn("x7.4"), 1: lambda: split_turn("x7.6")} if n == 0 else None)
                dve.wait_ge(group_act, groups[f"pg{n}"]["act_end"])
                cols = slice(n * HALF, (n + 1) * HALF)
                for tt in range(TT):
                    mark(dve.tensor_tensor(gate[:, tt, cols], gate[:, tt, cols], ple[:, tt, cols], ALU.mult))
                    own()
                    dve.tensor_tensor(gate[:, tt, cols], gate[:, tt, cols], x[:, tt, cols], ALU.add)\
                        .then_inc(out_ready, 1)

        @block.gpsimd
        def _(pool):
            mark, own = own_order(pool, pool_step)

            def factor(dst, means, sums, scale, eps, done):
                mark(pool.tensor_scalar(means, sums, scale, eps, ALU.mult, ALU.add))
                own()
                shape = dst.shape[1:]
                half = mhalf[:, 0:math.prod(shape)]
                if len(shape) == 2:
                    half = half.rearrange("p (a b) -> p a b", a=shape[0])
                pool.tensor_tensor(dst, means, half, ALU.pow).then_inc(done, 1)

            def x_factor(v):
                pool.wait_ge(x_squared, TT * (v + 1))
                factor(rstd[:, v, :], msx[:, v, :], ssx[:, v, :], 1 / D, EPS, rstd_ready)

            pool.dma_start(onehot[0:BUCKETS + 1, :], w["c_onehot"]).then_inc(small_loaded, 16)
            pool.dma_start(table[0:BUCKETS, :], w["rel_bias"]).then_inc(small_loaded, 16)
            mark(pool.memset(table[BUCKETS:BUCKETS + 1, :], NEG))
            own()
            mark(pool.memset(zeros[:, :], 0.0))
            own()
            pool.memset(mhalf[:, :], -0.5).then_inc(set_ready, 1)
            for i, name in enumerate(("attn_lambda_q1", "attn_lambda_k1", "attn_lambda_q2", "attn_lambda_k2")):
                pool.dma_start(lam_in[:, i, :], w[name][0, :].partition_broadcast(P)).then_inc(lam_loaded, 16)
            pool.dma_start(inv[:, :], w["c_inv"][0, :].partition_broadcast(P)).then_inc(pos_loaded, 16)
            with nc.allow_non_contiguous_dma(reason="256 positions"):
                pool.dma_start(pos_i[:, :], w["positions_2"][0, :].rearrange("(t p) -> p t", p=P))\
                    .then_inc(pos_loaded, 16)
            pool.wait_ge(bias_rows_ready, 1)
            pool.dma_start(bias_dram[:, 0:3 * P - 1], bias_rows[0:DA_H, :]).then_inc(bias_stored, 16)
            pool.wait_ge(bias_stored, 16)
            rows = bass.AP(bias_dram.tensor, 0, [[0, P], [SCORE, DA_H], [1, 3 * P - 1]])
            pool.dma_start(bias_rep[:, :, 0:3 * P - 1], rows).then_inc(bias_stored, 16)
            pool.wait_ge(bias_stored, 32)
            for cols, at in ((WIDE, P - 1), (TALL, 2 * P - 1)):
                n = cols.stop - cols.start
                skewed = bass.AP(bias_rep.tensor, at, [[DA_H * SCORE - 1, P], [SCORE, DA_H], [1, n]])
                pool.dma_start(bias[:, :, cols], skewed).then_inc(bias_loaded, 16)
            pool.wait_ge(set_ready, 1)
            x_factor(0)
            for half in range(2):
                pool.wait_ge(turn_act, turn[f"av{4 * half + 3}"]["act_end"])
                keep = (1.0 - LAMBDA_INIT) ** -2
                factor(da_r[:, half, :, :], da_ms[:, half, :, :], da_ss[:, half, :, :], keep / P, keep * EPS, da_norm)
            x_factor(1)
            pool.wait_ge(x_ready, x_version(2))
            pool.dma_start(gate_b[:, 0:ML_H], w["mlstm_b_i"][0, :].partition_broadcast(P)).then_inc(ml_loaded, 16)
            pool.dma_start(gate_b[:, ML_H:], w["mlstm_b_f"][0, :].partition_broadcast(P)).then_inc(ml_loaded, 16)
            pool.memset(ml_v[:, :, :, ML_V:], 1.0).then_inc(ml_ones, 1)
            x_factor(2)
            for half in range(2):
                two = slice(2 * half, 2 * half + 2)
                pool.wait_ge(ml_ms, half + 1)
                factor(r_r[:, :, two], r_t[:, :, two], r_ms[:, :, two], 1 / ML_V, EPS, ml_norm)
            pool.wait_ge(x_ready, x_version(3))
            pool.dma_start(final_gain[:, :], w["final_norm"].partition_broadcast(P)).then_inc(fgain_loaded, 16)
            x_factor(3)
            pool.wait_ge(gained_ready, 4)
            pool.dma_start(rope_gain[:, 0, :], w["q_norm_2"][0, NOPE:].partition_broadcast(P)).then_inc(b2_loaded, 16)
            pool.dma_start(rope_gain[:, 1, :], w["k_norm_2"][0, NOPE:].partition_broadcast(P)).then_inc(b2_loaded, 16)
            pool.dma_start(mask[:, :], w["c_mask"]).then_inc(b2_loaded, 16)
            pool.dma_start(ret_s[:, :, :], w["c_decay"]).then_inc(b2_loaded, 16)
            x_factor(4)
            pool.wait_ge(x_squared, TT * 6)
            pool.wait_ge(rstd_ready, 5)
            for _ in range(2):
                mark(pool.tensor_tensor(ssx[:, 5, :], ssx[:, 5, :], rstd[:, 4, :], ALU.mult))
                own()
            mark(pool.tensor_scalar(msx[:, 5, :], ssx[:, 5, :], 1 / D, EPS, ALU.mult, ALU.add))
            own()
            mark(pool.tensor_tensor(msx[:, 5, :], msx[:, 5, :], mhalf[:, 0:TT], ALU.pow))
            own()
            pool.tensor_tensor(rstd[:, 5, :], msx[:, 5, :], rstd[:, 4, :], ALU.mult).then_inc(rstd_ready, 1)
            pool.wait_ge(lat_sq, 2 * TT)
            mark(pool.tensor_scalar(lat_ms[:, 0, :], lat_ss[:, 0, :], 1 / Q_LORA, EPS, ALU.mult, ALU.add))
            mark(pool.tensor_scalar(lat_ms[:, 1, :], lat_ss[:, 1, :], 1 / KV_LORA, EPS, ALU.mult, ALU.add))
            own()
            pool.tensor_tensor(lat_r[:, :, :], lat_ms[:, :, :], mhalf[:, 0:4].rearrange("p (a b) -> p a b", a=2),
                               ALU.pow).then_inc(lat_norm, 1)
            pool.wait_ge(group_act, groups["uq2"]["act_end"])
            pool.wait_ge(ret_roped, 4)
            for tt in range(TT):
                q = flat_q[:, tt * MLA_H * MLA_QK:(tt + 1) * MLA_H * MLA_QK]
                scratch = (l_work if tt == 0 else lk_flat)[:, 0:MLA_H * MLA_QK]
                pool.tensor_tensor(scratch, q, q, ALU.mult).then_inc(l_squares, 1)
            pool.wait_ge(group_act, groups["ukv3"]["act_end"])
            for tt in range(TT):
                pool.wait_ge(l_sq, tt + 1)
                k = kv[:, tt, :, 0:NOPE]
                scratch = (l_work if tt == 0 else lk_flat)[:, 0:MLA_H * NOPE].rearrange("p (h d) -> p h d", d=NOPE)
                pool.tensor_tensor(scratch, k, k, ALU.mult).then_inc(l_squares, 1)
            factor(lq_r[:, :, :], lq_ms[:, :, :], lq_ss[:, :, :], 1.0, MLA_QK * EPS, l_norm)
            pool.wait_ge(l_sq, 6)
            factor(lk_r[:, :, :], lk_ms[:, :, :], lk_ss[:, :, :], 1 / MLA_QK, EPS, l_norm)
            pool.wait_ge(group_act, groups["ret3"]["act_end"])
            factor(ret_r[:, :, :], ret_ms[:, :, :], ret_ss[:, :, :], 1 / RET_V, EPS, ret_norm)
            pool.wait_ge(x_ready, x_version(6))
            for tt in range(TT):
                pool.dma_start(p_sb[:, tt, :], w["p_2"][0, 0, tt * P:(tt + 1) * P, :]).then_inc(p_loaded, 16)
            x_factor(6)
            x_factor(7)


_INS = ["x", "rel_bias", "attn_norm", "attn_w_in", "attn_lambda_q1", "attn_lambda_k1", "attn_lambda_q2",
        "attn_lambda_k2", "attn_subln", "attn_w_out", "mlstm_norm", "mlstm_w_in", "mlstm_b_i", "mlstm_b_f",
        "mlstm_conv_w", "mlstm_conv_b", "mlstm_head_norm", "mlstm_w_out", "mlp_norm", "mlp_w1", "mlp_w2",
        "final_norm", "p_2", "positions_2", "norm_mix_2", "w_in_2", "ret_norm_2", "q_lat_norm_2", "kv_lat_norm_2",
        "w_uq_2", "w_ukv_2", "q_norm_2", "k_norm_2", "w_br_2", "w_bm_2", "w_o_2", "norm_mlp_2", "w_up_2",
        "w_down_2", "norm_ple_2", "w_ple_gate_2", "w_ple_2"]
_ONE_LAYER = ["attn_w_in", "attn_w_out", "mlstm_w_in", "mlstm_w_out", "w_in_2", "w_uq_2", "w_ukv_2", "w_br_2",
              "w_bm_2", "w_o_2", "w_up_2", "w_down_2", "w_ple_gate_2", "w_ple_2"]


def kernel(**inputs):
    import concourse.bacc as bacc
    from concourse.bass_utils import run_bass_kernel_spmd

    nc = bacc.Bacc("TRN2", target_bir_lowering=False, num_devices=1)
    arrays, w = {}, {}
    for name, a in [(n, np.ascontiguousarray(inputs[n])) for n in _INS] + list(constants().items()):
        arrays[f"in_{name}"] = a
        w[name] = nc.dram_tensor(f"in_{name}", a.shape, mybir.dt.from_np(a.dtype), kind="ExternalInput").ap()
    for name in _ONE_LAYER:
        w[name] = w[name][0]
    out = nc.dram_tensor("out_0", (1, S, D), F32, kind="ExternalOutput").ap()
    build(nc, w, out)
    r = run_bass_kernel_spmd(nc, [arrays], core_ids=[0])
    return r.results[0]["out_0"]
```

```python
import math
from contextlib import ExitStack

import numpy as np

import concourse.bass as bass
from concourse import mybir

F32 = mybir.dt.float32
F32R = mybir.dt.float32r
BF16 = mybir.dt.bfloat16
I32 = mybir.dt.int32
ALU = mybir.AluOpType
ACT = mybir.ActivationFunctionType
AXIS = mybir.AxisListType.X

P = 128
S = 256
TT = S // P
D = 1024
DC = D // P
FF = 4 * D
HALF = 512
EPS = 1e-6
NEG = -1e30

UNIT = 1024
RING = 8
AHEAD = 6
AHEAD_0 = AHEAD - 1

DA_H, DA_D = 8, 64
ML_H, ML_QK, ML_V = 4, 128, 256
CONV = 4
RET_H, RET_QK, RET_V = 4, 256, 512
MLA_H, NOPE, ROPE = 8, 128, 64
MLA_QK = NOPE + ROPE
Q_LORA, KV_LORA = 384, 256
LAT = Q_LORA + KV_LORA
BUCKETS = 32
LAMBDA_INIT = 0.8 - 0.6 * math.exp(-0.3 * 0)

WIDE, TALL = slice(0, 2 * P), slice(2 * P, 3 * P)
SCORE = 3 * P

GAIN_ROWS = [("attn_norm", 8), ("mlp_norm", 16), ("mlstm_norm", 8), ("mlstm_head_norm", 8), ("norm_mix_2", 8),
             ("ret_norm_2", 16), ("q_lat_norm_2", 3), ("kv_lat_norm_2", 2), ("norm_mlp_2", 8), ("norm_ple_2", 8),
             ("attn_subln", 1), ("mlstm_conv_w", 32), ("mlstm_conv_b", 8), ("q_norm_2", 1), ("k_norm_2", 1)]
GAIN = {}
for _name, _rows in GAIN_ROWS:
    GAIN[_name] = sum(r for n, r in GAIN_ROWS[:len(GAIN)])
assert sum(r for _, r in GAIN_ROWS) == P

TWO_PI = 2 * math.pi
PI_A = 6.28125
PI_B = float(np.float32(math.floor((TWO_PI - PI_A) * 2**20) / 2**20))
PI_C = TWO_PI - PI_A - PI_B
ROUND = 1.5 * 2**23
PI_SAFE = 3.1415925


def constants():
    i = np.arange(P)
    causal = np.where(i[:, None] >= i[None, :], 0.0, NEG)
    dist = S - 1 - np.arange(3 * P - 1)
    d = np.maximum(dist, 1).astype(np.float32)
    exact = BUCKETS // 2
    large = exact + (np.log(d / exact) / math.log(128 / exact) * (BUCKETS - exact)).astype(np.int32)
    bucket = np.where(dist < exact, dist, np.minimum(large, BUCKETS - 1))
    bucket = np.where(dist < 0, BUCKETS, bucket)
    onehot = bucket[None, :] == np.arange(BUCKETS + 1)[:, None]
    log_g = np.log1p(-np.exp2(-5.0 - np.arange(RET_H)))
    diff = np.arange(S)[None, :] - i[:, None]
    wide = np.where(diff[:, None, :] >= 0, np.exp(np.maximum(diff, 0)[:, None, :] * log_g[None, :, None]), 0.0)
    decay = np.concatenate([wide, wide[:, :, 0:P]], axis=2)
    inv = [10000.0 ** (-np.arange(n, dtype=np.float32) / np.float32(n)) for n in (RET_QK // 2, ROPE // 2)]
    square = np.stack([np.eye(P), np.ones((P, P)), i[:, None] <= i[None, :], causal, causal.T], axis=1)
    mask = np.concatenate([np.zeros((P, P)), causal, causal], axis=1)
    out = {"c_square": square, "c_onehot": onehot, "c_decay": decay, "c_inv": np.concatenate(inv)[None, :],
           "c_mask": mask}
    return {k: np.ascontiguousarray(v, dtype=np.float32) for k, v in out.items()}


NINV = RET_QK // 2 + ROPE // 2


AO_UNITS = [(0, 0), (1, 0), (0, 1), (1, 1), (0, 2), (0, 3), (1, 2), (1, 3)]


def schedule(w):
    groups, stream = {}, []
    count = [0]

    def group(name, weight, col, ncols, source, nchunks, act, dve, rows=0, per=2, last=None):
        groups[name] = dict(index=len(groups), units=[], ncols=ncols, source=source, act=act, dve=dve,
                            weight=weight, col=col, nchunks=nchunks, rows=rows, per=per)
        if weight is not None:
            chunks(name, 0, nchunks if last is None else last)

    def chunks(name, first, last):
        g, c = groups[name], first
        while c < last:
            n = min(g["per"], last - c)
            src = g["weight"][g["rows"] + c * P:g["rows"] + (c + n) * P, g["col"]:g["col"] + g["ncols"]]
            g["units"].append((count[0], c, n))
            stream.append(("unit", count[0], src.rearrange("(c p) n -> p c n", p=P), n, g["ncols"]))
            count[0] += 1
            c += n

    def swap_pairs():
        group(f"none{len(groups)}", None, 0, 0, None, 0, 0, 0)

    def mlp(which, w1, w2):
        stream.append(("mlp", count[0], w1, w2, which))
        mlps.append(count[0])
        count[0] += 2 * 4 * (FF // HALF)

    mlps = []
    qkv = w["attn_w_in"]
    for name, col in (("q0", 0), ("k0", D), ("q1", HALF), ("k1", D + HALF), ("v0", 2 * D), ("v1", 2 * D + HALF)):
        group(name, qkv, col, HALF, "x0", DC, 2, 0)
    for n in range(2):
        group(f"ao{n}", w["attn_w_out"], n * HALF, HALF, "oT", DC, 0, 0, last=0)
    for n, u in AO_UNITS:
        chunks(f"ao{n}", 2 * u, 2 * u + 2)
    mlp(0, w["mlp_w1"][0], w["mlp_w2"][0])
    swap_pairs()
    ml = w["mlstm_w_in"]
    group("gate", ml, 3 * D, 2 * ML_H, "x2", DC, 2, 0, per=8, last=0)
    group("mq", ml, 0, HALF, "x2", DC, 2, 0, last=DC - 2)
    chunks("gate", 0, DC)
    chunks("mq", DC - 2, DC)
    for name, col in (("mk", HALF), ("mv0", D), ("mv1", D + HALF), ("mo0", 2 * D), ("mo1", 2 * D + HALF)):
        group(name, ml, col, HALF, "x2", DC, 2, 0)
    for n in range(2):
        group(f"mw{n}", w["mlstm_w_out"], n * HALF, HALF, "yT", DC, 0, 0, last=DC // 2)
    for n in range(2):
        chunks(f"mw{n}", DC // 2, DC)
    mlp(1, w["mlp_w1"][1], w["mlp_w2"][1])
    swap_pairs()
    win = w["w_in_2"]
    at = np.cumsum([0, D, D, 2 * D, 2 * D, Q_LORA, KV_LORA + ROPE, D, D]).tolist()
    group("cq", win, at[4], Q_LORA, "x5", DC, 2, 0, last=DC // 2)
    group("ckv", win, at[5], KV_LORA + ROPE, "x5", DC, 2, 0, last=DC // 2)
    for name in ("cq", "ckv"):
        chunks(name, DC // 2, DC)
    for name, col in (("rq0", at[0]), ("rq1", at[0] + HALF), ("rk0", at[1]), ("rk1", at[1] + HALF)):
        group(name, win, col, HALF, "x5", DC, 2, 0)
    for n in range(3):
        group(f"uq{n}", w["w_uq_2"], n * HALF, HALF, "latq", Q_LORA // P, 2, 0)
    for n in range(4):
        group(f"ukv{n}", w["w_ukv_2"], n * HALF, HALF, "latkv", KV_LORA // P, 2, 0)
    for n in range(4):
        group(f"rv{n}", win, at[2] + n * HALF, HALF, "x5", DC, 2, 0)
        if n:
            group(f"ret{n - 1}", None, 0, HALF, None, 0, 2, 2)
    group("rg0", win, at[3], HALF, "x5", DC, 2, 0)
    group("ret3", None, 0, HALF, None, 0, 2, 2)
    for n in range(1, 4):
        group(f"rg{n}", win, at[3] + n * HALF, HALF, "x5", DC, 2, 0)
    for name, col in (("gm0", at[7]), ("gm1", at[7] + HALF), ("gr0", at[6]), ("gr1", at[6] + HALF)):
        group(name, win, col, HALF, "x5", DC, 2, 0)
    for n in range(2):
        group(f"br{n}", w["w_br_2"], n * HALF, HALF, "roT", 2 * DC, 0, 2)
    for n in range(2):
        group(f"bm{n}", w["w_bm_2"], n * HALF, HALF, "moT", DC, 0, 2)
    for n in range(2):
        group(f"wo{n}", w["w_o_2"], n * HALF, HALF, "mixT", DC, 0, 0, last=DC // 2 if n == 0 else 2)
    for n in range(2):
        chunks(f"wo{n}", DC // 2 if n == 0 else 2, DC)
    mlp(2, w["w_up_2"], w["w_down_2"])
    assert groups["ao1"]["index"] % 2 and groups["mw1"]["index"] % 2 and groups["wo1"]["index"] % 2
    for n in range(2):
        group(f"pl{n}", w["w_ple_2"], n * HALF, HALF, "pT", 2, 2, 0)
    for n in range(2):
        group(f"pg{n}", w["w_ple_gate_2"], n * HALF, HALF, "x7", DC, 2, 0)

    act = dve = 0
    by_index = []
    for g in groups.values():
        act, dve = act + g["act"], dve + g["dve"]
        g["act_end"], g["dve_end"] = act, dve
        by_index.append(g)
    return groups, by_index, stream, mlps


def turns():
    order = [("gains0", 1, 0)]

    def split(name, chunks, c=0):
        for n in chunks:
            order.append((f"{name}.{c}", n, n))
            c += n

    pairs = [2] * (DC // 2)
    split("x0", pairs)
    order.append(("gains", 1, 0))
    for name in ("q0", "k0", "q1", "k1"):
        order.extend([(f"{name}a", 1, 0), (f"{name}b", 1, 0)])
    for kind, h in (("p", 0), ("v", 0), ("p", 2), ("o", 0), ("v", 2), ("p", 4), ("o", 2), ("v", 4), ("p", 6), ("o", 4),
                    ("v", 6), ("o", 6)):
        if kind == "o":
            split("oT", [2], h)
        else:
            order.extend([(f"a{kind}{h + j}", 1 if kind == "p" else 2, 0 if kind == "p" else 1) for j in range(2)])
    split("x1", pairs)
    split("x2", pairs)
    for b in range(4):
        order.append((f"conv{b}", 2, 1))
    for h in range(ML_H):
        order.extend([(f"mv{h}.0", 2, 0), (f"mv{h}.1", 2, 0)])
    split("yT", pairs)
    split("x3", pairs)
    split("x5", pairs)
    split("lat", [2, 2, 1])
    for name in ("rq0", "rq1", "rk0", "rk1"):
        order.extend([(f"{name}a", 0, 1), (f"{name}b", 0, 1)])
    for name in ("mq", "mk"):
        order.extend([(f"{name}n{b}", 1, 0) for b in range(4)])
        order.extend([(f"{name}r{b}", 0, 1) for b in range(2)])
    for h in range(MLA_H + 1):
        if h:
            order.append((f"lv{h - 1}", 2, 0))
        if h < MLA_H:
            order.append((f"lp{h}", 1, 0))
    split("roT", pairs + pairs)
    split("moT", pairs)
    split("mixT", pairs)
    split("x6", pairs)
    split("pT", [2])
    split("x7", pairs)
    table, act, dve = {}, 0, 0
    for i, (name, a, d) in enumerate(order):
        table[name] = dict(index=i, act=act, dve=dve, act_end=act + a, dve_end=dve + d)
        act, dve = act + a, dve + d
    by_index = [table[name] for name, _, _ in order]
    return table, by_index


def turn_of(source, c):
    if source == "latq":
        name = "lat"
    elif source == "latkv":
        name, c = "lat", c + Q_LORA // P
    else:
        name = source
    return f"{name}.{c // 2 * 2}", c % 2


def build(nc, w, out):
    groups, group_list, stream, mlps = schedule(w)
    turn, turn_list = turns()
    total_units = stream[-1][1] + 1
    NX = 8

    with ExitStack() as ctx:
        def sb(name, shape, dt=F32, scope=ctx):
            return scope.enter_context(nc.sbuf_tensor(name, [P, *shape], dt))

        def sem(name):
            return ctx.enter_context(nc.semaphore(name))

        x = sb("x", [TT, D])
        with ExitStack() as ph:
            raw = sb("raw", [RING, UNIT], scope=ph)
        w_lo = sb("w_lo", [RING, UNIT], F32R)
        w_hi = sb("w_hi", [RING, UNIT], F32R)
        a_hi = sb("a_hi", [DC, S], F32R)
        a_lo = sb("a_lo", [DC, S], F32R)
        junk = sb("junk", [D], BF16)
        square = sb("square", [5, P])
        ident, ones, triu, causal, causal_t = (square[:, i, :] for i in range(5))
        gains = sb("gains", [P])
        trig = sb("trig", [2, TT, NINV])
        zeros = sb("zeros", [HALF], BF16)
        mhalf = sb("mhalf", [2 * DA_H])
        ssx = sb("ssx", [NX, TT])
        msx = sb("msx", [NX, TT])
        rstd = sb("rstd", [NX, TT])
        inv_ms = sb("inv_ms", [NX, TT])
        means4 = sb("means4", [TT])
        lam_s = sb("lam_s", [2])
        lam_e = sb("lam_e", [2])
        neg_lam = sb("neg_lam", [1])

        with ExitStack() as ph:
            qk_sb = sb("qk_sb", [2, TT, HALF], scope=ph)
            da_q = sb("da_q", [DA_H, S], scope=ph)
            da_k = sb("da_k", [DA_H, S], scope=ph)
            da_v = sb("da_v", [TT, D], scope=ph)
            bias = sb("bias", [DA_H, SCORE], scope=ph)
            da_e = sb("da_e", [2, 2, SCORE], scope=ph)
            da_p = sb("da_p", [DA_H, SCORE], scope=ph)
            da_pt = sb("da_pt", [2, SCORE], scope=ph)
            da_o = sb("da_o", [TT, D], scope=ph)
            da_nm = sb("da_nm", [2, 4], scope=ph)
            da_sum = sb("da_sum", [2, 4], scope=ph)
            da_rec = sb("da_rec", [2, 4], scope=ph)
            da_nl = sb("da_nl", [2, 2], scope=ph)
            da_ss = sb("da_ss", [DA_H // 2, TT, 2], scope=ph)
            da_ms = sb("da_ms", [DA_H // 2, TT, 2], scope=ph)
            da_r = sb("da_r", [DA_H // 2, TT, 2], scope=ph)
        with ExitStack() as ph:
            o_hi = sb("o_hi", [DC, S], F32R, scope=ph)
            o_lo = sb("o_lo", [DC, S], F32R, scope=ph)
        with ExitStack() as ph:
            sb("below_setup", [2 * TT * HALF + 2 * DA_H * S], scope=ph)
            gain_rows = sb("gain_rows", [P], scope=ph)
            onehot = sb("onehot", [3 * P - 1], scope=ph)
            table = sb("table", [DA_H], scope=ph)
            bias_rows = sb("bias_rows", [3 * P - 1], scope=ph)
            lam_in = sb("lam_in", [4, DA_D], scope=ph)
            lam_prod = sb("lam_prod", [2, DA_D], scope=ph)
            pos_i = sb("pos_i", [TT], I32, scope=ph)
            pos_f = sb("pos_f", [TT], scope=ph)
            inv = sb("inv", [NINV], scope=ph)
            fgain_t = sb("fgain_t", [DC], scope=ph)
        with ExitStack() as ph:
            sb("below_angles", [2 * TT * HALF + 2 * DA_H * S + TT * D + DA_H * SCORE + 4 * SCORE + DA_H * SCORE
                                + 2 * SCORE], scope=ph)
            ang = sb("ang", [2, TT, NINV], scope=ph)
            turns_k = sb("turns_k", [2, TT, NINV], scope=ph)

        with ExitStack() as ph:
            relu = sb("relu", [TT, HALF], scope=ph)
            hid = sb("hid", [TT, HALF], scope=ph)
            h_hi = sb("h_hi", [HALF // P, S], F32R, scope=ph)
            h_lo = sb("h_lo", [HALF // P, S], F32R, scope=ph)
            final_gain = sb("final_gain", [D], scope=ph)
            p_sb = sb("p_sb", [TT, 2 * P], scope=ph)
            p_hi = sb("p_hi", [2, S], F32R, scope=ph)
            p_lo = sb("p_lo", [2, S], F32R, scope=ph)
            ple = sb("ple", [TT, D], scope=ph)
            gate = sb("gate", [TT, D], scope=ph)
            gained = gate

        with ExitStack() as ph:
            ml_qk = sb("ml_qk", [2, TT, HALF], scope=ph)
            ml_t = sb("ml_t", [2 * ML_H, S], scope=ph)
            ml_v = sb("ml_v", [TT, ML_H, ML_V + 1], scope=ph)
            ml_o = sb("ml_o", [TT, D], scope=ph)
            ml_n = sb("ml_n", [TT, ML_H, ML_V + 1], scope=ph)
            ml_w = sb("ml_w", [ML_H, SCORE], scope=ph)
            ml_s = sb("ml_s", [ML_H, SCORE], scope=ph)
            diag = sb("diag", [ML_H, S], scope=ph)
            maxed = sb("maxed", [ML_H, P], scope=ph)
            y_hi = sb("y_hi", [DC, S], F32R, scope=ph)
            y_lo = sb("y_lo", [DC, S], F32R, scope=ph)
            gate_b = sb("gate_b", [2 * ML_H], scope=ph)
            ml_g = sb("ml_g", [14, TT, ML_H], scope=ph)
            (g_fz, g_nfz, g_abs, g_exp, g_ln, g_lf, g_i, g_F, g_g, g_max, g_max2, g_nm, g_em, g_den) = (
                ml_g[:, i, :, :] for i in range(14))
            ml_r = sb("ml_r", [8, TT, ML_H], scope=ph)
            (r_abs, r_dmax, r_dinv, r_ss, r_t, r_ms, r_r, r_sc) = (ml_r[:, i, :, :] for i in range(8))
            gate_in = sb("gate_in", [TT, 2 * ML_H], scope=ph)

        ph = ctx
        lq_sb = sb("lq_sb", [TT, MLA_H, MLA_QK], scope=ph)
        ret = sb("ret", [TT, RET_H * RET_V], scope=ph)
        ret_s = sb("ret_s", [RET_H, SCORE], scope=ph)
        work = sb("work", [2, TT, HALF], scope=ph)
        mask = sb("mask", [SCORE], scope=ph)
        rope_gain = sb("rope_gain", [2, ROPE], scope=ph)
        lat_ss = sb("lat_ss", [2, TT], scope=ph)
        lat_ms = sb("lat_ms", [2, TT], scope=ph)
        lat_r = sb("lat_r", [2, TT], scope=ph)
        lq_ss = sb("lq_ss", [TT, MLA_H], scope=ph)
        lq_ms = sb("lq_ms", [TT, MLA_H], scope=ph)
        lq_r = sb("lq_r", [TT, MLA_H], scope=ph)
        lk_ss = sb("lk_ss", [TT, MLA_H], scope=ph)
        lk_ms = sb("lk_ms", [TT, MLA_H], scope=ph)
        lk_r = sb("lk_r", [TT, MLA_H], scope=ph)
        kr_ss = sb("kr_ss", [TT], scope=ph)
        l_nm = sb("l_nm", [2, TT], scope=ph)
        l_sum = sb("l_sum", [2, TT], scope=ph)
        l_rec = sb("l_rec", [2, TT], scope=ph)
        ret_ss = sb("ret_ss", [TT, RET_H], scope=ph)
        ret_ms = sb("ret_ms", [TT, RET_H], scope=ph)
        ret_r = sb("ret_r", [TT, RET_H], scope=ph)
        kr_sb = sb("kr_sb", [4, TT, ROPE], scope=ph)
        ret_t = ret[:, :, :].rearrange("p t n -> p (t n)").rearrange("p (c s) -> p c s", s=S)
        rq_t, rk_t = ret_t[:, 0:DC, :], ret_t[:, DC:2 * DC, :]
        flat_q = lq_sb[:, :, :, :].rearrange("p t h d -> p (t h d)")
        lo_sb = flat_q[:, 0:TT * D].rearrange("p (t n) -> p t n", t=TT)
        mix = lo_sb
        KV = TT * MLA_H * (NOPE + P)
        with ExitStack() as ph:
            lat_sb = sb("lat_sb", [TT, LAT + ROPE], scope=ph)
            sb("below_lat", [KV - TT * (LAT + ROPE)], scope=ph)
            lat_hi = sb("lat_hi", [LAT // P, S], F32R, scope=ph)
            lat_lo = sb("lat_lo", [LAT // P, S], F32R, scope=ph)
        with ExitStack() as ph:
            kv = sb("kv", [TT, MLA_H, NOPE + P], scope=ph)
            lq_n = sb("lq_n", [MLA_H, S], scope=ph)
            lq_t = sb("lq_t", [MLA_H // 2, S], scope=ph)
            lk_n = sb("lk_n", [MLA_H, S], scope=ph)
            lk_t = sb("lk_t", [MLA_H // 2, S], scope=ph)
            l_work = sb("l_work", [2048], scope=ph)
        lk_flat = lk_n[:, :, :].rearrange("p h s -> p (h s)")
        rot = l_work[:, 0:TT * MLA_H * ROPE].rearrange("p (t h d) -> p t h d", t=TT, h=MLA_H)
        prod = l_work[:, 1024:2048].rearrange("p (t h d) -> p t h d", t=TT, h=MLA_H)
        l_e = l_work[:, 0:2 * SCORE].rearrange("p (b n) -> p b n", b=2)
        l_pt = l_work[:, 2 * SCORE:4 * SCORE].rearrange("p (b n) -> p b n", b=2)
        with ExitStack() as ph:
            gm = sb("gm", [TT, D], scope=ph)
            gr = sb("gr", [TT, D], scope=ph)
            b_hi = sb("b_hi", [2 * DC, S], F32R, scope=ph)
            b_lo = sb("b_lo", [2 * DC, S], F32R, scope=ph)

        pair = [ctx.enter_context(nc.psum_tensor(f"pair{i}", [P, TT, HALF], F32)) for i in range(2)]
        turn_ps = ctx.enter_context(nc.psum_tensor("turn_ps", [P, 2, HALF], F32))
        score = ctx.enter_context(nc.psum_tensor("score", [P, 2, HALF], F32))
        down = [pair[1], score]

        landed = [sem(f"landed{i}") for i in range(RING)]
        hi_ready = sem("hi_ready")
        lo_ready = sem("lo_ready")
        unit_used = sem("unit_used")
        group_act = sem("group_act")
        group_dve = sem("group_dve")
        turn_filled = sem("turn_filled")
        turn_act = sem("turn_act")
        turn_dve = sem("turn_dve")
        x_loaded = [sem(f"x_loaded{i}") for i in range(2)]
        fgain_t_loaded = sem("fgain_t_loaded")
        gained_ready = sem("gained_ready")
        x_ready = sem("x_ready")
        x_squared = sem("x_squared")
        x4_squared = sem("x4_squared")
        rstd_ready = sem("rstd_ready")
        inv_ready = sem("inv_ready")
        act_step = sem("act_step")
        dve_step = sem("dve_step")
        pool_step = sem("pool_step")
        const_loaded = sem("const_loaded")
        squares_loaded = sem("squares_loaded")
        gains0_loaded = sem("gains0_loaded")
        gains_loaded = sem("gains_loaded")
        small_loaded = sem("small_loaded")
        pos_loaded = sem("pos_loaded")
        set_ready = sem("set_ready")
        bias_psum = sem("bias_psum")
        bias_rows_ready = sem("bias_rows_ready")
        bias_stored = sem("bias_stored")
        bias_loaded = sem("bias_loaded")
        lam_loaded = sem("lam_loaded")
        lam_sum = sem("lam_sum")
        lam_exp = sem("lam_exp")
        angles_ready = sem("angles_ready")
        trig_ready = sem("trig_ready")
        da_scored = sem("da_scored")
        da_biased = sem("da_biased")
        da_maxed = sem("da_maxed")
        da_exped = sem("da_exped")
        da_mixed = sem("da_mixed")
        da_norm = sem("da_norm")
        da_scaled = sem("da_scaled")
        up_relu = sem("up_relu")
        hid_ready = sem("hid_ready")
        hid_turned = sem("hid_turned")
        hid_hi = sem("hid_hi")
        hid_lo = sem("hid_lo")
        up_half = sem("up_half")
        down_half = sem("down_half")
        fgain_loaded = sem("fgain_loaded")
        ml_loaded = sem("ml_loaded")
        ml_abs = sem("ml_abs")
        ml_ln = sem("ml_ln")
        ml_lf = sem("ml_lf")
        ml_cum = sem("ml_cum")
        ml_diag = sem("ml_diag")
        ml_spread = sem("ml_spread")
        ml_args = sem("ml_args")
        ml_wexp = sem("ml_wexp")
        ml_em = sem("ml_em")
        ml_ones = sem("ml_ones")
        ml_silu = sem("ml_silu")
        ml_scored = sem("ml_scored")
        ml_weighted = sem("ml_weighted")
        ml_ms = sem("ml_ms")
        ml_norm = sem("ml_norm")
        ml_y = sem("ml_y")
        b2_loaded = sem("b2_loaded")
        decay_loaded = sem("decay_loaded")
        ret_roped = sem("ret_roped")
        lat_sq = sem("lat_sq")
        lat_norm = sem("lat_norm")
        ret_scored = sem("ret_scored")
        ret_decayed = sem("ret_decayed")
        ret_out = sem("ret_out")
        ret_norm = sem("ret_norm")
        l_squares = sem("l_squares")
        l_sq = sem("l_sq")
        l_norm = sem("l_norm")
        lq_ready = sem("lq_ready")
        lk_ready = sem("lk_ready")
        l_scored = sem("l_scored")
        l_masked = sem("l_masked")
        l_maxed = sem("l_maxed")
        l_exped = sem("l_exped")
        l_reced = sem("l_reced")
        gated = sem("gated")
        mixed = sem("mixed")
        p_loaded = sem("p_loaded")
        out_ready = sem("out_ready")
        out_stored = sem("out_stored")

        bias_dram = nc.dram_tensor("bias_scratch", (DA_H, SCORE), F32, kind="Internal").ap()
        bias_rep = nc.dram_tensor("bias_replicas", (P, DA_H, SCORE), F32, kind="Internal").ap()

        def own_order(eng, step):
            count = [0]

            def mark(ins):
                ins.then_inc(step, 1)
                count[0] += 1
                return count[0]

            def wait(n=None):
                eng.wait_ge(step, count[0] if n is None else n)
            return mark, wait

        def gain_source(name):
            flat = w[name].rearrange("a b -> (a b)") if len(w[name].shape) == 2 else \
                w[name].rearrange("a b c -> (a b c)")
            return flat[0:dict(GAIN_ROWS)[name] * P].rearrange("(r p) -> r p", p=P)

        def gain(name, c):
            i = GAIN[name] + c
            return gains[:, i:i + 1]

        def wait_group(eng, name):
            eng.wait_ge(unit_used, groups[name]["units"][-1][0] + 1)

        def group_ps(name):
            return pair[groups[name]["index"] % 2]

        def turn_bank(name):
            return turn_ps[:, turn[name]["index"] % 2, :]

        def wait_turn(eng, name):
            eng.wait_ge(turn_filled, turn[name]["index"] + 1)

        OPERAND = {"x0": (a_hi, a_lo, 0), "x2": (a_hi, a_lo, 0), "x5": (a_hi, a_lo, 0), "x7": (a_hi, a_lo, 0),
                   "oT": (o_hi, o_lo, 0), "yT": (y_hi, y_lo, 0), "latq": (lat_hi, lat_lo, 0),
                   "latkv": (lat_hi, lat_lo, Q_LORA // P), "roT": (b_hi, b_lo, 0), "moT": (a_hi, a_lo, 0),
                   "mixT": (b_hi, b_lo, 0), "pT": (p_hi, p_lo, 0)}
        SPLIT = {"x0": (a_hi, a_lo, "attn_norm", 0), "x1": (a_hi, a_lo, "mlp_norm", 0),
                 "x2": (a_hi, a_lo, "mlstm_norm", 0), "x3": (a_hi, a_lo, "mlp_norm", DC),
                 "x5": (a_hi, a_lo, "norm_mix_2", 0), "x6": (a_hi, a_lo, "norm_mlp_2", 0),
                 "x7": (a_hi, a_lo, "norm_ple_2", 0), "oT": (o_hi, o_lo, "attn_subln", None),
                 "yT": (y_hi, y_lo, "mlstm_head_norm", 0),
                 "lat": (lat_hi, lat_lo, "q_lat_norm_2", 0), "roT": (b_hi, b_lo, "ret_norm_2", 0),
                 "moT": (a_hi, a_lo, None, 0), "mixT": (b_hi, b_lo, None, 0), "pT": (p_hi, p_lo, None, 0)}

        def split_parts(name):
            base, c0 = name.split(".")
            hi, lo, g, at = SPLIT[base]
            c0 = int(c0)
            n = turn[name]["act_end"] - turn[name]["act"]
            for j in range(n):
                c = c0 + j
                scale = None if g is None else gain(g, 0 if at is None else at + c)
                yield turn_bank(name)[:, j * S:(j + 1) * S], hi[:, c, :], lo[:, c, :], scale

        def run_group(name, each, slots=None, part=slice(None)):
            for n, unit in list(enumerate(groups[name]["units"]))[part]:
                each(unit)
                if slots and n in slots:
                    slots[n]()

        def ao_units(dense, slots):
            for (n, u), slot in zip(AO_UNITS, slots):
                dense(f"ao{n}", slot and {u: slot}, slice(u, u + 1))

        def x_version(v, nblocks=4):
            return 4 * (v - 1) + nblocks

        block = ctx.enter_context(nc.Block())

        @block.sync
        def _(sp):
            for n in range(2):
                cols = slice(n * HALF, (n + 1) * HALF)
                src = w["x"][0, :, cols].rearrange("(t p) n -> p t n", p=P)
                sp.dma_start(x[:, :, cols], src).then_inc(x_loaded[n], 16)

            def load(k, src, chunks, ncols, it=None):
                if it is not None or k >= RING:
                    used = k - RING + 1
                    sp.wait_ge(unit_used, used if it is None else it * RING + used)
                dst = raw[:, k % RING, 0:chunks * ncols].rearrange("p (c n) -> p c n", n=ncols)
                sp.dma_start(dst, src).then_inc(landed[k % RING], 16)

            def load_up(w1, k, i, it=None):
                cols = slice(i * HALF, (i + 1) * HALF) if it is None else bass.ds(it * HALF, HALF)
                rows = w1.rearrange("(c p) n -> p c n", p=P)
                for u in range(4):
                    load(k + u, rows[:, 2 * u:2 * u + 2, cols], 2, HALF, it)

            def load_down(w2, k, i, it=None):
                for u in range(4):
                    at = i * HALF + u * P if it is None else it * HALF + (u * P - HALF)
                    src = w2[at:at + P, :] if it is None else w2[bass.ds(at, P), :]
                    load(k + u, src.rearrange("p (c n) -> p c n", c=1), 1, D, it)

            def load_small():
                for name, rows in GAIN_ROWS[1:]:
                    at = GAIN[name]
                    sp.dma_start(gain_rows[at:at + rows, :], gain_source(name)).then_inc(gains_loaded, 16)
                sp.dma_start(square[:, 1:, :], w["c_square"][:, 1:, :]).then_inc(squares_loaded, 16)

            for item in stream:
                if item[0] == "unit":
                    _, k, src, chunks, ncols = item
                    load(k, src, chunks, ncols)
                    if k == RING - 1:
                        load_small()
                else:
                    _, k, w1, w2, _ = item
                    load_up(w1, k, 0)
                    with sp.Fori(1, FF // HALF) as i:
                        load_up(w1, k - 4, None, i)
                        load_down(w2, k, None, i)
                    load_down(w2, k + 60, FF // HALF - 1)
            for n in range(2):
                for tt in range(TT):
                    sp.wait_ge(out_ready, 2 * n + tt + 1)
                    sp.dma_start(out[0, tt * P:(tt + 1) * P, n * HALF:(n + 1) * HALF],
                                 gate[:, tt, n * HALF:(n + 1) * HALF]).then_inc(out_stored, 16)
            sp.wait_ge(out_stored, 64)

        @block.tensor
        def _(pe):
            seen = {"source": 0}
            next_turn = [0]

            def product(o, hi, lo, whi, wlo, start, stop):
                pe.matmul(o, hi, whi, start=start, stop=False)
                pe.matmul(o, hi, wlo, start=False, stop=False)
                return pe.matmul(o, lo, whi, start=False, stop=stop)

            def wait_source(source, c):
                name, j = turn_of(source, c)
                value = turn[name]["dve"] + j + 1
                if value > seen["source"]:
                    pe.wait_ge(turn_dve, value)
                    seen["source"] = value

            def open_turn(name):
                assert turn[name]["index"] == next_turn[0], name
                next_turn[0] += 1
                if turn[name]["index"] >= 2:
                    before = turn_list[turn[name]["index"] - 2]
                    if before["act_end"] > before["act"]:
                        pe.wait_ge(turn_act, before["act_end"])
                    if before["dve_end"] > before["dve"]:
                        pe.wait_ge(turn_dve, before["dve_end"])
                return turn_bank(name)

            def transposed(name, sources):
                bank = open_turn(name)
                for j, src in enumerate(sources):
                    last = pe.transpose(bank[:, j * P:(j + 1) * P], src, ident)
                last.then_inc(turn_filled, 1)

            def chunks_of(tile, c0, n):
                return [tile[:, tt, c * P:(c + 1) * P] for c in range(c0, c0 + n) for tt in range(TT)]

            def x_turn(v, c):
                if v == 0:
                    pe.wait_ge(x_loaded[c // 4], 16)
                elif v == 5:
                    pe.wait_ge(x_ready, x_version(4, 2 if c < 4 else 4))
                else:
                    pe.wait_ge(x_ready, x_version(v, 2 if c < 4 else 4))
                transposed(f"x{v}.{c}", chunks_of(x, c, 2))

            def open_pair(name):
                i = groups[name]["index"]
                if i >= 2:
                    before = group_list[i - 2]
                    if before["act"]:
                        pe.wait_ge(group_act, before["act_end"])
                    if before["dve"]:
                        pe.wait_ge(group_dve, before["dve_end"])
                return group_ps(name)

            def dense(name, slots=None, part=slice(None)):
                g = groups[name]
                ps = group_ps(name) if part.start else open_pair(name)
                hi, lo, c_at = OPERAND[g["source"]]
                ncols, last_c = g["ncols"], g["units"][-1][1] + g["units"][-1][2] - 1

                def unit(u):
                    k, c0, n = u
                    wait_source(g["source"], c0 + n - 1)
                    pe.wait_ge(lo_ready, k + 1)
                    for tt in range(TT):
                        for j in range(n):
                            c = c0 + j
                            cols = slice(j * ncols, (j + 1) * ncols)
                            rows = slice(tt * P, (tt + 1) * P)
                            last = product(ps[:, tt, 0:ncols], hi[:, c_at + c, rows], lo[:, c_at + c, rows],
                                           w_hi[:, k % RING, cols], w_lo[:, k % RING, cols], c == 0, c == last_c)
                    last.then_inc(unit_used, 1)
                run_group(name, unit, slots, part)

            def mlp(m, source, slots, last_slot):
                k0 = mlps[m]
                steps = FF // HALF
                h0 = m * steps * TT

                def at(value, it, per):
                    return value if it is None else it * per + value

                def up(k, it):
                    for u in range(4):
                        pe.wait_ge(lo_ready, at(k + u + 1, it, RING))
                        for tt in range(TT):
                            for j in range(2):
                                c = 2 * u + j
                                rows, cols = slice(tt * P, (tt + 1) * P), slice(j * HALF, (j + 1) * HALF)
                                slot = (k + u) % RING
                                last = product(pair[0][:, tt, :], a_hi[:, c, rows], a_lo[:, c, rows],
                                               w_hi[:, slot, cols], w_lo[:, slot, cols], c == 0, c == DC - 1)
                        last.then_inc(unit_used, 1)

                def up_first(k):
                    def products(u, tt):
                        for j in range(2):
                            c = 2 * u + j
                            rows, cols = slice(tt * P, (tt + 1) * P), slice(j * HALF, (j + 1) * HALF)
                            slot = (k + u) % RING
                            last = product(pair[0][:, tt, :], a_hi[:, c, rows], a_lo[:, c, rows],
                                           w_hi[:, slot, cols], w_lo[:, slot, cols], c == 0, c == DC - 1)
                        return last

                    for u in range(2):
                        wait_source(source, 2 * u + 1)
                        pe.wait_ge(lo_ready, k + u + 1)
                        products(u, 0)
                        products(u, 1).then_inc(unit_used, 1)
                        if u in slots:
                            slots[u]()
                    for u in range(2, 4):
                        wait_source(source, 2 * u + 1)
                        pe.wait_ge(lo_ready, k + u + 1)
                        last = products(u, 0)
                    last.then_inc(up_half, 1)
                    for u in range(2, 4):
                        products(u, 1).then_inc(unit_used, 1)
                    if 3 in slots:
                        slots[3]()

                def turn_hidden(h, it=None):
                    for tt in range(TT):
                        pe.wait_ge(hid_ready, at(h + tt + 1, it, TT))
                        for c in range(HALF // P):
                            last = pe.transpose(turn_ps[:, tt, c * P:(c + 1) * P], hid[:, tt, c * P:(c + 1) * P], ident)
                        last.then_inc(hid_turned, 1)

                def down_last(k, h):
                    pe.wait_ge(lo_ready, k + 4)
                    for n in range(2):
                        cols = slice(n * HALF, (n + 1) * HALF)
                        for tt in range(TT):
                            rows = slice(tt * P, (tt + 1) * P)
                            if n == 0:
                                pe.wait_ge(hid_lo, h + tt + 1)
                            for u in range(4):
                                slot = (k + u) % RING
                                last = product(down[n][:, tt, :], h_hi[:, u, rows], h_lo[:, u, rows],
                                               w_hi[:, slot, cols], w_lo[:, slot, cols], False, u == 3)
                                if n == 1 and tt == 1:
                                    last.then_inc(unit_used, 1)
                            if n == 0 and tt == 1:
                                last.then_inc(down_half, 1)
                            if n == 1 and tt == 0:
                                last_slot()

                def down_step(k, h, it=None):
                    pe.wait_ge(hid_lo, at(h + TT, it, TT))
                    for u in range(4):
                        pe.wait_ge(lo_ready, at(k + u + 1, it, RING))
                        for tt in range(TT):
                            rows = slice(tt * P, (tt + 1) * P)
                            for n in range(2):
                                cols = slice(n * HALF, (n + 1) * HALF)
                                slot = (k + u) % RING
                                last = product(down[n][:, tt, :], h_hi[:, u, rows], h_lo[:, u, rows],
                                               w_hi[:, slot, cols], w_lo[:, slot, cols], False, False)
                        last.then_inc(unit_used, 1)

                up_first(k0)
                for n in range(2):
                    for tt in range(TT):
                        pe.matmul(down[n][:, tt, :], zeros[:, 0:P], zeros[:, :], start=True, stop=False)
                turn_hidden(h0)
                with pe.Fori(1, steps) as i:
                    up(k0 - 4, i)
                    down_step(k0, h0 - TT, i)
                    turn_hidden(h0, i)
                down_last(k0 + 60, h0 + TT * (steps - 1))

            pe.wait_ge(const_loaded, 16)
            pe.wait_ge(gains0_loaded, 16)
            bank = open_turn("gains0")
            pe.transpose(bank[:, 0:DC], gain_rows[0:DC, :], ident[0:DC, 0:DC]).then_inc(turn_filled, 1)

            def setup_slot():
                pe.wait_ge(squares_loaded, 16)
                pe.wait_ge(gains_loaded, 16 * (len(GAIN_ROWS) - 1))
                transposed("gains", [gain_rows[:, :]])
                pe.wait_ge(set_ready, 1)
                pe.wait_ge(small_loaded, 32)
                pe.matmul(score[0:DA_H, 0, 0:3 * P - 1], table[0:BUCKETS + 1, :], onehot[0:BUCKETS + 1, :],
                          start=True, stop=True).then_inc(bias_psum, 1)

            x_turn(0, 0)
            x_turn(0, 2)
            x_turn(0, 4)

            def qk_turns(name, n):
                pe.wait_ge(group_act, groups[name]["act_end"])
                for half in range(2):
                    cols = [qk_sb[:, n, tt, (2 * half + j) * P:(2 * half + j + 1) * P]
                            for j in range(2) for tt in range(TT)]
                    transposed(f"{name}{'ab'[half]}", cols)

            def da_score(h):
                if h == 0:
                    pe.wait_ge(bias_rows_ready, 1)
                else:
                    pe.wait_ge(da_biased, h)
                pe.wait_ge(turn_act, turn["k0b" if h < 4 else "k1b"]["act_end"])
                for m in range(2):
                    rows = slice(DA_D * m, DA_D * (m + 1))
                    pe.matmul(score[:, m, WIDE], da_q[rows, h, P:S], da_k[rows, h, :], start=True, stop=True)
                    last = pe.matmul(score[:, m, TALL], da_q[rows, h, 0:P], da_k[rows, h, 0:P], start=True, stop=True)
                last.then_inc(da_scored, 1)

            def da_probs(h):
                pe.wait_ge(da_mixed, h + 1)
                transposed(f"ap{h}", [da_p[:, h, j * P:(j + 1) * P] for j in range(3)])

            def da_value(h):
                bank = open_turn(f"av{h}")
                pe.wait_ge(turn_act, turn[f"ap{h}"]["act_end"])
                pe.wait_ge(group_act, groups[f"v{h // 4}"]["act_end"])
                cols = slice(h * P, (h + 1) * P)
                pe.matmul(bank[:, 0:P], da_pt[:, h % 2, TALL], da_v[:, 0, cols], start=True, stop=True)
                pe.matmul(bank[:, P:2 * P], da_pt[:, h % 2, 0:P], da_v[:, 0, cols], start=True, stop=False)
                pe.matmul(bank[:, P:2 * P], da_pt[:, h % 2, P:2 * P], da_v[:, 1, cols], start=False, stop=True)\
                    .then_inc(turn_filled, 1)

            def da_out_turn(h):
                pe.wait_ge(da_scaled, h + 2)
                transposed(f"oT.{h}", chunks_of(da_o, h, 2))

            dense("q0", {0: lambda: x_turn(0, 6), 2: setup_slot})
            dense("k0")
            qk_turns("q0", 0)
            dense("q1", {1: lambda: qk_turns("k0", 1), 2: lambda: da_score(0), 3: lambda: da_score(1)})
            dense("k1", {0: lambda: da_score(2), 1: lambda: da_score(3), 2: lambda: qk_turns("q1", 0)})
            dense("v0", {1: lambda: qk_turns("k1", 1), 2: lambda: (da_probs(0), da_score(4)),
                         3: lambda: (da_probs(1), da_score(5))})

            def values(h):
                da_value(h)
                da_value(h + 1)

            def probs(h):
                da_probs(h)
                da_probs(h + 1)
            dense("v1", {0: lambda: (da_score(6), values(0)), 1: lambda: (probs(2), da_score(7), da_out_turn(0)),
                         2: lambda: values(2), 3: lambda: (probs(4), da_out_turn(2))})
            ao_units(dense, [lambda: values(4), lambda: (probs(6), da_out_turn(4)), lambda: values(6),
                             lambda: da_out_turn(6), None, None, lambda: (x_turn(1, 0), x_turn(1, 2)), None])
            first, second = slice(0, 2), slice(2, 4)
            mlp(0, "x1", {0: lambda: (x_turn(1, 4), x_turn(1, 6))},
                lambda: (x_turn(2, 0), x_turn(2, 2)))


            def cumulate():
                pe.wait_ge(ml_lf, 1)
                pe.matmul(score[:, 0, 0:ML_H], triu, g_lf[:, 0, :], start=True, stop=True)
                pe.matmul(score[:, 0, ML_H:2 * ML_H], ones, g_lf[:, 0, :], start=True, stop=False)
                pe.matmul(score[:, 0, ML_H:2 * ML_H], triu, g_lf[:, 1, :], start=False, stop=True).then_inc(ml_cum, 1)

            def spread(n):
                pe.wait_ge(ml_diag, n + 1)
                for j in range(2):
                    last = pe.matmul(score[:, j, :], ones, diag[:, 2 * j:2 * j + 2, :], start=True, stop=True)
                last.then_inc(ml_spread, 1)

            def conv_turn(b):
                pe.wait_ge(group_act, groups["mq" if b < 2 else "mk"]["act_end"])
                c0 = 2 * (b % 2)
                transposed(f"conv{b}", [ml_qk[:, b // 2, tt, c * P:(c + 1) * P]
                                        for c in (c0, c0 + 1) for tt in range(TT)])

            def ml_score(h):
                if h < 2:
                    pe.wait_ge(ml_wexp, ML_H)
                else:
                    pe.wait_ge(ml_weighted, h - 1)
                pe.wait_ge(ml_silu, 4)
                q, k = ml_t[:, h, :], ml_t[:, ML_H + h, :]
                pe.matmul(score[:, h % 2, WIDE], k[:, 0:P], q, start=True, stop=True)
                pe.matmul(score[:, h % 2, TALL], k[:, P:S], q[:, P:S], start=True, stop=True).then_inc(ml_scored, 1)

            def ml_value(h):
                pe.wait_ge(ml_weighted, h + 1)
                pe.wait_ge(ml_ones, 1)
                pe.wait_ge(group_act, groups["mv1"]["act_end"])
                bank = open_turn(f"mv{h}.0")
                pe.matmul(bank[:, 0:ML_V + 1], ml_s[:, h, 0:P], ml_v[:, 0, h, :], start=True, stop=True)\
                    .then_inc(turn_filled, 1)
                bank = open_turn(f"mv{h}.1")
                pe.matmul(bank[:, 0:ML_V + 1], ml_s[:, h, P:S], ml_v[:, 0, h, :], start=True, stop=False)
                pe.matmul(bank[:, 0:ML_V + 1], ml_s[:, h, TALL], ml_v[:, 1, h, :], start=False, stop=True)\
                    .then_inc(turn_filled, 1)

            dense("mq", {0: lambda: (x_turn(2, 4), x_turn(2, 6))}, slice(0, 3))
            dense("gate")
            dense("mq", None, slice(3, 4))
            dense("mk", {0: cumulate, 1: lambda: spread(0), 2: lambda: conv_turn(0), 3: lambda: conv_turn(1)})
            dense("mv0", {0: lambda: spread(1), 1: lambda: conv_turn(2), 3: lambda: conv_turn(3)})
            dense("mv1")
            dense("mo0", {0: lambda: ml_score(0), 1: lambda: ml_score(1), 2: lambda: (ml_score(2), ml_value(0)),
                          3: lambda: (ml_score(3), ml_value(1))})

            def y_turn(c):
                pe.wait_ge(ml_y, c + 2)
                transposed(f"yT.{c}", chunks_of(ml_o, c, 2))
            dense("mo1", {0: lambda: ml_value(2), 1: lambda: ml_value(3), 2: lambda: (y_turn(0), y_turn(2))})
            dense("mw0", None, first)
            dense("mw1", {0: lambda: (y_turn(4), y_turn(6))}, first)
            dense("mw0", None, second)
            dense("mw1", {2: lambda: (x_turn(3, 0), x_turn(3, 2))}, second)
            mlp(1, "x3", {0: lambda: (x_turn(3, 4), x_turn(3, 6))},
                lambda: (x_turn(5, 0), x_turn(5, 2)))


            def lat_turn(c, n):
                pe.wait_ge(group_act, groups["ckv"]["act_end"])
                transposed(f"lat.{c}", chunks_of(lat_sb, c, n))

            def ret_turn(name, half):
                pe.wait_ge(ret_roped, ("rq0", "rq1", "rk0", "rk1").index(name) + 1)
                transposed(f"{name}{'ab'[half]}", [work[:, 1, tt, (2 * half + j) * P:(2 * half + j + 1) * P]
                                                   for j in range(2) for tt in range(TT)])

            def ret_score(h):
                if h >= 2:
                    pe.wait_ge(ret_decayed, h - 1)
                pe.wait_ge(turn_dve, turn["rk1b"]["dve_end"])
                for j in range(2):
                    c = 2 * h + j
                    pe.matmul(score[:, h % 2, WIDE], rk_t[:, c, 0:P], rq_t[:, c, :], start=j == 0, stop=j == 1)
                for j in range(2):
                    c = 2 * h + j
                    last = pe.matmul(score[:, h % 2, TALL], rk_t[:, c, P:S], rq_t[:, c, P:S],
                                     start=j == 0, stop=j == 1)
                last.then_inc(ret_scored, 1)

            def ret_value(h):
                ps = open_pair(f"ret{h}")
                pe.wait_ge(ret_decayed, h + 1)
                pe.wait_ge(group_act, groups[f"rv{h}"]["act_end"])
                v = work[:, h % 2, :, :]
                pe.matmul(ps[:, 0, :], ret_s[:, h, 0:P], v[:, 0, :], start=True, stop=True)
                pe.matmul(ps[:, 1, :], ret_s[:, h, P:S], v[:, 0, :], start=True, stop=False)
                pe.matmul(ps[:, 1, :], ret_s[:, h, TALL], v[:, 1, :], start=False, stop=True).then_inc(ret_out, 1)

            def mla_turn(which, part, b):
                tile, ready = (lq_sb, lq_ready) if which == "mq" else (kv, lk_ready)
                pe.wait_ge(ready, 1 if (which, part) == ("mk", "n") else 2)
                if part == "n":
                    src = [tile[:, tt, 2 * b + j, 0:NOPE] for j in range(2) for tt in range(TT)]
                else:
                    src = [rot[:, tt, 4 * b + 2 * j:4 * b + 2 * j + 2, :] for j in range(2) for tt in range(TT)]
                transposed(f"{which}{part}{b}", src)

            def mla_score(h):
                if h >= 2:
                    pe.wait_ge(l_masked, h - 1)
                else:
                    pe.wait_ge(ret_decayed, RET_H)
                pe.wait_ge(turn_act, turn["mkn3"]["act_end"])
                pe.wait_ge(turn_dve, turn["mkr1"]["dve_end"])
                rows = slice(ROPE * (h % 2), ROPE * (h % 2 + 1))
                for cols, q, k in ((WIDE, slice(P, S), slice(0, S)), (TALL, slice(0, P), slice(0, P))):
                    o = score[:, h % 2, cols]
                    pe.matmul(o, lq_n[:, h, q], lk_n[:, h, k], start=True, stop=False)
                    last = pe.matmul(o, lq_t[rows, h // 2, q], lk_t[rows, h // 2, k], start=False, stop=True)
                last.then_inc(l_scored, 1)

            def mla_probs(h):
                pe.wait_ge(l_exped, h + 1)
                transposed(f"lp{h}", [l_e[:, h % 2, j * P:(j + 1) * P] for j in range(3)])

            def mla_value(h):
                bank = open_turn(f"lv{h}")
                pe.wait_ge(turn_act, turn[f"lp{h}"]["act_end"])
                v = [kv[:, tt, h, NOPE:] for tt in range(TT)]
                pe.matmul(bank[:, 0:P], l_pt[:, h % 2, TALL], v[0], start=True, stop=True)
                pe.matmul(bank[:, P:S], l_pt[:, h % 2, 0:P], v[0], start=True, stop=False)
                pe.matmul(bank[:, P:S], l_pt[:, h % 2, P:S], v[1], start=False, stop=True).then_inc(turn_filled, 1)

            def mla_slot(n):
                if n < MLA_H:
                    mla_score(n)
                if n >= 2:
                    mla_value(n - 2)
                if 1 <= n <= MLA_H:
                    mla_probs(n - 1)

            dense("cq", {1: lambda: (x_turn(5, 4), x_turn(5, 6))}, first)
            dense("ckv", None, first)
            dense("cq", None, second)
            dense("ckv", None, second)
            dense("rq0", {1: lambda: lat_turn(0, 2), 2: lambda: lat_turn(2, 2), 3: lambda: lat_turn(4, 1)})
            dense("rq1", {2: lambda: ret_turn("rq0", 0), 3: lambda: ret_turn("rq0", 1)})
            dense("rk0", {2: lambda: ret_turn("rq1", 0), 3: lambda: ret_turn("rq1", 1)})
            dense("rk1", {2: lambda: ret_turn("rk0", 0), 3: lambda: ret_turn("rk0", 1)})
            dense("uq0")
            dense("uq1", {1: lambda: ret_turn("rk1", 0)})
            dense("uq2", {1: lambda: ret_turn("rk1", 1)})
            for n in range(4):
                dense(f"ukv{n}")
                ret_score(n)
            dense("rv0")
            dense("rv1")
            ret_value(0)

            def turns_q(n):
                mla_turn("mq", "n", n)

            def turns_k(n):
                if n == 0:
                    mla_turn("mq", "r", 0)
                    mla_turn("mq", "r", 1)
                mla_turn("mk", "n", n)
            dense("rv2", {n: (lambda n=n: turns_q(n)) for n in range(4)})
            ret_value(1)
            dense("rv3", {n: (lambda n=n: turns_k(n)) for n in range(4)})
            ret_value(2)
            dense("rg0", {0: lambda: mla_turn("mk", "r", 0), 1: lambda: mla_turn("mk", "r", 1)})
            ret_value(3)
            dense("rg1", {n: (lambda n=n: mla_slot(n)) for n in range(4)})
            dense("rg2", {n: (lambda n=n: mla_slot(4 + n)) for n in range(4)})
            dense("rg3", {0: lambda: mla_slot(8), 1: lambda: mla_slot(9)})

            def ro_turn(c):
                pe.wait_ge(gated, c // 4 + 1)
                transposed(f"roT.{c}", chunks_of(ret, c, 2))
            dense("gm0", {n: (lambda n=n: ro_turn(2 * n)) for n in range(4)})
            dense("gm1", {n: (lambda n=n: ro_turn(8 + 2 * n)) for n in range(4)})
            dense("gr0")
            dense("gr1")

            def mo_turn(c):
                pe.wait_ge(turn_act, turn["lv7"]["act_end"])
                transposed(f"moT.{c}", chunks_of(lo_sb, c, 2))
            dense("br0", {2 * n + 1: (lambda n=n: mo_turn(2 * n)) for n in range(4)})
            dense("br1")
            dense("bm0")

            def mix_turn(c):
                pe.wait_ge(mixed, 2 * (c // 4) + 2)
                transposed(f"mixT.{c}", chunks_of(mix, c, 2))
            dense("bm1", {2: lambda: mix_turn(0), 3: lambda: mix_turn(2)})
            dense("wo0", {1: lambda: (mix_turn(4), mix_turn(6))}, first)
            dense("wo1", None, slice(0, 1))
            dense("wo0", None, second)
            dense("wo1", {2: lambda: (x_turn(6, 0), x_turn(6, 2))}, slice(1, 4))

            def p_turn():
                pe.wait_ge(p_loaded, 16 * TT)
                transposed("pT.0", chunks_of(p_sb, 0, 2))
            mlp(2, "x6", {0: lambda: (x_turn(6, 4), x_turn(6, 6)), 3: p_turn},
                lambda: (x_turn(7, 0), x_turn(7, 2)))

            for n in range(2):
                pe.wait_ge(x_ready, x_version(7, 2))
                dense(f"pl{n}")
            dense("pg0", {0: lambda: (x_turn(7, 4), x_turn(7, 6))})
            dense("pg1")

        @block.scalar
        def _(act):
            mark, own = own_order(act, act_step)
            sizes = {item[1]: item[3] * item[4] for item in stream if item[0] == "unit"}
            split_to = [0]
            junk_free = [None]

            def square_sum(src, total, cols, done, value):
                if junk_free[0]:
                    act.wait_ge(*junk_free[0])
                junk_free[0] = (done, value)
                act.activation(junk[:, cols], src, ACT.Square, accum_out=total).then_inc(done, 1)

            def split_unit(k, it=None):
                if it is not None or k >= RING:
                    used = k - RING + 1
                    act.wait_ge(unit_used, used if it is None else it * RING + used)
                land = 16 * (k // RING + 1)
                act.wait_ge(landed[k % RING], land if it is None else it * 16 + land)
                n = sizes.get(k, UNIT) if it is None else UNIT
                act.activation(w_hi[:, k % RING, 0:n], raw[:, k % RING, 0:n], ACT.Copy).then_inc(hi_ready, 1)

            def split_until(k):
                while split_to[0] <= min(k, total_units - 1):
                    split_unit(split_to[0])
                    split_to[0] += 1

            def split_turn(name):
                wait_turn(act, name)
                for src, hi, _, scale in split_parts(name):
                    if scale is None:
                        act.activation(hi, src, ACT.Copy).then_inc(turn_act, 1)
                    else:
                        act.activation(hi, src, ACT.Copy, scale=scale).then_inc(turn_act, 1)

            first, second = slice(0, 2), slice(2, 4)

            def x_squares(v):
                if v == 0:
                    for half in x_loaded:
                        act.wait_ge(half, 16)
                elif v == 5:
                    act.wait_ge(gained_ready, 4)
                else:
                    act.wait_ge(x_ready, x_version(v))
                for tt in range(TT):
                    square_sum((gained if v == 5 else x)[:, tt, :], ssx[:, v, tt:tt + 1], slice(0, D), x_squared,
                               TT * (v - (v > 4)) + tt + 1)

            def dense(name, slots=None, part=slice(None), ahead=AHEAD):
                run_group(name, lambda u: split_until(u[0] + ahead), slots, part)

            def empty(name, outs, func=ACT.Copy, scales=None):
                wait_group(act, name)
                for tt in range(TT):
                    ps = group_ps(name)[:, tt, 0:groups[name]["ncols"]]
                    ps = ps if len(outs[tt].shape) == 2 else ps.rearrange("p (a b) -> p a b", a=outs[tt].shape[1])
                    if scales is None:
                        act.activation(outs[tt], ps, func).then_inc(group_act, 1)
                    else:
                        act.activation(outs[tt], ps, func, scale=scales[tt]).then_inc(group_act, 1)

            def row_norm(v):
                return [rstd[:, v, tt:tt + 1] for tt in range(TT)]

            def mlp(m, meanwhile=None):
                k0, steps = mlps[m], FF // HALF
                h0 = m * steps * TT

                def at(value, it, per):
                    return value if it is None else it * per + value

                def step(k, h, it=None):
                    for tt in range(TT):
                        if it is None and k == k0 and tt == 0:
                            act.wait_ge(up_half, m + 1)
                        else:
                            act.wait_ge(unit_used, at(k + 4, it, RING))
                        act.activation(relu[:, tt, :], pair[0][:, tt, :], ACT.Relu).then_inc(up_relu, 1)
                        if it is None and k == k0 and tt == 0 and meanwhile:
                            meanwhile()
                    for u in range(4):
                        split_unit(k + 8 + u, it)
                    for tt in range(TT):
                        act.wait_ge(hid_turned, at(h + tt + 1, it, TT))
                        act.activation(h_hi[:, :, tt * P:(tt + 1) * P],
                                       turn_ps[:, tt, :].rearrange("p (c s) -> p c s", s=P), ACT.Copy)\
                            .then_inc(hid_hi, 1)

                def step_tail(k, it=None):
                    for u in range(4):
                        split_unit(k + 12 + u, it)

                split_until(k0 + 7)
                step(k0, h0)
                with act.Fori(1, steps - 1) as i:
                    step(k0 - 4, h0, i)
                    step_tail(k0 - 4, i)
                step(k0 + 4 + RING * (steps - 2), h0 + TT * (steps - 1))
                split_to[0] = k0 + 8 * steps

            act.dma_start(gain_rows[0:DC, :], gain_source(GAIN_ROWS[0][0])).then_inc(gains0_loaded, 16)
            act.dma_start(square[:, 0, :], w["c_square"][:, 0, :]).then_inc(const_loaded, 16)
            wait_turn(act, "gains0")
            act.activation(gains[:, 0:DC], turn_bank("gains0")[:, 0:DC], ACT.Copy).then_inc(turn_act, 1)
            act.wait_ge(turn_act, 1)
            split_turn("x0.0")
            split_until(0)
            split_turn("x0.2")
            split_until(1)

            def setup_slot():
                wait_turn(act, "gains")
                act.activation(gains[:, DC:], turn_bank("gains")[:, DC:P], ACT.Copy).then_inc(turn_act, 1)
                act.wait_ge(turn_act, turn["gains"]["act_end"])
                act.wait_ge(lam_sum, 1)
                act.activation(lam_e[:, :], lam_s[:, :], ACT.Exp).then_inc(lam_exp, 1)

            def angle_slot():
                act.wait_ge(angles_ready, 1)
                act.activation(trig[:, :, :, :], ang[:, :, :, :], ACT.Sin).then_inc(trig_ready, 1)

            def da_exp(h):
                act.wait_ge(da_maxed, h + 1)
                b = h % 2
                for j, cols in enumerate((WIDE, TALL)):
                    for m in range(2):
                        i = 2 * j + m
                        last = act.activation(da_e[:, b, m, cols], da_e[:, b, m, cols], ACT.Exp,
                                              bias=da_nm[:, b, i:i + 1], accum_out=da_sum[:, b, i:i + 1])
                last.then_inc(da_exped, 1)

            def da_probs(h):
                wait_turn(act, f"ap{h}")
                act.activation(da_pt[:, h % 2, :], turn_bank(f"ap{h}")[:, 0:SCORE], ACT.Copy).then_inc(turn_act, 1)

            def da_value(h):
                wait_turn(act, f"av{h}")
                for tt in range(TT):
                    square_sum(turn_bank(f"av{h}")[:, tt * P:(tt + 1) * P], da_ss[:, h // 2, tt, h % 2:h % 2 + 1],
                               slice(0, P), turn_act, turn[f"av{h}"]["act"] + tt + 1)

            empty_qk = lambda name, n: empty(name, [qk_sb[:, n, tt, :] for tt in range(TT)], scales=row_norm(0))
            def copy_heads(name, dst, h0):
                for half in range(2):
                    turn_name = f"{name}{'ab'[half]}"
                    wait_turn(act, turn_name)
                    act.activation(dst[:, h0 + 2 * half:h0 + 2 * half + 2, :],
                                   turn_bank(turn_name).rearrange("p (h s) -> p h s", h=2), ACT.Copy)\
                        .then_inc(turn_act, 1)

            split_turn("x0.4")
            dense("q0", {0: lambda: split_turn("x0.6"), 1: lambda: x_squares(0), 2: setup_slot}, ahead=AHEAD_0)
            act.wait_ge(rstd_ready, 1)
            empty_qk("q0", 0)
            dense("k0")
            empty_qk("k0", 1)
            copy_heads("q0", da_q, 0)
            dense("q1", {1: lambda: copy_heads("k0", da_k, 0), 3: lambda: da_exp(0)})
            wait_turn(act, "q0b")
            empty_qk("q1", 0)
            dense("k1", {0: lambda: da_exp(1), 1: lambda: da_exp(2),
                         2: lambda: (copy_heads("q1", da_q, 4), da_exp(3))})
            wait_turn(act, "k0b")
            empty_qk("k1", 1)
            dense("v0", {0: angle_slot, 1: lambda: copy_heads("k1", da_k, 4), 2: lambda: da_probs(0),
                         3: lambda: (da_exp(4), da_probs(1))})
            empty("v0", [da_v[:, tt, 0:HALF] for tt in range(TT)], scales=row_norm(0))

            def values(h):
                da_value(h)
                da_value(h + 1)

            def probs(h):
                da_probs(h)
                da_probs(h + 1)
            dense("v1", {0: lambda: (da_exp(5), values(0)), 1: lambda: (probs(2), da_exp(6), split_turn("oT.0")),
                         2: lambda: (da_exp(7), values(2)), 3: lambda: (probs(4), split_turn("oT.2"))})
            empty("v1", [da_v[:, tt, HALF:D] for tt in range(TT)], scales=row_norm(0))
            ao_units(dense, [lambda: values(4), lambda: (probs(6), split_turn("oT.4")), lambda: values(6),
                             lambda: split_turn("oT.6"), None, None,
                             lambda: (split_turn("x1.0"), split_turn("x1.2")), None])
            split_turn("x1.4")
            split_turn("x1.6")
            x_squares(1)
            mlp(0)

            split_until(groups["mq"]["units"][0][0] + 2)
            split_turn("x2.0")
            split_turn("x2.2")
            dense("mq", {0: lambda: (split_turn("x2.4"), split_turn("x2.6")), 2: lambda: x_squares(2)},
                  slice(0, 3), AHEAD_0)
            dense("gate")
            act.wait_ge(rstd_ready, 3)
            empty("gate", [gate_in[:, tt, :] for tt in range(TT)], scales=row_norm(2))

            def gate_log():
                act.wait_ge(ml_abs, 1)
                mark(act.activation(g_exp, g_abs, ACT.Exp, scale=-1.0))
                own()
                act.activation(g_ln, g_exp, ACT.Ln, bias=1.0).then_inc(ml_ln, 1)

            def weights():
                act.wait_ge(ml_args, 2)
                for h in range(ML_H):
                    g0, g1 = g_g[:, 0, h:h + 1], g_g[:, 1, h:h + 1]
                    spread = score[:, h // 2, :].rearrange("p (h s) -> p h s", h=2)[:, h % 2, :]
                    act.activation(ml_w[:, h, 0:P], ml_w[:, h, 0:P], ACT.Exp, bias=g0)
                    act.activation(ml_w[:, h, P:S], spread[:, P:S], ACT.Exp, bias=g0, scale=-1.0)
                    act.activation(ml_w[:, h, TALL], ml_w[:, h, TALL], ACT.Exp, bias=g1).then_inc(ml_wexp, 1)
                act.activation(g_em, g_nm, ACT.Exp, scale=-1.0).then_inc(ml_em, 1)

            def convolve(b):
                wait_turn(act, f"conv{b}")
                for j in range(2):
                    c = 2 * b + j
                    act.activation(ml_t[:, c, :], turn_bank(f"conv{b}")[:, j * S:(j + 1) * S], ACT.Identity,
                                   scale=gain("mlstm_conv_w", (CONV - 1) * DC + c), bias=gain("mlstm_conv_b", c))\
                        .then_inc(turn_act, 1)

            def silu(b):
                act.wait_ge(turn_dve, turn[f"conv{b}"]["dve_end"])
                two = ml_t[:, 2 * b:2 * b + 2, :]
                act.activation(two, two, ACT.Silu).then_inc(ml_silu, 1)

            def ml_square(h):
                for tt in range(TT):
                    name = f"mv{h}.{tt}"
                    wait_turn(act, name)
                    act.activation(ml_n[:, tt, h, :], turn_bank(name)[:, 0:ML_V + 1], ACT.Copy).then_inc(turn_act, 1)
                    square_sum(turn_bank(name)[:, 0:ML_V], r_ss[:, tt, h:h + 1], slice(0, ML_V), turn_act,
                               turn[name]["act_end"])

            dense("mq", {3: gate_log}, slice(3, 4))
            empty("mq", [ml_qk[:, 0, tt, :] for tt in range(TT)], scales=row_norm(2))
            dense("mk", {2: lambda: convolve(0), 3: lambda: convolve(1)})
            empty("mk", [ml_qk[:, 1, tt, :] for tt in range(TT)], scales=row_norm(2))
            dense("mv0", {1: lambda: (convolve(2), weights()), 3: lambda: (convolve(3), silu(0), silu(1))})
            act.wait_ge(ml_ones, 1)
            half_v = lambda n: [ml_v[:, tt, 2 * n:2 * n + 2, 0:ML_V] for tt in range(TT)]
            empty("mv0", half_v(0), scales=row_norm(2))
            dense("mv1", {0: lambda: silu(2), 1: lambda: silu(3)})
            empty("mv1", half_v(1), scales=row_norm(2))
            dense("mo0", {2: lambda: ml_square(0), 3: lambda: ml_square(1)})
            empty("mo0", [ml_o[:, tt, 0:HALF] for tt in range(TT)], ACT.Sigmoid, row_norm(2))
            dense("mo1", {0: lambda: ml_square(2), 1: lambda: ml_square(3),
                          2: lambda: (split_turn("yT.0"), split_turn("yT.2"))})
            empty("mo1", [ml_o[:, tt, HALF:D] for tt in range(TT)], ACT.Sigmoid, row_norm(2))
            dense("mw0", None, first)
            dense("mw1", {0: lambda: (split_turn("yT.4"), split_turn("yT.6"))}, first)
            dense("mw0", None, second)
            dense("mw1", {2: lambda: (split_turn("x3.0"), split_turn("x3.2"))}, second)
            split_turn("x3.4")
            split_turn("x3.6")
            x_squares(3)
            mlp(1)

            split_until(groups["cq"]["units"][0][0] + 3)
            split_turn("x5.0")
            split_turn("x5.2")
            dense("cq", {1: lambda: (split_turn("x5.4"), split_turn("x5.6"))}, first)
            dense("ckv", None, first)
            dense("cq", {2: lambda: x_squares(5)}, second)

            def empty_cq():
                act.wait_ge(rstd_ready, 6)
                empty("cq", [lat_sb[:, tt, 0:Q_LORA] for tt in range(TT)], scales=row_norm(5))
            dense("ckv", {2: empty_cq}, second, AHEAD - 1)
            empty("ckv", [lat_sb[:, tt, Q_LORA:] for tt in range(TT)], scales=row_norm(5))

            def lat_squares():
                act.wait_ge(group_act, groups["ckv"]["act_end"])
                for tt in range(TT):
                    for n, cols in enumerate((slice(0, Q_LORA), slice(Q_LORA, LAT))):
                        square_sum(lat_sb[:, tt, cols], lat_ss[:, n, tt:tt + 1], cols, lat_sq, 2 * tt + n + 1)

            def empty_rope(name):
                n = ("rq0", "rq1", "rk0", "rk1").index(name)
                if n:
                    act.wait_ge(ret_roped, n)
                empty(name, [work[:, 0, tt, :] for tt in range(TT)], scales=row_norm(5))

            def mla_copy(which, b):
                name = f"{which}n{b}"
                wait_turn(act, name)
                dst = (lq_n if which == "mq" else lk_n)[:, 2 * b:2 * b + 2, :]
                act.activation(dst, turn_bank(name).rearrange("p (h s) -> p h s", h=2), ACT.Copy,
                               scale=gain("q_norm_2" if which == "mq" else "k_norm_2", 0)).then_inc(turn_act, 1)

            def ret_squares(h):
                act.wait_ge(ret_out, h + 1)
                ps = group_ps(f"ret{h}")
                for tt in range(TT):
                    square_sum(ps[:, tt, :], ret_ss[:, tt, h:h + 1], slice(0, HALF), group_act,
                               groups[f"ret{h}"]["act_end"] - 1 + tt)

            def mla_exp(h):
                act.wait_ge(l_maxed, h + 1)
                b = h % 2
                for j, cols in enumerate((WIDE, TALL)):
                    last = act.activation(l_e[:, b, cols], l_e[:, b, cols], ACT.Exp, bias=l_nm[:, b, j:j + 1],
                                          accum_out=l_sum[:, b, j:j + 1])
                last.then_inc(l_exped, 1)

            def mla_probs(h):
                wait_turn(act, f"lp{h}")
                act.activation(l_pt[:, h % 2, :], turn_bank(f"lp{h}")[:, 0:SCORE], ACT.Copy).then_inc(turn_act, 1)

            def mla_value(h):
                wait_turn(act, f"lv{h}")
                act.wait_ge(l_reced, h + 1)
                for tt in range(TT):
                    act.activation(lo_sb[:, tt, h * P:(h + 1) * P], turn_bank(f"lv{h}")[:, tt * P:(tt + 1) * P],
                                   ACT.Copy, scale=l_rec[:, h % 2, 1 - tt:2 - tt]).then_inc(turn_act, 1)

            def mla_slot(n):
                if 1 <= n <= MLA_H:
                    mla_exp(n - 1)
                if n >= 2:
                    mla_value(n - 2)
                if 1 <= n <= MLA_H:
                    mla_probs(n - 1)

            dense("rq0", {0: lat_squares, 1: lambda: split_turn("lat.0"), 2: lambda: split_turn("lat.2"),
                          3: lambda: split_turn("lat.4")})
            empty_rope("rq0")
            dense("rq1")
            empty_rope("rq1")
            dense("rk0")
            empty_rope("rk0")
            dense("rk1")
            empty_rope("rk1")
            act.wait_ge(lat_norm, 1)
            for n in range(3):
                dense(f"uq{n}")
                empty(f"uq{n}", [flat_q[:, tt * MLA_H * MLA_QK + n * HALF:tt * MLA_H * MLA_QK + (n + 1) * HALF]
                                 for tt in range(TT)], scales=[lat_r[:, 0, tt:tt + 1] for tt in range(TT)])
            for n in range(4):
                dense(f"ukv{n}")
                empty(f"ukv{n}", [kv[:, tt, 2 * n:2 * n + 2, :] for tt in range(TT)],
                      scales=[lat_r[:, 1, tt:tt + 1] for tt in range(TT)])

            def empty_value(n):
                if n == 0:
                    wait_turn(act, "rk1b")
                elif n >= 2:
                    act.wait_ge(ret_out, n - 1)
                else:
                    wait_turn(act, "rk1b")
                empty(f"rv{n}", [work[:, n % 2, tt, :] for tt in range(TT)], scales=row_norm(5))

            def empty_gate(n):
                act.wait_ge(ret_out, 3 if n == 0 else 4)
                if n >= 2:
                    act.wait_ge(gated, n - 1)
                empty(f"rg{n}", [work[:, n % 2, tt, :] for tt in range(TT)], ACT.Silu, row_norm(5))

            dense("rv0")
            empty_value(0)
            dense("rv1")
            empty_value(1)
            ret_squares(0)

            dense("rv2", {n: (lambda n=n: mla_copy("mq", n)) for n in range(4)})
            empty_value(2)
            ret_squares(1)
            dense("rv3", {n: (lambda n=n: mla_copy("mk", n)) for n in range(4)})
            empty_value(3)
            ret_squares(2)
            dense("rg0")
            empty_gate(0)
            ret_squares(3)
            dense("rg1", {n: (lambda n=n: mla_slot(n)) for n in range(4)})
            empty_gate(1)
            dense("rg2", {n: (lambda n=n: mla_slot(4 + n)) for n in range(4)})
            empty_gate(2)
            dense("rg3", {0: lambda: mla_slot(8), 1: lambda: mla_slot(9)})
            empty_gate(3)
            dense("gm0", {n: (lambda n=n: split_turn(f"roT.{2 * n}")) for n in range(4)})
            empty("gm0", [gm[:, tt, 0:HALF] for tt in range(TT)], ACT.Sigmoid, row_norm(5))
            dense("gm1", {n: (lambda n=n: split_turn(f"roT.{8 + 2 * n}")) for n in range(4)})
            empty("gm1", [gm[:, tt, HALF:D] for tt in range(TT)], ACT.Sigmoid, row_norm(5))
            dense("gr0")
            empty("gr0", [gr[:, tt, 0:HALF] for tt in range(TT)], ACT.Sigmoid, row_norm(5))
            dense("gr1")
            empty("gr1", [gr[:, tt, HALF:D] for tt in range(TT)], ACT.Sigmoid, row_norm(5))
            dense("br0", {2 * n + 1: (lambda n=n: split_turn(f"moT.{2 * n}")) for n in range(4)})
            dense("br1")
            dense("bm0")
            dense("bm1", {2: lambda: split_turn("mixT.0"), 3: lambda: split_turn("mixT.2")})
            dense("wo0", {1: lambda: (split_turn("mixT.4"), split_turn("mixT.6"))}, first)
            dense("wo1", None, slice(0, 1))
            dense("wo0", None, second)
            dense("wo1", {2: lambda: (split_turn("x6.0"), split_turn("x6.2"))}, slice(1, 4))
            split_turn("x6.4")
            split_turn("x6.6")
            x_squares(6)
            mlp(2, lambda: split_turn("pT.0"))

            split_until(groups["pl0"]["units"][0][0] + 3)
            split_turn("x7.0")
            split_turn("x7.2")
            for n in range(2):
                cols = slice(n * HALF, (n + 1) * HALF)
                dense(f"pl{n}", ahead=AHEAD - 2 + n)
                empty(f"pl{n}", [ple[:, tt, cols] for tt in range(TT)])
            for n in range(2):
                cols = slice(n * HALF, (n + 1) * HALF)
                if n == 0:
                    dense("pg0", {0: lambda: (split_turn("x7.4"), split_turn("x7.6")), 2: lambda: x_squares(7)})
                    act.wait_ge(rstd_ready, 8)
                else:
                    dense("pg1")
                empty(f"pg{n}", [gate[:, tt, cols] for tt in range(TT)], ACT.Sigmoid, row_norm(7))

        @block.vector
        def _(dve):
            mark, own = own_order(dve, dve_step)
            sizes = {item[1]: item[3] * item[4] for item in stream if item[0] == "unit"}
            split_to = [0]

            def split_unit(k, it=None):
                dve.wait_ge(hi_ready, k + 1 if it is None else it * RING + (k + 1))
                n = sizes.get(k, UNIT) if it is None else UNIT
                dve.tensor_tensor(w_lo[:, k % RING, 0:n], raw[:, k % RING, 0:n], w_hi[:, k % RING, 0:n],
                                  ALU.subtract).then_inc(lo_ready, 1)

            def split_until(k):
                while split_to[0] <= min(k, total_units - 1):
                    split_unit(split_to[0])
                    split_to[0] += 1

            def dense(name, slots=None, part=slice(None), ahead=AHEAD):
                run_group(name, lambda u: split_until(u[0] + ahead), slots, part)

            def split_turn(name):
                dve.wait_ge(turn_act, turn[name]["act_end"])
                for src, hi, lo, scale in split_parts(name):
                    if scale is None:
                        dve.tensor_tensor(lo, src, hi, ALU.subtract).then_inc(turn_dve, 1)
                    else:
                        dve.scalar_tensor_tensor(lo, src, scale, hi.bitcast(F32), ALU.mult, ALU.subtract)\
                            .then_inc(turn_dve, 1)

            def copy_turn(name, dst, src):
                if turn[name]["act_end"] > turn[name]["act"]:
                    dve.wait_ge(turn_act, turn[name]["act_end"])
                else:
                    wait_turn(dve, name)
                dve.tensor_copy(dst, src).then_inc(turn_dve, 1)

            def invert(v):
                dve.wait_ge(rstd_ready, v + 1)
                dve.reciprocal(inv_ms[:, v, :], msx[:, v, :]).then_inc(inv_ready, 1)

            first, second = slice(0, 2), slice(2, 4)

            def mlp(m, v, meanwhile=None):
                k0, steps = mlps[m], FF // HALF
                h0 = m * steps * TT

                def at(value, it, per):
                    return value if it is None else it * per + value

                def step(k, h, it=None):
                    for tt in range(TT):
                        dve.wait_ge(up_relu, at(h + tt + 1, it, TT))
                        dve.scalar_tensor_tensor(hid[:, tt, :], pair[0][:, tt, :], 0.0, relu[:, tt, :],
                                                 ALU.max, ALU.mult).then_inc(hid_ready, 1)
                        if it is None and k == k0 and tt == 0 and meanwhile:
                            meanwhile()
                    for u in range(4):
                        split_unit(k + 8 + u, it)
                    for tt in range(TT):
                        dve.wait_ge(hid_hi, at(h + tt + 1, it, TT))
                        rows = slice(tt * P, (tt + 1) * P)
                        dve.tensor_tensor(h_lo[:, :, rows], turn_ps[:, tt, :].rearrange("p (c s) -> p c s", s=P),
                                          h_hi[:, :, rows], ALU.subtract).then_inc(hid_lo, 1)

                def step_tail(k, it=None):
                    for u in range(4):
                        split_unit(k + 12 + u, it)

                split_until(k0 + 7)
                step(k0, h0)
                invert(v)
                with dve.Fori(1, steps - 1) as i:
                    step(k0 - 4, h0, i)
                    step_tail(k0 - 4, i)
                step(k0 + 4 + RING * (steps - 2), h0 + TT * (steps - 1))
                split_to[0] = k0 + 8 * steps
                split_until(k0 + 8 * steps + 2)
                dve.wait_ge(inv_ready, m + 1)

            def mlp_out(m, v, n):
                if n == 0:
                    dve.wait_ge(down_half, m + 1)
                else:
                    dve.wait_ge(unit_used, mlps[m] + 8 * (FF // HALF))
                cols = slice(n * HALF, (n + 1) * HALF)
                for tt in range(TT):
                    dve.scalar_tensor_tensor(x[:, tt, cols], down[n][:, tt, :], inv_ms[:, v, tt:tt + 1],
                                             x[:, tt, cols], ALU.mult, ALU.add).then_inc(x_ready, 1)

            def mlp_end(m, v, turns_of):
                for n in range(2):
                    mlp_out(m, v, n)
                    if n == 0:
                        split_turn(f"{turns_of}.0")
                        split_turn(f"{turns_of}.2")

            def add_to_x(name, n):
                wait_group(dve, name)
                cols = slice(n * HALF, (n + 1) * HALF)
                for tt in range(TT):
                    dve.tensor_tensor(x[:, tt, cols], x[:, tt, cols], group_ps(name)[:, tt, :], ALU.add)\
                        .then_inc(x_ready, 1)

            def rotate(o1, o2, t1, t2, x1, x2, cos, sin):
                mark(dve.tensor_tensor(o1, x1, cos, ALU.mult))
                n = mark(dve.tensor_tensor(t1, x2, sin, ALU.mult))
                mark(dve.tensor_tensor(o2, x2, cos, ALU.mult))
                mark(dve.tensor_tensor(t2, x1, sin, ALU.mult))
                own(n)
                mark(dve.tensor_tensor(o1, o1, t1, ALU.subtract))
                own()
                return dve.tensor_tensor(o2, o2, t2, ALU.add)

            def spread_to(ap, axis, shape):
                return ap.unsqueeze(axis).to_broadcast([P, *shape])

            split_turn("x0.0")
            split_until(0)
            split_turn("x0.2")
            split_until(1)

            def setup_slot():
                dve.wait_ge(lam_loaded, 64)
                mark(dve.tensor_tensor(lam_prod[:, :, :], lam_in[:, 0::2, :], lam_in[:, 1::2, :], ALU.mult))
                own()
                dve.tensor_reduce(lam_s[:, :], lam_prod[:, :, :], AXIS, ALU.add).then_inc(lam_sum, 1)
                dve.wait_ge(fgain_t_loaded, 16)
                dve.wait_ge(turn_act, turn["gains"]["act_end"])
                two_norms = gains[:, GAIN["norm_mix_2"]:GAIN["norm_mix_2"] + DC]
                mark(dve.tensor_tensor(two_norms, two_norms, fgain_t[:, :], ALU.mult))
                dve.wait_ge(bias_psum, 1)
                dve.tensor_copy(bias_rows[0:DA_H, :], score[0:DA_H, 0, 0:3 * P - 1]).then_inc(bias_rows_ready, 1)
                dve.wait_ge(lam_exp, 1)
                mark(dve.scalar_tensor_tensor(neg_lam[:, :], lam_e[:, 1:2], LAMBDA_INIT, lam_e[:, 0:1],
                                              ALU.subtract, ALU.subtract))

            k_flat = turns_k[:, :, :, :].rearrange("p a t n -> p (a t n)")
            a_flat = ang[:, :, :, :].rearrange("p a t n -> p (a t n)")

            def angles():
                dve.wait_ge(pos_loaded, 32)
                mark(dve.tensor_copy(pos_f[:, :], pos_i[:, :]))
                own()
                for a in range(2):
                    for tt in range(TT):
                        mark(dve.tensor_scalar(ang[:, a, tt, :], inv[:, :], pos_f[:, tt:tt + 1], None, ALU.mult))
                own()
                for a in range(2):
                    mark(dve.tensor_scalar(turns_k[:, a, :, :], ang[:, a, :, :], 1 / TWO_PI, 0.25 * a,
                                           ALU.mult, ALU.add))
                for step in (ROUND, -ROUND):
                    own()
                    mark(dve.tensor_scalar(turns_k[:, :, :, :], turns_k[:, :, :, :], step, None, ALU.add))

            def reduced_angles():
                for part in (PI_A, PI_B, PI_C):
                    own()
                    mark(dve.scalar_tensor_tensor(a_flat, k_flat, -part, a_flat, ALU.mult, ALU.add))
                own()
                mark(dve.tensor_scalar(ang[:, 1, :, :], ang[:, 1, :, :], TWO_PI / 4, None, ALU.add))
                own()
                dve.tensor_scalar(a_flat, a_flat, PI_SAFE, -PI_SAFE, ALU.min, ALU.max).then_inc(angles_ready, 1)

            def da_logits(h):
                dve.wait_ge(da_scored, h + 1)
                b = h % 2
                if h >= 2:
                    dve.wait_ge(da_mixed, h - 1)
                dve.scalar_tensor_tensor(da_e[:, b, :, :], score[:, :, 0:SCORE], DA_D ** -0.5,
                                         spread_to(bias[:, h, :], 1, [2, SCORE]), ALU.mult, ALU.add)\
                    .then_inc(da_biased, 1)

            def da_maxima(h):
                dve.wait_ge(da_biased, h + 1)
                b = h % 2
                for j, cols in enumerate((WIDE, TALL)):
                    last = dve.tensor_reduce(da_nm[:, b, 2 * j:2 * j + 2], da_e[:, b, :, cols], AXIS, ALU.max,
                                             negate=True)
                last.then_inc(da_maxed, 1)

            def da_factors(h):
                dve.wait_ge(da_exped, h + 1)
                b = h % 2
                mark(dve.reciprocal(da_rec[:, b, :], da_sum[:, b, :]))
                own()
                mark(dve.tensor_scalar(da_nl[:, b, :], da_rec[:, b, 1::2], neg_lam[:, 0:1], None, ALU.mult))

            def da_mix(h):
                own()
                b = h % 2
                scaled = [mark(dve.tensor_scalar(da_e[:, b, 1, cols], da_e[:, b, 1, cols], da_nl[:, b, j:j + 1], None,
                                                 ALU.mult)) for j, cols in enumerate((WIDE, TALL))]
                for j, cols in enumerate((WIDE, TALL)):
                    own(scaled[j])
                    last = dve.scalar_tensor_tensor(da_p[:, h, cols], da_e[:, b, 0, cols],
                                                    da_rec[:, b, 2 * j:2 * j + 1], da_e[:, b, 1, cols],
                                                    ALU.mult, ALU.add)
                last.then_inc(da_mixed, 1)

            def da_head(h, between=None):
                if h < DA_H:
                    da_logits(h)
                if h:
                    da_factors(h - 1)
                if h < DA_H:
                    da_maxima(h)
                if between:
                    between()
                if h:
                    da_mix(h - 1)

            def da_value(h):
                copy_turn(f"av{h}", da_o[:, :, h * P:(h + 1) * P],
                          turn_bank(f"av{h}")[:, 0:2 * P].rearrange("p (t d) -> p t d", t=TT))

            def da_scale(h):
                dve.wait_ge(da_norm, h // 2 + 1)
                dve.wait_ge(turn_dve, turn[f"av{h + 1}"]["dve_end"])
                for tt in range(TT):
                    o = da_o[:, tt, h * P:(h + 2) * P].rearrange("p (h d) -> p h d", d=P)
                    dve.tensor_tensor(o, o, spread_to(da_r[:, h // 2, tt, :], 2, [2, P]), ALU.mult)\
                        .then_inc(da_scaled, 1)

            split_turn("x0.4")
            dense("q0", {0: lambda: split_turn("x0.6"), 2: setup_slot}, ahead=AHEAD_0)
            dense("k0", {0: angles, 1: reduced_angles})
            dve.wait_ge(bias_loaded, 32)
            dense("q1", {2: lambda: da_head(0), 3: lambda: da_head(1)})
            dense("k1", {0: lambda: da_head(2), 1: lambda: da_head(3), 2: lambda: (da_factors(3), da_mix(3))})
            dense("v0", {2: lambda: (da_logits(4), da_maxima(4)), 3: lambda: da_head(5)})
            dense("v1", {0: lambda: (da_head(6, lambda: (da_value(0), da_value(1))), da_scale(0)),
                         1: lambda: da_head(7, lambda: split_turn("oT.0")),
                         2: lambda: (da_factors(7), da_value(2), da_value(3), da_mix(7), da_scale(2)),
                         3: lambda: split_turn("oT.2")})
            ao_units(dense, [lambda: (da_value(4), da_value(5), da_scale(4)), lambda: split_turn("oT.4"),
                             lambda: (da_value(6), da_value(7), da_scale(6)), lambda: split_turn("oT.6"), None,
                             lambda: add_to_x("ao0", 0), lambda: (split_turn("x1.0"), split_turn("x1.2")), None])
            add_to_x("ao1", 1)
            split_turn("x1.4")
            split_turn("x1.6")
            mlp(0, 1)
            mlp_end(0, 1, "x2")

            def ml_gates():
                dve.wait_ge(group_act, groups["gate"]["act_end"])
                dve.wait_ge(ml_loaded, 32)
                mark(dve.tensor_tensor(g_i, gate_in[:, :, 0:ML_H], spread_to(gate_b[:, 0:ML_H], 1, [TT, ML_H]), ALU.add))
                mark(dve.tensor_tensor(g_fz, gate_in[:, :, ML_H:], spread_to(gate_b[:, ML_H:], 1, [TT, ML_H]), ALU.add))
                own()
                mark(dve.tensor_scalar(g_nfz, g_fz, -1.0, None, ALU.mult))
                own()
                dve.tensor_tensor(g_abs, g_fz, g_nfz, ALU.max).then_inc(ml_abs, 1)

            def ml_log_forget():
                dve.wait_ge(ml_ln, 1)
                last = None
                for tt in range(TT):
                    last = dve.scalar_tensor_tensor(g_lf[:, tt, :], g_fz[:, tt, :], 0.0, g_ln[:, tt, :],
                                                    ALU.min, ALU.subtract)
                last.then_inc(ml_lf, 1)

            def diagonals(values):
                for h in range(ML_H):
                    for tt in range(TT):
                        last = dve.tensor_scalar(diag[:, h, tt * P:(tt + 1) * P], ident, values[:, tt, h:h + 1], None,
                                                 ALU.mult)
                last.then_inc(ml_diag, 1)

            def ml_cumulated():
                dve.wait_ge(ml_cum, 1)
                mark(dve.tensor_copy(g_F, score[:, 0, 0:2 * ML_H].rearrange("p (t h) -> p t h", t=TT)))
                own()
                mark(dve.tensor_tensor(g_g, g_i, g_F, ALU.subtract))
                own()
                diagonals(g_g)

            spread = score[:, :, :].rearrange("p b (h s) -> p (b h) s", h=2)

            def ml_maxima():
                dve.wait_ge(ml_spread, 1)
                for tt in range(TT):
                    mark(dve.tensor_tensor(maxed[:, :, :], spread[:, :, tt * P:(tt + 1) * P],
                                           spread_to(causal, 1, [ML_H, P]), ALU.add))
                    own()
                    mark(dve.tensor_reduce(g_max[:, tt, :], maxed[:, :, :], AXIS, ALU.max))
                    own()
                mark(dve.tensor_reduce(g_max2[:, 1, :], spread[:, :, 0:P], AXIS, ALU.max))
                own()
                mark(dve.tensor_tensor(g_max[:, 1, :], g_max[:, 1, :], g_max2[:, 1, :], ALU.max))
                own()
                mark(dve.tensor_scalar(g_max, g_max, 0.0, None, ALU.max))
                own()
                mark(dve.tensor_tensor(g_nm, g_F, g_max, ALU.add))
                diagonals(g_max)

            def ml_arguments():
                dve.wait_ge(ml_spread, 2)
                for src, dst in ((slice(0, P), slice(0, P)), (slice(P, S), TALL)):
                    dve.tensor_tensor(ml_w[:, :, dst], spread_to(causal_t, 1, [ML_H, P]), spread[:, :, src],
                                      ALU.subtract).then_inc(ml_args, 1)

            def convolve(b):
                name = f"conv{b}"
                dve.wait_ge(turn_act, turn[name]["act_end"])
                done = [0, 0]
                for shift in range(1, CONV):
                    for j in range(2):
                        c = 2 * b + j
                        tap = gain("mlstm_conv_w", (CONV - 1 - shift) * DC + c)
                        src = turn_bank(name)[:, j * S:(j + 1) * S - shift]
                        dst = ml_t[:, c, shift:]
                        if shift > 1:
                            own(done[j])
                        ins = dve.scalar_tensor_tensor(dst, src, tap, dst, ALU.mult, ALU.add)
                        if shift == CONV - 1 and j == 1:
                            ins.then_inc(turn_dve, 1)
                        else:
                            done[j] = mark(ins)

            def ml_weigh(h):
                dve.wait_ge(ml_scored, h + 1)
                dve.wait_ge(ml_wexp, h + 1)
                dve.scalar_tensor_tensor(ml_s[:, h, :], score[:, h % 2, 0:SCORE], ML_QK ** -0.5, ml_w[:, h, :],
                                         ALU.mult, ALU.mult).then_inc(ml_weighted, 1)

            def ml_denominators(half):
                two = slice(2 * half, 2 * half + 2)
                dve.wait_ge(turn_act, turn[f"mv{2 * half + 1}.1"]["act_end"])
                dve.wait_ge(ml_em, 1)
                den = ml_n[:, :, two, ML_V]
                mark(dve.scalar_tensor_tensor(r_abs[:, :, two], den, -1.0, den, ALU.mult, ALU.max))
                own()
                mark(dve.tensor_tensor(r_dmax[:, :, two], r_abs[:, :, two], g_em[:, :, two], ALU.max))
                own()
                mark(dve.reciprocal(r_dinv[:, :, two], r_dmax[:, :, two]))
                own()
                mark(dve.tensor_tensor(r_t[:, :, two], r_ss[:, :, two], r_dinv[:, :, two], ALU.mult))
                own()
                dve.tensor_tensor(r_ms[:, :, two], r_t[:, :, two], r_dinv[:, :, two], ALU.mult).then_inc(ml_ms, 1)

            def ml_finish(half):
                two = slice(2 * half, 2 * half + 2)
                dve.wait_ge(ml_norm, half + 1)
                mark(dve.tensor_tensor(r_sc[:, :, two], r_dinv[:, :, two], r_r[:, :, two], ALU.mult))
                own()
                dve.wait_ge(group_act, groups[f"mo{half}"]["act_end"])
                for h in range(2 * half, 2 * half + 2):
                    cols = slice(h * ML_V, (h + 1) * ML_V)
                    for tt in range(TT):
                        dve.scalar_tensor_tensor(ml_o[:, tt, cols], ml_n[:, tt, h, 0:ML_V], r_sc[:, tt, h:h + 1],
                                                 ml_o[:, tt, cols], ALU.mult, ALU.mult).then_inc(ml_y, 1)

            dense("mq", {0: lambda: (split_turn("x2.4"), split_turn("x2.6"))}, slice(0, 3), AHEAD_0)
            dense("gate")
            ml_gates()
            dense("mq", {3: ml_log_forget}, slice(3, 4))
            dense("mk", {0: ml_cumulated, 1: ml_maxima, 2: lambda: convolve(0), 3: lambda: convolve(1)})
            dense("mv0", {0: ml_arguments, 1: lambda: convolve(2), 3: lambda: convolve(3)})
            dense("mv1")
            dense("mo0", {n: (lambda n=n: ml_weigh(n)) for n in range(4)})
            dense("mo1", {0: lambda: ml_denominators(0), 1: lambda: (ml_finish(0), ml_denominators(1)),
                          2: lambda: (split_turn("yT.0"), split_turn("yT.2"))})
            dense("mw0", {0: lambda: ml_finish(1)}, first)
            dense("mw1", {0: lambda: (split_turn("yT.4"), split_turn("yT.6"))}, first)
            dense("mw0", None, second)
            add_to_x("mw0", 0)
            dense("mw1", {2: lambda: (split_turn("x3.0"), split_turn("x3.2"))}, second)
            add_to_x("mw1", 1)
            split_turn("x3.4")
            split_turn("x3.6")
            mlp(1, 3)

            mlp_end(1, 3, "x5")

            def normed(n):
                dve.wait_ge(rstd_ready, 5)
                dve.wait_ge(gained_ready, 4)
                tt, cols = n % 2, slice(n // 2 * HALF, (n // 2 + 1) * HALF)
                dve.tensor_scalar(x[:, tt, cols], gained[:, tt, cols], rstd[:, 4, tt:tt + 1], None, ALU.mult)\
                    .then_inc(x_ready, 1)

            def x4_squares(tt):
                dve.wait_ge(gained_ready, 4)
                dve.tensor_tensor_reduce(out=flat_q[:, tt * D:(tt + 1) * D], in0=x[:, tt, :], in1=x[:, tt, :], scale=1.0, scalar=0.0, op0=ALU.mult,
                                         op1=ALU.add, accum_out=ssx[:, 4, tt:tt + 1]).then_inc(x4_squared, 1)

            def shared_key():
                dve.wait_ge(group_act, groups["ckv"]["act_end"])
                dve.wait_ge(b2_loaded, 32)
                dve.wait_ge(trig_ready, 1)
                kr = lat_sb[:, :, LAT:]
                mark(dve.tensor_tensor(kr_sb[:, 1, :, :], kr, kr, ALU.mult))
                mark(dve.tensor_tensor(kr_sb[:, 0, :, :], kr, spread_to(rope_gain[:, 1, :], 1, [TT, ROPE]), ALU.mult))
                own()
                mark(dve.tensor_reduce(kr_ss[:, :], kr_sb[:, 1, :, :], AXIS, ALU.add))
                own()
                lo_half, hi_half = slice(0, ROPE // 2), slice(ROPE // 2, ROPE)
                mark(rotate(kr_sb[:, 3, :, lo_half], kr_sb[:, 3, :, hi_half], kr_sb[:, 1, :, lo_half],
                            kr_sb[:, 2, :, lo_half], kr_sb[:, 0, :, lo_half], kr_sb[:, 0, :, hi_half],
                            trig[:, 1, :, P:], trig[:, 0, :, P:]))

            def ret_rotate(name):
                n = ("rq0", "rq1", "rk0", "rk1").index(name)
                dve.wait_ge(group_act, groups[name]["act_end"])
                if n:
                    wait_turn(dve, ("rq0", "rq1", "rk0")[n - 1] + "b")
                    dve.wait_ge(ret_roped, n)
                src, dst = (work[:, i, :, :].rearrange("p t (h d) -> p t h d", h=2) for i in range(2))
                tmp = [l_work[:, i * HALF:(i + 1) * HALF].rearrange("p (t h d) -> p t h d", t=TT, h=2)
                       for i in range(2)]
                cos, sin = (spread_to(trig[:, i, :, 0:P], 2, [TT, 2, P]) for i in (1, 0))
                rotate(dst[:, :, :, 0:P], dst[:, :, :, P:], tmp[0], tmp[1], src[:, :, :, 0:P], src[:, :, :, P:],
                       cos, sin).then_inc(ret_roped, 1)

            def ret_copy(name, half):
                n = ("rq0", "rq1", "rk0", "rk1").index(name)
                turn_name = f"{name}{'ab'[half]}"
                c = 4 * (n % 2) + 2 * half
                copy_turn(turn_name, (rq_t if n < 2 else rk_t)[:, c:c + 2, :],
                          turn_bank(turn_name).rearrange("p (c s) -> p c s", c=2))

            def ret_decay(h):
                dve.wait_ge(decay_loaded, 32)
                dve.wait_ge(ret_scored, h + 1)
                dve.scalar_tensor_tensor(ret_s[:, h, :], score[:, h % 2, 0:SCORE], RET_QK ** -0.5, ret_s[:, h, :],
                                         ALU.mult, ALU.mult).then_inc(ret_decayed, 1)

            def ret_value(h):
                dve.wait_ge(group_act, groups[f"ret{h}"]["act_end"])
                for tt in range(TT):
                    dve.tensor_copy(ret[:, tt, h * HALF:(h + 1) * HALF], group_ps(f"ret{h}")[:, tt, :])\
                        .then_inc(group_dve, 1)

            def gate_out(n):
                dve.wait_ge(ret_norm, 1)
                dve.wait_ge(group_act, groups[f"rg{n}"]["act_end"])
                dve.wait_ge(group_dve, groups["ret3"]["dve_end"])
                cols = slice(n * HALF, (n + 1) * HALF)
                for tt in range(TT):
                    last = dve.scalar_tensor_tensor(ret[:, tt, cols], ret[:, tt, cols], ret_r[:, tt, n:n + 1],
                                                    work[:, n % 2, tt, :], ALU.mult, ALU.mult)
                last.then_inc(gated, 1)

            def mla_sums_q():
                for tt in range(TT):
                    dve.wait_ge(l_squares, tt + 1)
                    scratch = l_work[:, 0:MLA_H * MLA_QK] if tt == 0 else lk_flat[:, 0:MLA_H * MLA_QK]
                    dve.tensor_reduce(lq_ss[:, tt, :], scratch.rearrange("p (h d) -> p h d", d=MLA_QK), AXIS, ALU.add)\
                        .then_inc(l_sq, 1)

            def mla_sums_k():
                for tt in range(TT):
                    dve.wait_ge(l_squares, TT + tt + 1)
                    scratch = l_work[:, 0:MLA_H * NOPE] if tt == 0 else lk_flat[:, 0:MLA_H * NOPE]
                    dve.tensor_reduce(lk_ss[:, tt, :], scratch.rearrange("p (h d) -> p h d", d=NOPE), AXIS, ALU.add)\
                        .then_inc(l_sq, 1)
                dve.wait_ge(l_sq, 4)
                for tt in range(TT):
                    dve.tensor_scalar(lk_ss[:, tt, :], lk_ss[:, tt, :], kr_ss[:, tt:tt + 1], None, ALU.add)\
                        .then_inc(l_sq, 1)

            def mla_q(tt):
                dve.wait_ge(l_norm, 1)
                q = lq_sb[:, tt, :, :]
                mark(dve.tensor_tensor(q, q, spread_to(lq_r[:, tt, :], 2, [MLA_H, MLA_QK]), ALU.mult))
                own()
                part = lq_sb[:, tt, :, NOPE:]
                mark(dve.tensor_tensor(part, part, spread_to(rope_gain[:, 0, :], 1, [MLA_H, ROPE]), ALU.mult))
                own()
                half = ROPE // 2
                cos, sin = (spread_to(trig[:, i, tt, P:], 1, [MLA_H, half]) for i in (1, 0))
                rotate(rot[:, tt, :, 0:half], rot[:, tt, :, half:], prod[:, tt, :, 0:half], prod[:, tt, :, half:],
                       part[:, :, 0:half], part[:, :, half:], cos, sin).then_inc(lq_ready, 1)

            def mla_k():
                dve.wait_ge(l_norm, 2)
                for tt in range(TT):
                    k = kv[:, tt, :, 0:NOPE]
                    last = dve.tensor_tensor(k, k, spread_to(lk_r[:, tt, :], 2, [MLA_H, NOPE]), ALU.mult)
                last.then_inc(lk_ready, 1)

            def mla_k_rot():
                wait_turn(dve, "mqr1")
                for tt in range(TT):
                    last = dve.tensor_tensor(rot[:, tt, :, :], spread_to(kr_sb[:, 3, tt, :], 1, [MLA_H, ROPE]),
                                             spread_to(lk_r[:, tt, :], 2, [MLA_H, ROPE]), ALU.mult)
                last.then_inc(lk_ready, 1)

            def mla_rot_copy(which, b):
                name = f"{which}r{b}"
                copy_turn(name, (lq_t if which == "mq" else lk_t)[:, 2 * b:2 * b + 2, :],
                          turn_bank(name).rearrange("p (h s) -> p h s", h=2))

            def mla_logits(h):
                dve.wait_ge(l_scored, h + 1)
                b = h % 2
                if h >= 2:
                    wait_turn(dve, f"lp{h - 2}")
                dve.tensor_tensor(l_e[:, b, :], score[:, b, 0:SCORE], mask[:, :], ALU.add).then_inc(l_masked, 1)
                dve.wait_ge(l_masked, h + 1)
                for j, cols in enumerate((WIDE, TALL)):
                    last = dve.tensor_reduce(l_nm[:, b, j:j + 1], l_e[:, b, cols], AXIS, ALU.max, negate=True)
                last.then_inc(l_maxed, 1)

            def mla_recip(h):
                dve.wait_ge(l_exped, h + 1)
                if h >= 2:
                    dve.wait_ge(turn_act, turn[f"lv{h - 2}"]["act_end"])
                dve.reciprocal(l_rec[:, h % 2, :], l_sum[:, h % 2, :]).then_inc(l_reced, 1)

            def mla_slot(n):
                if n < MLA_H:
                    mla_logits(n)
                if 1 <= n <= MLA_H:
                    mla_recip(n - 1)

            dense("cq", {1: lambda: (split_turn("x5.4"), split_turn("x5.6"))}, first)
            dense("ckv", None, first)
            x4_squares(0)
            x4_squares(1)
            dense("cq", None, second)
            dense("ckv", {2: lambda: (normed(0), normed(1)), 3: lambda: (normed(2), normed(3))}, second)
            dense("rq0", {0: shared_key, 1: lambda: split_turn("lat.0"), 2: lambda: split_turn("lat.2"),
                          3: lambda: split_turn("lat.4")})
            for name, before in (("rq1", "rq0"), ("rk0", "rq1"), ("rk1", "rk0")):
                dense(name, {0: lambda before=before: ret_rotate(before), 2: lambda before=before: ret_copy(before, 0),
                             3: lambda before=before: ret_copy(before, 1)})
            dense("uq0", {0: lambda: ret_rotate("rk1")})
            dense("uq1", {1: lambda: ret_copy("rk1", 0)})
            dense("uq2", {1: lambda: ret_copy("rk1", 1)})
            for n in range(4):
                dense(f"ukv{n}")
                ret_decay(n)
            dense("rv0", {0: mla_sums_q, 3: mla_sums_k})
            dense("rv1", {0: lambda: mla_q(0), 1: lambda: mla_q(1), 2: mla_k})
            ret_value(0)
            dense("rv2")
            ret_value(1)

            def rv3_slot(n):
                if n == 0:
                    mla_rot_copy("mq", 0)
                    mla_rot_copy("mq", 1)
                    mla_k_rot()
            dense("rv3", {n: (lambda n=n: rv3_slot(n)) for n in range(4)})
            ret_value(2)
            dense("rg0", {n: (lambda n=n: mla_rot_copy("mk", n)) for n in range(2)})
            ret_value(3)
            dense("rg1", {n: (lambda n=n: mla_slot(n)) for n in range(4)})
            gate_out(0)
            dense("rg2", {n: (lambda n=n: mla_slot(4 + n)) for n in range(4)})
            gate_out(1)
            dense("rg3", {0: lambda: mla_slot(8)})
            gate_out(2)
            gate_out(3)
            dense("gm0", {n: (lambda n=n: split_turn(f"roT.{2 * n}")) for n in range(4)})
            dense("gm1", {n: (lambda n=n: split_turn(f"roT.{8 + 2 * n}")) for n in range(4)})
            dense("gr0")
            dense("gr1")

            def mix_ret(n):
                wait_group(dve, f"br{n}")
                dve.wait_ge(group_act, groups["gr1"]["act_end"])
                cols = slice(n * HALF, (n + 1) * HALF)
                for tt in range(TT):
                    dve.tensor_tensor(mix[:, tt, cols], group_ps(f"br{n}")[:, tt, :], gr[:, tt, cols], ALU.mult)\
                        .then_inc(group_dve, 1)

            def mix_mla(n):
                wait_group(dve, f"bm{n}")
                cols = slice(n * HALF, (n + 1) * HALF)
                for tt in range(TT):
                    dve.tensor_tensor(gm[:, tt, cols], group_ps(f"bm{n}")[:, tt, :], gm[:, tt, cols], ALU.mult)\
                        .then_inc(group_dve, 1)
                for tt in range(TT):
                    dve.wait_ge(group_dve, groups[f"bm{n}"]["dve_end"] - 1 + tt)
                    dve.tensor_tensor(mix[:, tt, cols], mix[:, tt, cols], gm[:, tt, cols], ALU.add)\
                        .then_inc(mixed, 1)

            dense("br0", {2 * n + 1: (lambda n=n: split_turn(f"moT.{2 * n}")) for n in range(4)})
            mix_ret(0)
            dense("br1")
            mix_ret(1)
            dense("bm0")
            mix_mla(0)
            dense("bm1", {2: lambda: split_turn("mixT.0"), 3: lambda: split_turn("mixT.2")})
            mix_mla(1)
            dense("wo0", {1: lambda: (split_turn("mixT.4"), split_turn("mixT.6"))}, first)
            dense("wo1", None, slice(0, 1))
            dense("wo0", None, second)
            add_to_x("wo0", 0)
            dense("wo1", {2: lambda: (split_turn("x6.0"), split_turn("x6.2"))}, slice(1, 4))
            add_to_x("wo1", 1)
            split_turn("x6.4")
            split_turn("x6.6")
            mlp(2, 6, lambda: split_turn("pT.0"))
            mlp_end(2, 6, "x7")

            dense("pl0", ahead=AHEAD - 2)
            dense("pl1", ahead=AHEAD - 1)
            for n in range(2):
                dense(f"pg{n}", {0: lambda: (split_turn("x7.4"), split_turn("x7.6"))} if n == 0 else None)
                dve.wait_ge(group_act, groups[f"pg{n}"]["act_end"])
                cols = slice(n * HALF, (n + 1) * HALF)
                for tt in range(TT):
                    mark(dve.tensor_tensor(gate[:, tt, cols], gate[:, tt, cols], ple[:, tt, cols], ALU.mult))
                    own()
                    dve.tensor_tensor(gate[:, tt, cols], gate[:, tt, cols], x[:, tt, cols], ALU.add)\
                        .then_inc(out_ready, 1)

        @block.gpsimd
        def _(pool):
            mark, own = own_order(pool, pool_step)

            def factor(dst, means, sums, scale, eps, done):
                mark(pool.tensor_scalar(means, sums, scale, eps, ALU.mult, ALU.add))
                own()
                shape = dst.shape[1:]
                half = mhalf[:, 0:math.prod(shape)]
                if len(shape) == 2:
                    half = half.rearrange("p (a b) -> p a b", a=shape[0])
                pool.tensor_tensor(dst, means, half, ALU.pow).then_inc(done, 1)

            def x_factor(v):
                pool.wait_ge(x_squared, TT * (v + 1 - (v > 4)))
                factor(rstd[:, v, :], msx[:, v, :], ssx[:, v, :], 1 / D, EPS, rstd_ready)

            pool.dma_start(onehot[0:BUCKETS + 1, :], w["c_onehot"]).then_inc(small_loaded, 16)
            pool.dma_start(table[0:BUCKETS, :], w["rel_bias"]).then_inc(small_loaded, 16)
            mark(pool.memset(table[BUCKETS:BUCKETS + 1, :], NEG))
            own()
            mark(pool.memset(zeros[:, :], 0.0))
            own()
            pool.memset(mhalf[:, :], -0.5).then_inc(set_ready, 1)
            for i, name in enumerate(("attn_lambda_q1", "attn_lambda_k1", "attn_lambda_q2", "attn_lambda_k2")):
                pool.dma_start(lam_in[:, i, :], w[name][0, :].partition_broadcast(P)).then_inc(lam_loaded, 16)
            pool.dma_start(inv[:, :], w["c_inv"][0, :].partition_broadcast(P)).then_inc(pos_loaded, 16)
            with nc.allow_non_contiguous_dma(reason="256 positions"):
                pool.dma_start(pos_i[:, :], w["positions_2"][0, :].rearrange("(t p) -> p t", p=P))\
                    .then_inc(pos_loaded, 16)
            with nc.allow_non_contiguous_dma(reason="8 values a partition"):
                pool.dma_start(fgain_t[:, :], w["final_norm"].rearrange("(c p) -> p c", p=P))\
                    .then_inc(fgain_t_loaded, 16)
            pool.wait_ge(set_ready, 1)
            x_factor(0)
            pool.wait_ge(bias_rows_ready, 1)
            pool.dma_start(bias_dram[:, 0:3 * P - 1], bias_rows[0:DA_H, :]).then_inc(bias_stored, 16)
            pool.wait_ge(bias_stored, 16)
            rows = bass.AP(bias_dram.tensor, 0, [[0, P], [SCORE, DA_H], [1, 3 * P - 1]])
            pool.dma_start(bias_rep[:, :, 0:3 * P - 1], rows).then_inc(bias_stored, 16)
            pool.wait_ge(bias_stored, 32)
            for cols, at in ((WIDE, P - 1), (TALL, 2 * P - 1)):
                n = cols.stop - cols.start
                skewed = bass.AP(bias_rep.tensor, at, [[DA_H * SCORE - 1, P], [SCORE, DA_H], [1, n]])
                pool.dma_start(bias[:, :, cols], skewed).then_inc(bias_loaded, 16)
            for n in range(DA_H // 2):
                pool.wait_ge(turn_act, turn[f"av{2 * n + 1}"]["act_end"])
                keep = (1.0 - LAMBDA_INIT) ** -2
                factor(da_r[:, n, :, :], da_ms[:, n, :, :], da_ss[:, n, :, :], keep / P, keep * EPS, da_norm)
            x_factor(1)
            pool.wait_ge(x_ready, x_version(2))
            pool.dma_start(gate_b[:, 0:ML_H], w["mlstm_b_i"][0, :].partition_broadcast(P)).then_inc(ml_loaded, 16)
            pool.dma_start(gate_b[:, ML_H:], w["mlstm_b_f"][0, :].partition_broadcast(P)).then_inc(ml_loaded, 16)
            pool.memset(ml_v[:, :, :, ML_V:], 1.0).then_inc(ml_ones, 1)
            x_factor(2)
            for half in range(2):
                two = slice(2 * half, 2 * half + 2)
                pool.wait_ge(ml_ms, half + 1)
                factor(r_r[:, :, two], r_t[:, :, two], r_ms[:, :, two], 1 / ML_V, EPS, ml_norm)
            pool.wait_ge(x_ready, x_version(3))
            pool.dma_start(final_gain[:, :], w["final_norm"].partition_broadcast(P)).then_inc(fgain_loaded, 16)
            x_factor(3)
            pool.wait_ge(fgain_loaded, 16)
            for n in range(2):
                cols = slice(n * HALF, (n + 1) * HALF)
                for tt in range(TT):
                    pool.wait_ge(x_ready, x_version(4, 2 * n + tt + 1))
                    if 2 * n + tt:
                        pool.wait_ge(gained_ready, 2 * n + tt)
                    pool.tensor_tensor(gained[:, tt, cols], x[:, tt, cols], final_gain[:, cols], ALU.mult)\
                        .then_inc(gained_ready, 1)
            pool.wait_ge(gained_ready, 4)
            pool.dma_start(rope_gain[:, 0, :], w["q_norm_2"][0, NOPE:].partition_broadcast(P)).then_inc(b2_loaded, 16)
            pool.dma_start(rope_gain[:, 1, :], w["k_norm_2"][0, NOPE:].partition_broadcast(P)).then_inc(b2_loaded, 16)
            pool.wait_ge(x4_squared, TT)
            factor(rstd[:, 4, :], msx[:, 4, :], ssx[:, 4, :], 1 / D, EPS, rstd_ready)
            mark(pool.tensor_scalar(means4[:, :], msx[:, 4, :], EPS, None, ALU.mult))
            pool.wait_ge(x_squared, TT * 5)
            mark(pool.tensor_scalar(msx[:, 5, :], ssx[:, 5, :], 1 / D, None, ALU.mult))
            own()
            mark(pool.tensor_tensor(msx[:, 5, :], msx[:, 5, :], means4[:, :], ALU.add))
            own()
            pool.tensor_tensor(rstd[:, 5, :], msx[:, 5, :], mhalf[:, 0:TT], ALU.pow).then_inc(rstd_ready, 1)
            pool.wait_ge(lat_sq, 2 * TT)
            mark(pool.tensor_scalar(lat_ms[:, 0, :], lat_ss[:, 0, :], 1 / Q_LORA, EPS, ALU.mult, ALU.add))
            mark(pool.tensor_scalar(lat_ms[:, 1, :], lat_ss[:, 1, :], 1 / KV_LORA, EPS, ALU.mult, ALU.add))
            own()
            pool.tensor_tensor(lat_r[:, :, :], lat_ms[:, :, :], mhalf[:, 0:4].rearrange("p (a b) -> p a b", a=2),
                               ALU.pow).then_inc(lat_norm, 1)
            pool.dma_start(ret_s[:, :, :], w["c_decay"]).then_inc(decay_loaded, 16)
            pool.dma_start(mask[:, :], w["c_mask"]).then_inc(decay_loaded, 16)
            pool.wait_ge(group_act, groups["uq2"]["act_end"])
            pool.wait_ge(ret_roped, 4)
            for tt in range(TT):
                q = flat_q[:, tt * MLA_H * MLA_QK:(tt + 1) * MLA_H * MLA_QK]
                scratch = (l_work if tt == 0 else lk_flat)[:, 0:MLA_H * MLA_QK]
                pool.tensor_tensor(scratch, q, q, ALU.mult).then_inc(l_squares, 1)
            pool.wait_ge(group_act, groups["ukv3"]["act_end"])
            for tt in range(TT):
                pool.wait_ge(l_sq, tt + 1)
                k = kv[:, tt, :, 0:NOPE]
                scratch = (l_work if tt == 0 else lk_flat)[:, 0:MLA_H * NOPE].rearrange("p (h d) -> p h d", d=NOPE)
                pool.tensor_tensor(scratch, k, k, ALU.mult).then_inc(l_squares, 1)
            factor(lq_r[:, :, :], lq_ms[:, :, :], lq_ss[:, :, :], 1.0, MLA_QK * EPS, l_norm)
            pool.wait_ge(l_sq, 6)
            factor(lk_r[:, :, :], lk_ms[:, :, :], lk_ss[:, :, :], 1 / MLA_QK, EPS, l_norm)
            pool.wait_ge(group_act, groups["ret3"]["act_end"])
            factor(ret_r[:, :, :], ret_ms[:, :, :], ret_ss[:, :, :], 1 / RET_V, EPS, ret_norm)
            pool.wait_ge(x_ready, x_version(6))
            for tt in range(TT):
                pool.dma_start(p_sb[:, tt, :], w["p_2"][0, 0, tt * P:(tt + 1) * P, :]).then_inc(p_loaded, 16)
            x_factor(6)
            x_factor(7)


_INS = ["x", "rel_bias", "attn_norm", "attn_w_in", "attn_lambda_q1", "attn_lambda_k1", "attn_lambda_q2",
        "attn_lambda_k2", "attn_subln", "attn_w_out", "mlstm_norm", "mlstm_w_in", "mlstm_b_i", "mlstm_b_f",
        "mlstm_conv_w", "mlstm_conv_b", "mlstm_head_norm", "mlstm_w_out", "mlp_norm", "mlp_w1", "mlp_w2",
        "final_norm", "p_2", "positions_2", "norm_mix_2", "w_in_2", "ret_norm_2", "q_lat_norm_2", "kv_lat_norm_2",
        "w_uq_2", "w_ukv_2", "q_norm_2", "k_norm_2", "w_br_2", "w_bm_2", "w_o_2", "norm_mlp_2", "w_up_2",
        "w_down_2", "norm_ple_2", "w_ple_gate_2", "w_ple_2"]
_ONE_LAYER = ["attn_w_in", "attn_w_out", "mlstm_w_in", "mlstm_w_out", "w_in_2", "w_uq_2", "w_ukv_2", "w_br_2",
              "w_bm_2", "w_o_2", "w_up_2", "w_down_2", "w_ple_gate_2", "w_ple_2"]


def kernel(**inputs):
    import concourse.bacc as bacc
    from concourse.bass_utils import run_bass_kernel_spmd

    nc = bacc.Bacc("TRN2", target_bir_lowering=False, num_devices=1)
    arrays, w = {}, {}
    for name, a in [(n, np.ascontiguousarray(inputs[n])) for n in _INS] + list(constants().items()):
        arrays[f"in_{name}"] = a
        w[name] = nc.dram_tensor(f"in_{name}", a.shape, mybir.dt.from_np(a.dtype), kind="ExternalInput").ap()
    for name in _ONE_LAYER:
        w[name] = w[name][0]
    out = nc.dram_tensor("out_0", (1, S, D), F32, kind="ExternalOutput").ap()
    build(nc, w, out)
    r = run_bass_kernel_spmd(nc, [arrays], core_ids=[0])
    return r.results[0]["out_0"]
```
